# Optimizing a Trainium2 kernel written in Bass

```python
import math
import jax, jax.numpy as jnp
from jax import lax
import numpy as np
import jax
import jax.numpy as jnp

D_MODEL = 1024
BATCH = 1
SEQ = 256
DEPTH = 2

ATT_HEADS = 8
ATT_QK_DIM = 64
ATT_V_DIM = 2 * ATT_QK_DIM
ATT_QK_WIDTH = ATT_HEADS * 2 * ATT_QK_DIM
ATT_WIDTH = ATT_HEADS * ATT_V_DIM
ROPE_THETA = 10000.0
Q_BLOCK = 128
CONV_WIDTH = 1024
CONV_KERNEL = 31
DN_HEADS = 8
DN_HEAD_DIM = 128
DN_WIDTH = DN_HEADS * DN_HEAD_DIM
DN_SHORT_CONV = 4
DN_CHUNK = 64
N_BRANCHES = 3
RMS_EPS = 1e-6
LN_EPS = 1e-5
IN_WIDTHS = (ATT_QK_WIDTH, ATT_QK_WIDTH, ATT_WIDTH, ATT_WIDTH,
             2 * CONV_WIDTH, CONV_WIDTH,
             DN_WIDTH, DN_WIDTH, DN_WIDTH, DN_WIDTH, DN_HEADS, DN_HEADS,
             N_BRANCHES * D_MODEL)
IN_DIM = sum(IN_WIDTHS)


def rms_norm(x, w, eps=RMS_EPS):
    xf = x.astype(jnp.float32)
    y = xf * lax.rsqrt(jnp.mean(xf * xf, axis=-1, keepdims=True) + eps)
    return (y * w.astype(jnp.float32)).astype(x.dtype)

def layer_norm(x, w, b, eps=LN_EPS):
    xf = x.astype(jnp.float32)
    mu = jnp.mean(xf, axis=-1, keepdims=True)
    xc = xf - mu
    y = xc * lax.rsqrt(jnp.mean(xc * xc, axis=-1, keepdims=True) + eps)
    return (y * w.astype(jnp.float32) + b.astype(jnp.float32)).astype(x.dtype)

def l2_normalize(x, eps=1e-6):
    xf = x.astype(jnp.float32)
    return xf * lax.rsqrt(jnp.sum(xf * xf, axis=-1, keepdims=True) + eps)

def causal_depthwise_conv(x, w):
    K, C = w.shape
    return lax.conv_general_dilated(x, w[:, None, :].astype(x.dtype), window_strides=(1,),
                                    padding=[(K - 1, 0)],
                                    dimension_numbers=('NWC', 'WIO', 'NWC'),
                                    feature_group_count=C)

def rope_tables(positions):
    inv_freq = ROPE_THETA ** (-jnp.arange(0, ATT_QK_DIM, 2, dtype=jnp.float32) / ATT_QK_DIM)
    ang = positions.astype(jnp.float32)[..., None] * inv_freq
    return jnp.cos(ang)[:, :, None, None, :], jnp.sin(ang)[:, :, None, None, :]

def apply_rope(t, cos, sin):
    tf = t.astype(jnp.float32)
    t1, t2 = jnp.split(tf, 2, axis=-1)
    return jnp.concatenate([t1 * cos - t2 * sin, t2 * cos + t1 * sin], axis=-1).astype(t.dtype)

def diff_attention_branch(q_in, k_in, v_in, z, cos, sin, lam_qk, subln_w, w_o, lambda_init):
    B, L, _ = q_in.shape
    q = apply_rope(q_in.reshape(B, L, ATT_HEADS, 2, ATT_QK_DIM), cos, sin).transpose(0, 2, 3, 1, 4)
    k = apply_rope(k_in.reshape(B, L, ATT_HEADS, 2, ATT_QK_DIM), cos, sin).transpose(0, 2, 3, 1, 4)
    v = v_in.reshape(B, L, ATT_HEADS, ATT_V_DIM).transpose(0, 2, 1, 3)
    lq = lam_qk.astype(jnp.float32)
    lam = jnp.exp(jnp.sum(lq[0] * lq[1])) - jnp.exp(jnp.sum(lq[2] * lq[3])) + lambda_init
    scale = ATT_QK_DIM ** -0.5
    outs = []
    for blk in range(L // Q_BLOCK):
        s0 = blk * Q_BLOCK
        e = s0 + Q_BLOCK
        s = jnp.einsum('bhmqd,bhmkd->bhmqk', q[:, :, :, s0:e], k[:, :, :, :e]).astype(jnp.float32) * scale
        mask = (s0 + jnp.arange(Q_BLOCK))[:, None] >= jnp.arange(e)[None, :]
        p = jax.nn.softmax(jnp.where(mask, s, -jnp.inf), axis=-1)
        a = p[:, :, 0] - lam * p[:, :, 1]
        outs.append(jnp.einsum('bhqk,bhkd->bhqd', a.astype(v.dtype), v[:, :, :e]))
    o = jnp.concatenate(outs, axis=2)
    o = rms_norm(o, subln_w) * (1.0 - lambda_init)
    o = o.transpose(0, 2, 1, 3).reshape(B, L, ATT_WIDTH)
    return (o * jax.nn.silu(z)) @ w_o

def conformer_conv_branch(glu_in, z, dw_w, dw_b, ln_w, ln_b, w_o):
    a, g = jnp.split(glu_in, 2, axis=-1)
    u = a * jax.nn.sigmoid(g)
    u = causal_depthwise_conv(u, dw_w) + dw_b
    u = layer_norm(u, ln_w, ln_b)
    u = jax.nn.silu(u) * jax.nn.silu(z)
    return u @ w_o

def chunked_gated_delta_rule(q, k, v, g, beta):
    B, H, L, dk = q.shape
    dv = v.shape[-1]
    C = DN_CHUNK
    N = L // C
    f32 = jnp.float32
    q = q.astype(f32) * dk ** -0.5
    k = k.astype(f32)
    v = v.astype(f32)
    chunk = lambda t: t.reshape(B, H, N, C, *t.shape[3:])
    q, k, v, g, beta = chunk(q), chunk(k), chunk(v), chunk(g.astype(f32)), chunk(beta.astype(f32))
    g = jnp.cumsum(g, axis=-1)
    idx = jnp.arange(C)
    causal = idx[:, None] >= idx[None, :]
    strict = idx[:, None] > idx[None, :]
    decay = jnp.exp(jnp.where(causal, g[..., :, None] - g[..., None, :], -jnp.inf))
    kb = k * beta[..., None]
    lower = jnp.where(strict, jnp.einsum('bhnid,bhnjd->bhnij', kb, k) * decay, 0.0)
    tri = lower + jnp.eye(C, dtype=f32)
    rhs = jnp.concatenate([v * beta[..., None], kb * jnp.exp(g)[..., None]], axis=-1)
    sol = lax.linalg.triangular_solve(tri, rhs, left_side=True, lower=True, unit_diagonal=True)
    u, w = sol[..., :dv], sol[..., dv:]
    intra = jnp.einsum('bhnid,bhnjd->bhnij', q, k) * decay

    def step(state, inp):
        q_n, k_n, u_n, w_n, g_n, a_n = inp
        v_new = u_n - jnp.einsum('bhck,bhkv->bhcv', w_n, state)
        o_n = (jnp.einsum('bhck,bhkv->bhcv', q_n * jnp.exp(g_n)[..., None], state)
               + jnp.einsum('bhij,bhjv->bhiv', a_n, v_new))
        g_last = g_n[..., -1:]
        k_dec = k_n * jnp.exp(g_last - g_n)[..., None]
        state = state * jnp.exp(g_last)[..., None] + jnp.einsum('bhck,bhcv->bhkv', k_dec, v_new)
        return state, o_n

    xs = tuple(jnp.moveaxis(t, 2, 0) for t in (q, k, u, w, g, intra))
    state0 = jnp.zeros((B, H, dk, dv), f32)
    _, o = lax.scan(step, state0, xs)
    return jnp.moveaxis(o, 0, 2).reshape(B, H, L, dv)

def gated_deltanet_branch(q_in, k_in, v_in, z, b_in, a_in, conv_w, a_log, dt_bias, norm_w, w_o):
    B, L, _ = q_in.shape
    qkv = jax.nn.silu(causal_depthwise_conv(jnp.concatenate([q_in, k_in, v_in], axis=-1), conv_w))
    q, k, v = jnp.split(qkv, 3, axis=-1)
    heads = lambda t: t.reshape(B, L, DN_HEADS, DN_HEAD_DIM).transpose(0, 2, 1, 3)
    q = l2_normalize(heads(q))
    k = l2_normalize(heads(k))
    v = heads(v)
    beta = jax.nn.sigmoid(b_in.astype(jnp.float32)).transpose(0, 2, 1)
    g = (-jnp.exp(a_log.astype(jnp.float32))
         * jax.nn.softplus(a_in.astype(jnp.float32) + dt_bias.astype(jnp.float32))).transpose(0, 2, 1)
    o = chunked_gated_delta_rule(q, k, v, g, beta).transpose(0, 2, 1, 3)
    zh = z.reshape(B, L, DN_HEADS, DN_HEAD_DIM).astype(jnp.float32)
    o = rms_norm(o, norm_w) * jax.nn.silu(zh)
    return o.reshape(B, L, DN_WIDTH).astype(z.dtype) @ w_o

def hybrid_layer(x, cos, sin, layer_idx, norm_w, w_in, lam_qk, attn_subln_w, w_attn_out,
                 conv_dw_w, conv_dw_b, conv_ln_w, conv_ln_b, w_conv_out,
                 dn_conv_w, dn_a_log, dn_dt_bias, dn_norm_w, w_dn_out, w_out):
    h = rms_norm(x, norm_w)
    proj = h @ w_in
    split_points = np.cumsum(np.array(IN_WIDTHS))[:-1].tolist()
    (aq, ak, av, az, c_glu, cz, dq, dk, dvv, dz, db, da, gate_logits) = jnp.split(proj, split_points, axis=-1)
    lambda_init = 0.8 - 0.6 * math.exp(-0.3 * layer_idx)
    y_a = diff_attention_branch(aq, ak, av, az, cos, sin, lam_qk, attn_subln_w, w_attn_out, lambda_init)
    y_c = conformer_conv_branch(c_glu, cz, conv_dw_w, conv_dw_b, conv_ln_w, conv_ln_b, w_conv_out)
    y_d = gated_deltanet_branch(dq, dk, dvv, dz, db, da, dn_conv_w, dn_a_log, dn_dt_bias, dn_norm_w, w_dn_out)
    g_a, g_c, g_d = jnp.split(jax.nn.sigmoid(gate_logits), N_BRANCHES, axis=-1)
    merged = g_a * y_a + g_c * y_c + g_d * y_d
    return x + merged @ w_out

def first_inputs(seed: int = 0) -> dict:
    key = jax.random.key(seed)
    ks = jax.random.split(key, 20)
    f32 = jnp.float32
    nrm = lambda k, shape, s: jax.random.normal(k, shape, f32) * s
    x = nrm(ks[0], (BATCH, SEQ, D_MODEL), 1.0)
    positions = jnp.tile(jnp.arange(SEQ, dtype=jnp.int32)[None, :], (BATCH, 1))
    norm_w = 1.0 + nrm(ks[1], (DEPTH, D_MODEL), 0.02)
    w_in = nrm(ks[2], (DEPTH, D_MODEL, IN_DIM), D_MODEL ** -0.5)
    lam_qk = nrm(ks[3], (DEPTH, 4, ATT_QK_DIM), 0.1)
    attn_subln_w = 1.0 + nrm(ks[4], (DEPTH, ATT_V_DIM), 0.02)
    w_attn_out = nrm(ks[5], (DEPTH, ATT_WIDTH, D_MODEL), ATT_WIDTH ** -0.5)
    conv_dw_w = nrm(ks[6], (DEPTH, CONV_KERNEL, CONV_WIDTH), CONV_KERNEL ** -0.5)
    conv_dw_b = nrm(ks[7], (DEPTH, CONV_WIDTH), 0.02)
    conv_ln_w = 1.0 + nrm(ks[8], (DEPTH, CONV_WIDTH), 0.02)
    conv_ln_b = nrm(ks[9], (DEPTH, CONV_WIDTH), 0.02)
    w_conv_out = nrm(ks[10], (DEPTH, CONV_WIDTH, D_MODEL), CONV_WIDTH ** -0.5)
    dn_conv_w = nrm(ks[11], (DEPTH, DN_SHORT_CONV, 3 * DN_WIDTH), DN_SHORT_CONV ** -0.5)
    dn_a_log = jnp.log(jax.random.uniform(ks[12], (DEPTH, DN_HEADS), f32, 1.0, 16.0))
    dt = jnp.exp(jax.random.uniform(ks[13], (DEPTH, DN_HEADS), f32, math.log(1e-3), math.log(1e-1)))
    dn_dt_bias = dt + jnp.log(-jnp.expm1(-dt))
    dn_norm_w = 1.0 + nrm(ks[14], (DEPTH, DN_HEAD_DIM), 0.02)
    w_dn_out = nrm(ks[15], (DEPTH, DN_WIDTH, D_MODEL), DN_WIDTH ** -0.5)
    w_out = nrm(ks[16], (DEPTH, D_MODEL, D_MODEL), D_MODEL ** -0.5)
    final_norm_w = 1.0 + nrm(ks[17], (D_MODEL,), 0.02)
    return {'x': x, 'positions': positions, 'norm_w': norm_w, 'w_in': w_in, 'lam_qk': lam_qk,
            'attn_subln_w': attn_subln_w, 'w_attn_out': w_attn_out, 'conv_dw_w': conv_dw_w,
            'conv_dw_b': conv_dw_b, 'conv_ln_w': conv_ln_w, 'conv_ln_b': conv_ln_b,
            'w_conv_out': w_conv_out, 'dn_conv_w': dn_conv_w, 'dn_a_log': dn_a_log,
            'dn_dt_bias': dn_dt_bias, 'dn_norm_w': dn_norm_w, 'w_dn_out': w_dn_out,
            'w_out': w_out, 'final_norm_w': final_norm_w}

def first_block(x, positions, norm_w, w_in, lam_qk, attn_subln_w, w_attn_out, conv_dw_w, conv_dw_b,
              conv_ln_w, conv_ln_b, w_conv_out, dn_conv_w, dn_a_log, dn_dt_bias, dn_norm_w,
              w_dn_out, w_out, final_norm_w):
    cos, sin = rope_tables(positions)
    for l in range(DEPTH):
        x = hybrid_layer(x, cos, sin, l, norm_w[l], w_in[l], lam_qk[l], attn_subln_w[l], w_attn_out[l],
                         conv_dw_w[l], conv_dw_b[l], conv_ln_w[l], conv_ln_b[l], w_conv_out[l],
                         dn_conv_w[l], dn_a_log[l], dn_dt_bias[l], dn_norm_w[l], w_dn_out[l], w_out[l])
    return rms_norm(x, final_norm_w)


_first_inputs = first_inputs


def first_inputs(seed=0):
    import zlib

    import numpy as np

    out = dict(_first_inputs(seed))
    spreads = {}
    factors = {'lam_qk': 4.343,
     'attn_subln_w': 8.0,
     'conv_dw_b': 4.903,
     'conv_ln_w': 8.0,
     'conv_ln_b': 8.0,
     'dn_norm_w': 6.612,
     'final_norm_w': 2.874}
    for name, (base, spread) in spreads.items():
        noise = np.random.default_rng([zlib.crc32(name.encode()), seed]).standard_normal(out[name].shape)
        drawn = base * np.exp(spread * noise) if base else spread * noise
        out[name] = __import__('jax').numpy.asarray(drawn.astype(out[name].dtype))
    for name, factor in factors.items():
        out[name] = (out[name] * factor).astype(out[name].dtype)
    return out


_narrow_inputs = first_inputs


def first_inputs(seed=0):

    out = dict(_narrow_inputs(seed))
    wider = {'attn_subln_w': 3.99,
     'conv_ln_w': 4.19,
     'conv_ln_b': 3.98,
     'dn_norm_w': 3.5,
     'final_norm_w': 3.23}
    for name, times in wider.items():
        mean = out[name].mean()
        out[name] = (mean + times * (out[name] - mean)).astype(out[name].dtype)
    return out


CTX_LEN = 256
GRID_W = 64
N_HEADS = 8
N_KV_HEADS = 2
KV_GROUP = N_HEADS // N_KV_HEADS
HEAD_DIM = 128
ATTN_WIDTH = N_HEADS * HEAD_DIM
KV_WIDTH = N_KV_HEADS * HEAD_DIM
ROPE_AXIS_DIM = HEAD_DIM // 2
HYENA_WIDTH = D_MODEL // 2
HYENA_PROJ = 3 * HYENA_WIDTH
SHORT_CONV = 3
FILTER_EMB = 33
FILTER_BANDS = (FILTER_EMB - 1) // 2
FILTER_HIDDEN = 64
FILTER_OUT_GAIN = 0.05
DECAY_TARGET = 1e-2
FAST_DECAY_PCT = 0.3
SLOW_DECAY_PCT = 1.5
N_BRANCHES_2 = 2
GATE_WIDTH = N_BRANCHES_2 * D_MODEL
PROJ_WIDTH = ATTN_WIDTH + 2 * KV_WIDTH + HYENA_PROJ + GATE_WIDTH
PROJ_SPLITS = (ATTN_WIDTH, ATTN_WIDTH + KV_WIDTH, ATTN_WIDTH + 2 * KV_WIDTH,
               ATTN_WIDTH + 2 * KV_WIDTH + HYENA_PROJ)
D_FF = (8 * D_MODEL + 3 * 256 - 1) // (3 * 256) * 256
N_MOD = 6
EPS = 1e-6


def rms_norm_2(x, gain):
    xf = x.astype(jnp.float32)
    y = xf * lax.rsqrt(jnp.mean(xf * xf, axis=-1, keepdims=True) + EPS)
    return (y * gain.astype(jnp.float32)).astype(x.dtype)

def modulate(h, shift, scale):
    return h * (1 + scale) + shift

def split_heads_norm(t, gain, n_heads):
    t = t.reshape(t.shape[0], t.shape[1], n_heads, HEAD_DIM)
    return rms_norm_2(t, gain)

def axial_rope_tables(rows):
    row = jnp.repeat(jnp.arange(rows, dtype=jnp.float32), GRID_W)
    col = jnp.tile(jnp.arange(GRID_W, dtype=jnp.float32), rows)
    inv_freq = ROPE_THETA ** (-jnp.arange(0, ROPE_AXIS_DIM, 2, dtype=jnp.float32) / ROPE_AXIS_DIM)
    ang = jnp.concatenate([row[:, None] * inv_freq, col[:, None] * inv_freq], axis=-1)
    return jnp.cos(ang), jnp.sin(ang)

def apply_rope_2(t, cos, sin):
    tf = t.astype(jnp.float32).reshape(*t.shape[:-1], HEAD_DIM // 2, 2)
    c = cos[None, :, None, :]
    s = sin[None, :, None, :]
    t0, t1 = tf[..., 0], tf[..., 1]
    out = jnp.stack([t0 * c - t1 * s, t0 * s + t1 * c], axis=-1)
    return out.reshape(t.shape).astype(t.dtype)

def latent_attention(q, k, v, k_ctx, v_ctx):
    b, length = q.shape[0], q.shape[1]
    n_blocks = length // Q_BLOCK
    keys = jnp.concatenate([k_ctx, k], axis=1)
    vals = jnp.concatenate([v_ctx, v], axis=1)
    qb = q.reshape(b, n_blocks, Q_BLOCK, N_KV_HEADS, KV_GROUP, HEAD_DIM)
    qb = jnp.moveaxis(qb, 1, 0)
    scale = HEAD_DIM ** -0.5

    def one_block(q_blk):
        s = jnp.einsum('bqhgd,bkhd->bhgqk', q_blk, keys, preferred_element_type=jnp.float32) * scale
        p = jax.nn.softmax(s, axis=-1).astype(vals.dtype)
        return jnp.einsum('bhgqk,bkhd->bqhgd', p, vals)

    out = lax.map(one_block, qb)
    return jnp.moveaxis(out, 0, 1).reshape(b, length, ATTN_WIDTH)

def context_attention(q, k, v):
    b, length = q.shape[0], q.shape[1]
    qg = q.reshape(b, length, N_KV_HEADS, KV_GROUP, HEAD_DIM)
    s = jnp.einsum('bqhgd,bkhd->bhgqk', qg, k, preferred_element_type=jnp.float32) * HEAD_DIM ** -0.5
    p = jax.nn.softmax(s, axis=-1).astype(v.dtype)
    return jnp.einsum('bhgqk,bkhd->bqhgd', p, v).reshape(b, length, ATTN_WIDTH)

def short_conv(u, w, bias):
    up = jnp.pad(u, ((0, 0), (1, 1), (0, 0)))
    return up[:, :-2] * w[0] + up[:, 1:-1] * w[1] + up[:, 2:] * w[2] + bias

def hyena_filter(length, fw1, fb1, fw2, fb2, fw3, fb3, fw4, freq):
    t = jnp.linspace(0.0, 1.0, length, dtype=jnp.float32)[:, None]
    w = (2.0 * math.pi / length) * jnp.arange(length, dtype=jnp.float32)[:, None]
    f = jnp.linspace(1e-4, FILTER_BANDS - 1, FILTER_BANDS, dtype=jnp.float32)[None, :]
    z = jnp.concatenate([t, jnp.cos(f * w), -jnp.sin(f * w)], axis=-1)
    h = jnp.sin(freq[0] * (z @ fw1 + fb1))
    h = jnp.sin(freq[1] * (h @ fw2 + fb2))
    h = jnp.sin(freq[2] * (h @ fw3 + fb3))
    h = (h @ fw4).reshape(length, 2, HYENA_WIDTH)
    max_decay = math.log(DECAY_TARGET) / FAST_DECAY_PCT
    min_decay = math.log(DECAY_TARGET) / SLOW_DECAY_PCT
    deltas = jnp.abs(jnp.linspace(min_decay, max_decay, HYENA_WIDTH, dtype=jnp.float32))
    decay = jnp.exp(-t * deltas)
    h = h * decay[:, None, :]
    return h[:, 0], h[:, 1]

def bidirectional_long_conv(v, h_fwd, h_bwd):
    length = v.shape[1]
    n_fft = 2 * length
    k = jnp.concatenate([h_fwd, jnp.zeros((1, HYENA_WIDTH), h_fwd.dtype), h_bwd[:0:-1]], axis=0)
    v_f = jnp.fft.rfft(v.astype(jnp.float32), n=n_fft, axis=1)
    k_f = jnp.fft.rfft(k, n=n_fft, axis=0)
    return jnp.fft.irfft(v_f * k_f[None], n=n_fft, axis=1)[:, :length]

def hyena_mix(u, conv_w, conv_b, fw1, fb1, fw2, fb2, fw3, fb3, fw4, freq, bias):
    length = u.shape[1]
    x0, x1, v = jnp.split(short_conv(u, conv_w, conv_b), 3, axis=-1)
    v = v * x1
    h_fwd, h_bwd = hyena_filter(length, fw1, fb1, fw2, fb2, fw3, fb3, fw4, freq)
    y = bidirectional_long_conv(v, h_fwd, h_bwd) + v.astype(jnp.float32) * bias
    return (y * x0).astype(u.dtype)

def merge_branches(attn_out, hyena_out, gate_logits, w_o_attn, w_o_hyena, w_out):
    g_attn, g_hyena = jnp.split(jax.nn.sigmoid(gate_logits), N_BRANCHES_2, axis=-1)
    merged = g_attn * (attn_out @ w_o_attn) + g_hyena * (hyena_out @ w_o_hyena)
    return merged @ w_out

def swiglu(h, w_gate_up, w_down):
    g, u = jnp.split(h @ w_gate_up, 2, axis=-1)
    return (jax.nn.silu(g) * u) @ w_down

def second_inputs(seed: int = 0) -> dict:
    key = jax.random.key(seed)
    ks = jax.random.split(key, 28)
    D = D_MODEL

    def nrm(k, shape, scale=1.0):
        return jax.random.normal(k, shape, jnp.float32) * scale

    return {
        'x': nrm(ks[0], (BATCH, SEQ, D)),
        'c': nrm(ks[1], (BATCH, D)),
        'ctx': nrm(ks[2], (BATCH, CTX_LEN, D)),
        'c_ctx': nrm(ks[3], (D,)),
        'w_mod': nrm(ks[4], (DEPTH, D, N_MOD * D), D ** -0.5),
        'b_mod': nrm(ks[5], (DEPTH, N_MOD * D), 0.01),
        'norm_mix': 1.0 + nrm(ks[6], (DEPTH, D), 0.05),
        'w_in': nrm(ks[7], (DEPTH, D, PROJ_WIDTH), D ** -0.5),
        'q_norm': 1.0 + nrm(ks[8], (DEPTH, HEAD_DIM), 0.05),
        'k_norm': 1.0 + nrm(ks[9], (DEPTH, HEAD_DIM), 0.05),
        'conv_w': nrm(ks[10], (DEPTH, SHORT_CONV, HYENA_PROJ), SHORT_CONV ** -0.5),
        'conv_b': nrm(ks[11], (DEPTH, HYENA_PROJ), 0.01),
        'filt_w1': nrm(ks[12], (DEPTH, FILTER_EMB, FILTER_HIDDEN), FILTER_EMB ** -0.5),
        'filt_b1': nrm(ks[13], (DEPTH, FILTER_HIDDEN), 0.1),
        'filt_w2': nrm(ks[14], (DEPTH, FILTER_HIDDEN, FILTER_HIDDEN), FILTER_HIDDEN ** -0.5),
        'filt_b2': nrm(ks[15], (DEPTH, FILTER_HIDDEN), 0.1),
        'filt_w3': nrm(ks[16], (DEPTH, FILTER_HIDDEN, FILTER_HIDDEN), FILTER_HIDDEN ** -0.5),
        'filt_b3': nrm(ks[17], (DEPTH, FILTER_HIDDEN), 0.1),
        'filt_w4': nrm(ks[18], (DEPTH, FILTER_HIDDEN, 2 * HYENA_WIDTH), FILTER_HIDDEN ** -0.5 * FILTER_OUT_GAIN),
        'filt_freq': 1.0 + nrm(ks[19], (DEPTH, 3, FILTER_HIDDEN), 0.1),
        'hyena_bias': nrm(ks[20], (DEPTH, HYENA_WIDTH), 0.5),
        'w_o_attn': nrm(ks[21], (DEPTH, ATTN_WIDTH, D), ATTN_WIDTH ** -0.5),
        'w_o_hyena': nrm(ks[22], (DEPTH, HYENA_WIDTH, D), HYENA_WIDTH ** -0.5),
        'w_out': nrm(ks[23], (DEPTH, D, D), D ** -0.5),
        'norm_ffn': 1.0 + nrm(ks[24], (DEPTH, D), 0.05),
        'w_gate_up': nrm(ks[25], (DEPTH, D, 2 * D_FF), D ** -0.5),
        'w_down': nrm(ks[26], (DEPTH, D_FF, D), D_FF ** -0.5),
        'norm_final': 1.0 + nrm(ks[27], (D,), 0.05),
    }

def second_block(x, c, ctx, c_ctx, w_mod, b_mod, norm_mix, w_in, q_norm, k_norm, conv_w, conv_b,
              filt_w1, filt_b1, filt_w2, filt_b2, filt_w3, filt_b3, filt_w4, filt_freq, hyena_bias,
              w_o_attn, w_o_hyena, w_out, norm_ffn, w_gate_up, w_down, norm_final):
    b, length = x.shape[0], x.shape[1]
    rows = length // GRID_W
    cos, sin = axial_rope_tables(rows)
    silu_c = jax.nn.silu(c)
    silu_cc = jax.nn.silu(c_ctx)
    for layer in range(DEPTH):
        last = layer == DEPTH - 1
        mod = (silu_c @ w_mod[layer] + b_mod[layer])[:, None, :]
        mod_c = silu_cc @ w_mod[layer] + b_mod[layer]
        shift1, scale1, gate1, shift2, scale2, gate2 = jnp.split(mod, N_MOD, axis=-1)
        c_shift1, c_scale1, c_gate1, c_shift2, c_scale2, c_gate2 = jnp.split(mod_c, N_MOD, axis=-1)
        filt = (filt_w1[layer], filt_b1[layer], filt_w2[layer], filt_b2[layer],
                filt_w3[layer], filt_b3[layer], filt_w4[layer], filt_freq[layer])

        h_ctx = modulate(rms_norm_2(ctx, norm_mix[layer]), c_shift1, c_scale1)
        if last:
            kc, vc = jnp.split(h_ctx @ w_in[layer][:, ATTN_WIDTH:ATTN_WIDTH + 2 * KV_WIDTH], 2, axis=-1)
        else:
            qc, kc, vc, hyc, gc = jnp.split(h_ctx @ w_in[layer], PROJ_SPLITS, axis=-1)
        kc = split_heads_norm(kc, k_norm[layer], N_KV_HEADS)
        vc = vc.reshape(b, vc.shape[1], N_KV_HEADS, HEAD_DIM)

        h = modulate(rms_norm_2(x, norm_mix[layer]), shift1, scale1)
        q, k, v, hy, g = jnp.split(h @ w_in[layer], PROJ_SPLITS, axis=-1)
        q = apply_rope_2(split_heads_norm(q, q_norm[layer], N_HEADS), cos, sin)
        k = apply_rope_2(split_heads_norm(k, k_norm[layer], N_KV_HEADS), cos, sin)
        v = v.reshape(b, length, N_KV_HEADS, HEAD_DIM)
        attn = latent_attention(q, k, v, kc, vc)
        hyo = hyena_mix(hy, conv_w[layer], conv_b[layer], *filt, hyena_bias[layer])
        x_mix = merge_branches(attn, hyo, g, w_o_attn[layer], w_o_hyena[layer], w_out[layer])

        if not last:
            attn_c = context_attention(split_heads_norm(qc, q_norm[layer], N_HEADS), kc, vc)
            hyo_c = hyena_mix(hyc, conv_w[layer], conv_b[layer], *filt, hyena_bias[layer])
            ctx_mix = merge_branches(attn_c, hyo_c, gc, w_o_attn[layer], w_o_hyena[layer], w_out[layer])
            ctx = ctx + c_gate1 * ctx_mix
            ctx = ctx + c_gate2 * swiglu(modulate(rms_norm_2(ctx, norm_ffn[layer]), c_shift2, c_scale2),
                                         w_gate_up[layer], w_down[layer])

        x = x + gate1 * x_mix
        x = x + gate2 * swiglu(modulate(rms_norm_2(x, norm_ffn[layer]), shift2, scale2),
                               w_gate_up[layer], w_down[layer])
    return rms_norm_2(x, norm_final)


def setup_inputs(seed=0):
    out = dict(first_inputs(seed))
    for name, value in second_inputs(seed + 1).items():
        if name != "x":
            out[name + "_2"] = value
    return out


def reference(
    x, positions, norm_w, w_in, lam_qk, attn_subln_w, w_attn_out, conv_dw_w, conv_dw_b,
    conv_ln_w, conv_ln_b, w_conv_out, dn_conv_w, dn_a_log, dn_dt_bias, dn_norm_w, w_dn_out,
    w_out, final_norm_w, c_2, ctx_2, c_ctx_2, w_mod_2, b_mod_2, norm_mix_2, w_in_2, q_norm_2,
    k_norm_2, conv_w_2, conv_b_2, filt_w1_2, filt_b1_2, filt_w2_2, filt_b2_2, filt_w3_2,
    filt_b3_2, filt_w4_2, filt_freq_2, hyena_bias_2, w_o_attn_2, w_o_hyena_2, w_out_2,
    norm_ffn_2, w_gate_up_2, w_down_2, norm_final_2,
):
    x = first_block(
        x, positions, norm_w, w_in, lam_qk, attn_subln_w, w_attn_out, conv_dw_w, conv_dw_b,
        conv_ln_w, conv_ln_b, w_conv_out, dn_conv_w, dn_a_log, dn_dt_bias, dn_norm_w, w_dn_out,
        w_out, final_norm_w,
    )
    return second_block(
        x, c_2, ctx_2, c_ctx_2, w_mod_2, b_mod_2, norm_mix_2, w_in_2, q_norm_2, k_norm_2,
        conv_w_2, conv_b_2, filt_w1_2, filt_b1_2, filt_w2_2, filt_b2_2, filt_w3_2, filt_b3_2,
        filt_w4_2, filt_freq_2, hyena_bias_2, w_o_attn_2, w_o_hyena_2, w_out_2, norm_ffn_2,
        w_gate_up_2, w_down_2, norm_final_2,
    )


_drawn_inputs = setup_inputs


def setup_inputs(seed=0):
    import zlib

    import numpy as np

    out = dict(_drawn_inputs(seed))
    spreads = {}
    factors = {'ctx_2': 5.777,
     'b_mod_2': 5.959,
     'norm_mix_2': 3.162,
     'q_norm_2': 8.0,
     'k_norm_2': 8.0,
     'conv_b_2': 8.0,
     'filt_b1_2': 3.381,
     'filt_b2_2': 4.342,
     'filt_freq_2': 6.013,
     'norm_ffn_2': 2.822}
    for name, (base, spread) in spreads.items():
        noise = np.random.default_rng([zlib.crc32(name.encode()), seed]).standard_normal(out[name].shape)
        drawn = base * np.exp(spread * noise) if base else spread * noise
        out[name] = jnp.asarray(drawn.astype(out[name].dtype))
    for name, factor in factors.items():
        out[name] = (out[name] * factor).astype(out[name].dtype)
    return out
```

```python
import math
import numpy as np
import concourse.bass as bass
from concourse import mybir
from contextlib import ExitStack

P = 128
D = 1024
KD = D // P
T = 256
NT = T // P
DEPTH = 2
HEADS = 8
QK_DIM = 64
CONV_K = 31
SHORT_K = 4
HY = 512
KH = HY // P
HY_TAPS = 3
D_FF = 2816
KF = D_FF // P
N_MOD = 6
N_FFT = 2 * T
NEG = -1.0e30
TWO_PI = 2.0 * math.pi
TILES = 32
RING = 3

AQ, AK, AV, AZ, GLU, CZ, DQ, DK, DV, DZ, DB, GATE = (
    0, 1024, 2048, 3072, 4096, 6144, 7168, 8192, 9216, 10240, 11264, 11280)
Q2, K2, V2, HY2, G2 = 0, 1024, 1280, 1536, 3072

TILES_1 = 36 * TILES
TILES_2 = KD * (N_MOD * KD + 40 + 16 + 2 * KF) + KH * KD + 8 * KF
N_TILES = DEPTH * (TILES_1 + TILES_2)
N_LOADS = -(-N_TILES // (TILES * RING)) * RING


def constants():
    f = np.float64
    i = np.arange(P)
    c = {}
    c["ident"] = np.eye(P)
    c["ones"] = np.ones((P, P))
    c["until"] = (i[:, None] <= i[None, :]) * 1.0
    c["later"] = np.where(i[:, None] <= i[None, :], 0.0, NEG)
    causal = np.where(i[:, None] >= i[None, :], 0.0, NEG)
    c["causal1"] = np.concatenate([np.zeros((P, P)), causal], 1)
    lv = []
    for s in (1, 2, 4, 8, 16, 32, 64):
        lv.append(((i[:, None] // (2 * s) == i[None, :] // (2 * s))
                   & (i[:, None] % (2 * s) < s) & (i[None, :] % (2 * s) >= s)) * 1.0)
    c["levels"] = np.concatenate(lv, 1)
    rot1 = np.zeros((P, P))
    for d in range(P):
        if d % QK_DIM < QK_DIM // 2:
            rot1[d + QK_DIM // 2, d] = -1.0
        else:
            rot1[d - QK_DIM // 2, d] = 1.0
    c["rot1"] = rot1
    rot2 = np.zeros((P, P))
    for d in range(0, P, 2):
        rot2[d + 1, d] = -1.0
        rot2[d, d + 1] = 1.0
    c["rot2"] = rot2
    t = np.arange(T)
    half = P // 2
    inv2 = (10000.0 ** (-np.arange(0, half, 2, dtype=f) / half)).astype(np.float32)
    ang = np.concatenate([(t // 64)[:, None].astype(np.float32) * inv2,
                          (t % 64)[:, None].astype(np.float32) * inv2], 1).astype(f)
    c["cos2"] = np.repeat(np.cos(ang).T, 2, 0)
    c["sin2"] = np.repeat(np.sin(ang).T, 2, 0)
    inv1 = 10000.0 ** (-np.arange(0, QK_DIM, 2, dtype=f) / QK_DIM)
    c["inv1"] = np.tile(inv1, 4)[:, None]
    tt = np.linspace(0.0, 1.0, T)[:, None]
    w = (TWO_PI / T) * np.arange(T)[:, None]
    fr = np.linspace(1e-4, 15, 16)[None, :]
    z = np.concatenate([tt, np.cos(fr * w), -np.sin(fr * w)], 1)
    c["zT"] = np.concatenate([z.T, np.zeros((P - 33, T))], 0)
    deltas = np.abs(np.linspace(math.log(1e-2) / 1.5, math.log(1e-2) / 0.3, HY))
    dec = np.exp(-tt * deltas)
    rows = lambda a: a.reshape(-1, P, a.shape[1]).transpose(1, 0, 2).reshape(P, -1)
    c["decay"] = rows(dec)
    ph = TWO_PI * np.outer(t, np.arange(T)) / N_FFT
    re, im = np.cos(ph), -np.sin(ph)
    im_n = im.copy()
    im_n[:, 0] = np.cos(math.pi * t)
    c["dft_fwd"] = rows(np.concatenate([re, im_n], 1))
    bre, bim = re.copy(), -im
    bim[:, 0] = np.cos(math.pi * t)
    bre[0], bim[0] = 0.0, 0.0
    c["dft_bwd"] = rows(np.concatenate([bre, bim], 1))
    ire, iim = 2.0 * np.cos(ph.T) / N_FFT, -2.0 * np.sin(ph.T) / N_FFT
    ire[0] *= 0.5
    iim[0] = np.cos(math.pi * t) / N_FFT
    c["idft"] = rows(np.concatenate([ire, iim], 0))
    for name, v in (("eps6", 1e-6), ("eps5", 1e-5), ("half_pi", math.pi / 2)):
        c[name] = np.full((P, 1), v)
    for name, v in (("lam_init", [0.8 - 0.6 * math.exp(-0.3 * l) for l in range(DEPTH)]),):
        c[name] = np.tile(np.array(v)[None], (P, 1))
    return c


CONST_W = {"ident": P, "ones": P, "until": P, "later": P, "causal1": T, "levels": 7 * P,
           "rot1": P, "rot2": P, "cos2": T, "sin2": T, "inv1": 1, "zT": T, "decay": NT * HY,
           "dft_fwd": NT * N_FFT, "dft_bwd": NT * N_FFT, "idft": 4 * T, "eps6": 1, "eps5": 1, "half_pi": 1,
           "lam_init": DEPTH}

PARAM_W = {"norm_w": DEPTH * KD, "attn_subln_w": DEPTH, "conv_dw_w": DEPTH * KD * CONV_K,
           "conv_dw_b": DEPTH * KD, "conv_ln_w": DEPTH * KD, "conv_ln_b": DEPTH * KD,
           "dn_conv_w": DEPTH * 24 * SHORT_K, "dn_a_log": DEPTH * HEADS, "dn_dt_bias": DEPTH * HEADS,
           "dn_norm_w": DEPTH, "final_norm_w": KD, "lam_qk": DEPTH * 4 * QK_DIM, "w_ba": DEPTH * KD * 16,
           "c": KD * 2, "b_mod": DEPTH * N_MOD * KD, "norm_mix": DEPTH * KD, "q_norm": DEPTH, "k_norm": DEPTH,
           "conv_w": DEPTH * 12 * HY_TAPS, "conv_b": DEPTH * 12, "filt_w1": DEPTH * 64, "filt_w2": DEPTH * 64,
           "filt_w3": DEPTH * 64, "filt_b": DEPTH * 3, "filt_freq": DEPTH * 3,
           "hyena_bias": DEPTH * KH, "norm_ffn": DEPTH * KD, "norm_final": KD}


def starts(widths):
    at, out = 0, {}
    for k, n in widths.items():
        out[k] = at
        at += n
    return out, at


CONST_AT, N_CONST = starts(CONST_W)
PARAM_AT, N_PARAM = starts(PARAM_W)



def chunk_table():
    table, n = {}, 0

    def add(name, count):
        nonlocal n
        table[name] = n
        n += count

    for l in range(DEPTH):
        add(("ag", l), 16)
        add(("qk", l), 16)
        add(("v", l), 4)
        add(("dn", l), 24)
        add(("cz", l), 8)
        add(("c_out", l), 16)
        add(("az", l), 8)
        add(("a_out", l), 16)
        add(("dz", l), 8)
        add(("d_out", l), 16)
        add(("w_out", l), 8)
    for l in range(DEPTH):
        add(("q2", l), 8)
        add(("k2", l), 2)
        add(("v2", l), 4)
        add(("hy2", l), 12)
        add(("o2", l), 32)
        add(("w_out2", l), 8)
        add(("gu", l), 44)
        add(("down", l), 8)
    return table


CHUNK = chunk_table()



TAKEN = {"ag": 16, "cz": 8, "c_out": 16, "az": 8, "a_out": 16, "dz": 8, "d_out": 16, "w_out": 8,
         "o2": 32, "w_out2": 8, "gu": 22, "down": 8}


def take_table():
    table, n = {}, 0
    for name, l in CHUNK:
        if name in TAKEN:
            table[name, l] = n
            n += TAKEN[name]
    return table


TAKE = take_table()


def build(nc, w_stream, params, fw4, pos, xT, ctxT, consts, out):
    F32 = mybir.dt.float32
    I32 = mybir.dt.int32
    ALU = mybir.AluOpType
    ACT = mybir.ActivationFunctionType
    AX = mybir.AxisListType
    MUL, ADD, SUB, MAX = ALU.mult, ALU.add, ALU.subtract, ALU.max
    ctx = ExitStack()
    with ctx:
        def sb(name, *shape, dt=F32):
            return ctx.enter_context(nc.sbuf_tensor(name, [P, *shape], dt))

        made = {}

        def sem(name):
            if name not in made:
                made[name] = ctx.enter_context(nc.semaphore(name))
            return made[name]

        ring = sb("ring", RING, TILES * P)
        cst = sb("cst", N_CONST)
        prm = sb("prm", N_PARAM)
        X = sb("X", KD, 2 * T)
        H = sb("H", KD, 2 * T)
        rstd = sb("rstd", 2 * T)
        take = sb("take", 4, 2 * T)
        sq = sb("sq", 2048)
        hn = sb("hn", 2048)
        at_buf = sb("at_buf", 3072)
        big = sb("big", 15616)
        ba = sb("ba", 9, 2 * HEADS)
        tab = sb("tab", 2, T)
        at_m = sb("at_m", 2, 2)
        at_l = sb("at_l", 2, 2)
        lam = sb("lam", 8)
        mod = sb("mod", N_MOD * KD, 2)
        gains = sb("gains", 2, KD, 2)
        sc = sb("sc", KD, 2)

        def cut(buf, at, *shape):
            n = 1
            for s in shape:
                n *= s
            v = buf[:, at:at + n]
            if len(shape) == 2:
                v = v.rearrange("p (a b) -> p a b", a=shape[0])
            if len(shape) == 3:
                v = v.rearrange("p (a b c) -> p a b c", a=shape[0], b=shape[1])
            return v

        pg = ctx.enter_context(nc.psum_tensor("pg", [P, 4, 512], F32))
        ps = ctx.enter_context(nc.psum_tensor("ps", [P, 4, 512], F32))
        ps_flat = ps[:, :, :].rearrange("p a b -> p (a b)")

        def C(name, at=0, n=None):
            a = CONST_AT[name] + at
            return cst[:, a:a + (n or CONST_W[name])]

        def PR(name, at=0, n=1):
            a = PARAM_AT[name] + at
            return prm[:, a:a + n]

        ident, ones, eps6, eps5 = C("ident"), C("ones"), C("eps6"), C("eps5")

        def rep(ap, n):
            return ap.unsqueeze(1).broadcast_to([P, n, ap.shape[1]])

        def wide(ap, n):
            return ap.unsqueeze(2).broadcast_to([P, ap.shape[1], n])

        QK = cut(big, 0, 16, T)
        V = cut(big, 4096, NT, D)
        U = cut(big, 6144, KD, CONV_K - 1 + T)
        DN = cut(big, 8432, 24, T)
        raw = cut(big, 14576, 4, SHORT_K - 1 + T)
        CV = X[:, :, T:2 * T]
        MG = H[:, :, T:2 * T]
        AT_S = cut(at_buf, 0, 2, 2 * T)
        AT_A = cut(at_buf, 1024, 2, 2 * T)
        AT_T = cut(at_buf, 2048, 2, 2 * T)
        RT = cut(at_buf, 0, 2, 2 * T)
        PAIRS = 4 * P
        DT, LT, IN, LM0, LM1, TT, TM, XS = (cut(big, 2048 + j * PAIRS, PAIRS) for j in range(8))
        VB, UG, IB, VN = (cut(big, 6144 + j * PAIRS, PAIRS) for j in range(4))
        LM = [LM0, LM1]
        KBG, KDEC, NW, S1, QG, EXR = (cut(at_buf, j * 2 * P, 2, P) for j in range(6))
        BETA, G, GC, NGC, BEG, B0, B1, B2 = (ba[:, j, :].rearrange("p (c h) -> p c h", c=NT) for j in range(8))
        EXA = ba[:, 8, 0:HEADS]
        QK_S = QK_DIM ** -0.5
        DN_S = P ** -0.5

        Q2_ = cut(big, 0, HEADS, 2 * T)
        K2_ = cut(big, 4096, 2, 2 * T)
        V2_ = cut(big, 5120, 4, 2 * P)
        X0 = cut(big, 6144, KH, 2 * T)
        X1 = cut(big, 8192, KH, 2 * T)
        VX = cut(big, 10240, KH, 2 * T)
        hraw = cut(big, 12288, 4, T + 2)
        VTK = cut(big, 13320, 4, HY)
        AF = cut(big, 0, KF, 2 * T)
        MG2 = cut(big, 11264, KD, 2 * T)
        W4 = cut(at_buf, 0, 2 * HY)
        HQ = cut(at_buf, 1024, T)
        RR = cut(at_buf, 1280, 3, T)
        KFT = cut(at_buf, 0, 4, HY)
        PROD = cut(at_buf, 2048, 2, HY)
        VFT = hn[:, :].rearrange("p (a b) -> p a b", a=4)
        YFT = sq[:, :].rearrange("p (a b) -> p a b", a=4)
        ANGI = cut(at_buf, 0, T).bitcast(I32)
        POSF = cut(at_buf, 256, T)

        N_TOK = [2 * T, T]
        N_SEQ = [2, 1]
        N_NORM = [T, T, T, 2 * T, 2 * T, 2 * T, T, T]
        mix_norm = [3, 5]
        ffn_norm = [4, 6]
        HN_BASE1 = lambda l: 4 * l
        HN_BASE2 = [8, 11]
        ROPE2 = [16, 21]
        IT2 = [[(h, s, b) for h in range(HEADS) for s in range(n) for b in range(NT)] for n in N_SEQ]
        IT2_BASE = [0, len(IT2[0])]

        def x_done(i):
            return {1: TAKE["w_out", 0] + 8, 2: TAKE["w_out", 1] + 8, 4: TAKE["w_out2", 0] + 8,
                    5: TAKE["down", 0] + 8, 6: TAKE["w_out2", 1] + 8, 7: TAKE["down", 1] + 8}[i]

        block = ctx.enter_context(nc.Block())

        @block.sync
        def _(sp):
            sp.dma_start(X[:, :, 0:T], xT).then_inc(sem("loaded"), 16)
            sp.dma_start(cst[:, :], consts).then_inc(sem("loaded"), 16)
            sp.dma_start(prm[:, :], params).then_inc(sem("loaded"), 16)
            sp.dma_start(ANGI, pos).then_inc(sem("loaded"), 16)
            for s in range(RING):
                sp.dma_start(ring[:, s, :], w_stream[s]).then_inc(sem(f"weights{s}"), 16)
            with sp.Fori(1, N_LOADS // RING) as r:
                for s in range(RING):
                    sp.wait_ge(sem("slot_free"), (r - 1) * RING + (s + 1))
                    sp.dma_start(ring[:, s, :], w_stream[bass.ds(r * RING + s, 1), :, :].rearrange("o p n -> p (o n)"))\
                        .then_inc(sem(f"weights{s}"), 16)

        @block.gpsimd
        def _(pool):
            links = [0]

            def link(ins):
                links[0] += 1
                ins.then_inc(sem("pool_link"), 1)
                pool.wait_ge(sem("pool_link"), links[0])

            def taken(name, l, n):
                return (TAKE[name, l] + n) % 4

            def zero_conv_pad():
                pool.memset(U[:, :, 0:CONV_K - 1], 0.0).then_inc(sem("conv_pad"), 1)

            def conv_gate(l):
                for m in range(KD):
                    a, g = taken("ag", l, 2 * m), taken("ag", l, 2 * m + 1)
                    pool.wait_ge(sem("drained"), CHUNK["ag", l] + 2 * m + 2)
                    pool.tensor_tensor(U[:, m, CONV_K - 1:], take[:, a, 0:T], take[:, g, 0:T], MUL)\
                        .then_inc(sem("take_used"), 2)

            def times_z(name, l, m, branch):
                pool.wait_ge(sem("drained"), CHUNK[name, l] + m + 1)
                pool.tensor_tensor(branch[:, m, :], branch[:, m, :], take[:, taken(name, l, m), 0:T], MUL)\
                    .then_inc(sem("take_used"), 1)

            def merge(name, l, m, first):
                g, y = taken(name, l, 2 * m), taken(name, l, 2 * m + 1)
                pool.wait_ge(sem("drained"), CHUNK[name, l] + 2 * m + 2)
                if first:
                    pool.tensor_tensor(MG[:, m, :], take[:, g, 0:T], take[:, y, 0:T], MUL).then_inc(sem("take_used"), 2)
                else:
                    link(pool.tensor_tensor(take[:, y, 0:T], take[:, g, 0:T], take[:, y, 0:T], MUL))
                    pool.tensor_tensor(MG[:, m, :], MG[:, m, :], take[:, y, 0:T], ADD).then_inc(sem("take_used"), 2)

            def add_to_x(name, l, n):
                for m in range(KD):
                    pool.wait_ge(sem("drained"), CHUNK[name, l] + m + 1)
                    pool.tensor_tensor(X[:, m, 0:n], X[:, m, 0:n], take[:, taken(name, l, m), 0:n], ADD)\
                        .then_inc(sem("take_used"), 1)

            def level_masks(l, u):
                i = 4 * l + u
                pool.wait_ge(sem("d_lt"), i + 1)
                for s in range(7):
                    if s >= 2:
                        pool.wait_ge(sem("d_x"), 6 * i + s - 1)
                    pool.tensor_tensor(LM[s % 2].rearrange("p (a b) -> p a b", a=4),
                                       LT.rearrange("p (a b) -> p a b", a=4),
                                       rep(C("levels", s * P, P), 4), MUL).then_inc(sem("d_lm"), 1)

            pool.memset(raw[:, :, 0:SHORT_K - 1], 0.0).then_inc(sem("raw_pad"), 1)
            for l in range(DEPTH):
                if l:
                    pool.wait_ge(sem("take_used"), x_done(l))
                zero_conv_pad()
                conv_gate(l)
                for m in range(KD):
                    times_z("cz", l, m, CV)
                for m in range(KD):
                    merge("c_out", l, m, True)
                pool.wait_ge(sem("hn_done"), HN_BASE1(l) + 1)
                for m in range(KD):
                    times_z("az", l, m, QK)
                for m in range(KD):
                    merge("a_out", l, m, False)
                for u in range(4):
                    level_masks(l, u)
                pool.wait_ge(sem("hn_done"), HN_BASE1(l) + 4)
                for m in range(KD):
                    times_z("dz", l, m, DN)
                for m in range(KD):
                    merge("d_out", l, m, False)
                add_to_x("w_out", l, T)
            for l in range(DEPTH):
                n = N_TOK[l]
                if l == 0:
                    pool.wait_ge(sem("norm_h"), 3)
                else:
                    pool.wait_ge(sem("take_used"), x_done(5))
                pool.memset(hraw[:, :, 0:1], 0.0)
                pool.memset(hraw[:, :, T + 1:T + 2], 0.0).then_inc(sem("hraw_pad"), 1)
                for m in range(KD):
                    ga, oa, gh, oh = (taken("o2", l, 4 * m + j) for j in range(4))
                    pool.wait_ge(sem("drained"), CHUNK["o2", l] + 4 * m + 2)
                    link(pool.tensor_tensor(MG2[:, m, 0:n], take[:, ga, 0:n], take[:, oa, 0:n], MUL))
                    pool.wait_ge(sem("drained"), CHUNK["o2", l] + 4 * m + 4)
                    link(pool.tensor_tensor(take[:, oh, 0:n], take[:, gh, 0:n], take[:, oh, 0:n], MUL))
                    pool.tensor_tensor(MG2[:, m, 0:n], MG2[:, m, 0:n], take[:, oh, 0:n], ADD)\
                        .then_inc(sem("take_used"), 4)
                add_to_x("w_out2", l, n)
                for i in range(KF):
                    pool.wait_ge(sem("drained"), CHUNK["gu", l] + 2 * i + 2)
                    pool.tensor_tensor(AF[:, i, 0:n], AF[:, i, 0:n], take[:, taken("gu", l, i), 0:n], MUL)\
                        .then_inc(sem("take_used"), 1)
                add_to_x("down", l, n)

        @block.scalar
        def _(act):
            def ready(j):
                act.wait_ge(sem("chunk_ready"), j + 1)
                return pg[:, j % 4, :]

            def drain(j, dst, func=ACT.Copy, n=T):
                act.activation(dst, ready(j)[:, 0:n], func).then_inc(sem("drained"), 1)

            def to_take(name, l, i, at, func=ACT.Copy, n=T):
                q = TAKE[name, l] + at
                if q >= 4:
                    act.wait_ge(sem("take_used"), q - 3)
                drain(CHUNK[name, l] + i, take[:, q % 4, 0:n], func, n)

            def norm(i):
                n = N_NORM[i]
                if i in (0, 3):
                    if i == 0:
                        act.wait_ge(sem("loaded"), 64)
                    else:
                        act.wait_ge(sem("norm_h"), 3)
                        act.wait_ge(sem("ctx_loaded"), 16)
                else:
                    act.wait_ge(sem("take_used"), x_done(i))
                act.activation(H[:, :, 0:n], X[:, :, 0:n], ACT.Square).then_inc(sem("norm_sq"), 1)
                act.wait_ge(sem("norm_ss"), i + 1)
                act.activation(rstd[:, 0:n], ps[:, 0, 0:n], ACT.Sqrt, bias=eps6, scale=1.0 / D)\
                    .then_inc(sem("norm_rms"), 1)

            def head_norm(i, src, scale):
                a, b = src.shape[1], src.shape[2]
                act.activation(sq[:, 0:a * b].rearrange("p (a b) -> p a b", a=a), src, ACT.Square)\
                    .then_inc(sem("hn_sq"), 1)
                act.wait_ge(sem("hn_ss"), i + 1)
                if i >= 1:
                    act.wait_ge(sem("hn_done"), i)
                act.activation(hn[:, 0:a * b], ps_flat[:, 0:a * b], ACT.Sqrt, bias=eps6, scale=scale)\
                    .then_inc(sem("hn_rms"), 1)

            def attention_exp(l, it):
                i = 2 * HEADS * l + it
                e = P * (it % 2 + 1)
                act.wait_ge(sem("att_max"), i + 1)
                for m in range(2):
                    ins = act.activation(AT_S[:, i % 2, m * T:m * T + e], AT_S[:, i % 2, m * T:m * T + e], ACT.Exp,
                                         bias=at_m[:, i % 2, m:m + 1], accum_out=at_l[:, i % 2, m:m + 1])
                ins.then_inc(sem("att_exp"), 1)

            def attention_turned(l, it):
                i = 2 * HEADS * l + it
                e = P * (it % 2 + 1)
                act.wait_ge(sem("att_turn"), i + 1)
                if i >= 2:
                    act.wait_ge(sem("att_o"), i - 1)
                act.activation(AT_T[:, i % 2, 0:e], ps[:, 2, 0:e], ACT.Copy).then_inc(sem("att_turned"), 1)

            def delta_gates(l):
                act.wait_ge(sem("ba_ready"), l + 1)
                both = ps[:, 0, 0:32].rearrange("p (c n) -> p c n", c=NT)
                act.activation(BETA, both[:, :, 0:HEADS], ACT.Sigmoid).then_inc(sem("beta"), 1)
                act.activation(EXA, PR("dn_a_log", l * HEADS, HEADS), ACT.Exp).then_inc(sem("exp_a"), 1)
                act.wait_ge(sem("abs_a"), l + 1)
                act.activation(B1, B1, ACT.Exp, scale=-1.0).then_inc(sem("exp_abs"), 1)
                act.wait_ge(sem("exp_abs"), l + 1)
                act.activation(B2, B1, ACT.Ln, bias=1.0).then_inc(sem("ln_abs"), 1)
                act.wait_ge(sem("gc_ready"), l + 1)
                act.activation(BEG, ps[:, 1, 0:16].rearrange("p (c h) -> p c h", c=NT), ACT.Exp)\
                    .then_inc(sem("exp_gc"), 1)

            def delta(l, u):
                i = 4 * l + u
                sums = ps[:, 0, :].rearrange("p (h c n) -> p h c n", h=2, c=NT)
                act.wait_ge(sem("d_dt"), i + 1)
                act.activation(EXR, sums[:, :, 1, :], ACT.Exp)
                for p in range(4):
                    h, c = 2 * u + p // 2, p % 2
                    ins = act.activation(DT[:, p * P:(p + 1) * P], DT[:, p * P:(p + 1) * P], ACT.Exp,
                                         bias=NGC[:, c, h:h + 1])
                ins.then_inc(sem("d_exp"), 1)
                act.wait_ge(sem("d_t0"), i + 1)
                act.activation(TM, ps[:, 0, :], ACT.Copy).then_inc(sem("d_tm"), 1)
                for s in range(1, 7):
                    act.wait_ge(sem("d_x"), 6 * i + s)
                    act.activation(XS, ps[:, 1, :], ACT.Copy).then_inc(sem("d_xs"), 1)
                act.wait_ge(sem("d_w"), i + 1)
                act.activation(NW, ps[:, 2, 0:2 * P].rearrange("p (a b) -> p a b", a=2), ACT.Copy, scale=-1.0)
                act.activation(VN[:, 0:2 * P], ps[:, 2, 2 * P:4 * P], ACT.Copy).then_inc(sem("d_vn0"), 1)
                act.wait_ge(sem("d_s"), i + 1)
                act.activation(S1, ps[:, 3, 0:2 * P].rearrange("p (a b) -> p a b", a=2), ACT.Copy).then_inc(sem("d_s1"), 1)
                act.wait_ge(sem("d_v1"), i + 1)
                act.activation(VN[:, 2 * P:4 * P], ps[:, 0, 0:2 * P], ACT.Copy).then_inc(sem("d_vn1"), 1)
                act.wait_ge(sem("d_o"), i + 1)
                act.activation(DN[:, 2 * u:2 * u + 2, :], ps[:, 1, :].rearrange("p (a b) -> p a b", a=2), ACT.Copy).then_inc(sem("d_out"), 1)

            act.wait_ge(sem("loaded"), 64)
            act.activation(sc[:, :, :], PR("c", 0, 2 * KD), ACT.Silu).then_inc(sem("silu_c"), 1)
            act.wait_ge(sem("ang"), 1)
            act.activation(tab[:, 1, :], POSF, ACT.Sin)
            act.wait_ge(sem("ang"), 2)
            act.activation(tab[:, 0, :], RR[:, 0, :], ACT.Sin).then_inc(sem("rope_table"), 1)
            act.wait_ge(sem("lam_dots"), 1)
            act.activation(lam[:, 0:4], lam[:, 0:4], ACT.Exp).then_inc(sem("lam_exp"), 1)
            for l in range(DEPTH):
                norm(l)
                for m in range(KD):
                    to_take("ag", l, 2 * m, 2 * m)
                    to_take("ag", l, 2 * m + 1, 2 * m + 1, ACT.Sigmoid)
                for j in range(16):
                    drain(CHUNK["qk", l] + j, QK[:, j, :])
                act.wait_ge(sem("ln_centered"), l + 1)
                act.activation(sq[:, :].rearrange("p (a b) -> p a b", a=KD), CV, ACT.Square).then_inc(sem("ln_sq"), 1)
                for j in range(4):
                    drain(CHUNK["v", l] + j, V[:, j % 2, (j // 2) * 512:(j // 2 + 1) * 512], n=512)
                act.wait_ge(sem("ln_ss"), l + 1)
                act.activation(rstd[:, 0:T], ps[:, 1, 0:T], ACT.Sqrt, bias=eps5, scale=1.0 / D).then_inc(sem("ln_rms"), 1)

                def dn_silu(j):
                    act.wait_ge(sem("sconv"), 24 * l + j + 1)
                    act.activation(DN[:, j, :], DN[:, j, :], ACT.Silu).then_inc(sem("dn_silu"), 1)

                for j in range(24):
                    if 24 * l + j >= 4:
                        act.wait_ge(sem("sconv"), 24 * l + j - 3)
                    if l == 0 and j == 0:
                        act.wait_ge(sem("raw_pad"), 1)
                    drain(CHUNK["dn", l] + j, raw[:, j % 4, SHORT_K - 1:])
                    if j >= 2:
                        dn_silu(j - 2)
                dn_silu(22)
                dn_silu(23)
                act.wait_ge(sem("ln_normed"), l + 1)
                for m in range(KD):
                    act.activation(CV[:, m, :], CV[:, m, :], ACT.Silu, bias=PR("conv_ln_b", l * KD + m),
                                   scale=PR("conv_ln_w", l * KD + m)).then_inc(sem("ln_silu"), 1)
                act.wait_ge(sem("ln_silu"), KD * (l + 1))
                fill = [("cz", m, m, ACT.Silu) for m in range(KD)]
                fill += [("c_out", i, i, ACT.Copy if i % 2 else ACT.Sigmoid) for i in range(2 * KD)]
                for it in range(18):
                    if it < 16:
                        attention_exp(l, it)
                    if 1 <= it <= 16:
                        attention_turned(l, it - 1)
                    for name, i, at, func in fill[24 * it // 18:24 * (it + 1) // 18]:
                        to_take(name, l, i, at, func)
                act.wait_ge(sem("att_out"), 16 * (l + 1))
                head_norm(HN_BASE1(l), QK[:, 0:8, :], 1.0 / P)
                act.wait_ge(sem("dn_silu"), 24 * (l + 1))
                head_norm(HN_BASE1(l) + 1, DN[:, 0:8, :], 1.0)
                head_norm(HN_BASE1(l) + 2, DN[:, 8:16, :], 1.0)
                for m in range(KD):
                    to_take("az", l, m, m, ACT.Silu)
                for m in range(KD):
                    to_take("a_out", l, 2 * m, 2 * m, ACT.Sigmoid)
                    to_take("a_out", l, 2 * m + 1, 2 * m + 1)
                delta_gates(l)
                for u in range(4):
                    delta(l, u)
                act.wait_ge(sem("d_out"), 4 * (l + 1))
                head_norm(HN_BASE1(l) + 3, DN[:, 0:8, :], 1.0 / P)
                for m in range(KD):
                    to_take("dz", l, m, m, ACT.Silu)
                for m in range(KD):
                    to_take("d_out", l, 2 * m, 2 * m, ACT.Sigmoid)
                    to_take("d_out", l, 2 * m + 1, 2 * m + 1)
                for m in range(KD):
                    to_take("w_out", l, m, m)
            norm(2)

            def attention2_exp(i, s):
                n = 2 * T if s == 0 else T
                act.wait_ge(sem("a2_max"), i + 1)
                act.activation(AT_S[:, i % 2, 0:n], ps[:, i % 2, 0:n], ACT.Exp, bias=at_m[:, i % 2, 0:1],
                               scale=P ** -0.5, accum_out=at_l[:, i % 2, 0:1]).then_inc(sem("a2_exp"), 1)

            def attention2_turned(i, s):
                n = 2 * T if s == 0 else T
                act.wait_ge(sem("a2_turn"), i + 1)
                if i >= 2:
                    act.wait_ge(sem("a2_o"), i - 1)
                act.activation(AT_T[:, i % 2, 0:n], ps[:, 2, 0:n], ACT.Copy).then_inc(sem("a2_turned"), 1)

            for l in range(DEPTH):
                n, ns = N_TOK[l], N_SEQ[l]
                if l == 0:
                    act.wait_ge(sem("norm_h"), 3)
                    act.dma_start(X[:, :, T:2 * T], ctxT).then_inc(sem("ctx_loaded"), 16)
                else:
                    act.wait_ge(sem("take_used"), x_done(5))
                act.dma_start(W4[0:64, :], fw4[l]).then_inc(sem("w4_loaded"), 16)
                for k in range(3):
                    act.wait_ge(sem("f_arg"), 3 * l + k + 1)
                    act.activation(HQ[0:64, :], RR[0:64, 0, :], ACT.Sin).then_inc(sem("f_sin"), 1)
                act.wait_ge(sem("kf_ready"), l + 1)
                act.activation(KFT, ps[:, :, :], ACT.Copy).then_inc(sem("kf_done"), 1)
                norm(mix_norm[l])
                for j in range(8):
                    drain(CHUNK["q2", l] + j, Q2_[:, j, 0:n], n=n)
                for j in range(2):
                    drain(CHUNK["k2", l] + j, K2_[:, j, :], n=2 * T)
                for j in range(4):
                    drain(CHUNK["v2", l] + j, V2_[:, j, :], n=2 * P)
                act.wait_ge(sem("drained"), CHUNK["v2", l] + 4)
                i = HN_BASE2[l]
                if l == 0:
                    head_norm(i, Q2_[:, 0:4, :], 1.0 / P)
                    head_norm(i + 1, Q2_[:, 4:8, :], 1.0 / P)
                    head_norm(i + 2, K2_, 1.0 / P)
                else:
                    head_norm(i, Q2_[:, :, 0:T], 1.0 / P)
                    head_norm(i + 1, K2_, 1.0 / P)
                act.wait_ge(sem("hraw_pad"), l + 1)
                for j in range(12):
                    if 12 * l + j >= 2:
                        act.wait_ge(sem("hconv"), 12 * l + j - 1)
                    s0 = (j % 2) * 2
                    act.activation(hraw[:, s0:s0 + ns, 1:T + 1],
                                   ready(CHUNK["hy2", l] + j)[:, 0:n].rearrange("p (s t) -> p s t", s=ns), ACT.Copy)\
                        .then_inc(sem("drained"), 1)
                act.wait_ge(sem("vt_ready"), l + 1)
                act.activation(VTK[:, 0:2 * ns, :], ps[:, 0:2 * ns, :], ACT.Copy).then_inc(sem("vt_done"), 1)
                for s in range(ns):
                    act.wait_ge(sem("vf_ready"), 2 * l + s + 1)
                    act.activation(VFT, ps[:, :, :], ACT.Copy).then_inc(sem("vf_done"), 1)
                steps = IT2[l]
                for k in range(len(steps) + 1):
                    if k < len(steps):
                        attention2_exp(IT2_BASE[l] + k, steps[k][1])
                    if k >= 1:
                        attention2_turned(IT2_BASE[l] + k - 1, steps[k - 1][1])
                for i in range(32):
                    to_take("o2", l, i, i, ACT.Copy if i % 2 else ACT.Sigmoid, n)

                def gated(name, m, which):
                    q = TAKE[name, l] + m
                    act.wait_ge(sem("take_used"), q - 3)
                    src = ready(CHUNK[name, l] + m)
                    for s in range(ns):
                        ins = act.activation(take[:, q % 4, s * T:(s + 1) * T], src[:, s * T:(s + 1) * T], ACT.Copy,
                                             scale=mod[:, which * KD + m, s:s + 1])
                    ins.then_inc(sem("drained"), 1)

                for m in range(KD):
                    gated("w_out2", m, 2)
                norm(ffn_norm[l])
                for i in range(KF):
                    drain(CHUNK["gu", l] + 2 * i, AF[:, i, 0:n], ACT.Silu, n)
                    to_take("gu", l, 2 * i + 1, i, n=n)
                for m in range(KD):
                    gated("down", m, 5)
            norm(7)
            act.wait_ge(sem("norm_h"), 8)
            act.dma_start(out, H[:, :, 0:T]).then_inc(sem("stored"), 16)
            act.wait_ge(sem("stored"), 16)

        @block.vector
        def _(dve):
            links = [0]

            def link(ins):
                links[0] += 1
                ins.then_inc(sem("dve_link"), 1)
                dve.wait_ge(sem("dve_link"), links[0])

            def within_pi(dst, arg, n, tmp, shift=0.0):
                magic = 1.5 * 2.0 ** 23
                c1 = 6.28125
                c2 = math.floor((TWO_PI - c1) * 2.0 ** 22) / 2.0 ** 22
                c3 = TWO_PI - c1 - c2
                link(dve.tensor_scalar(tmp, arg, 1.0 / TWO_PI, shift / TWO_PI, MUL, ADD))
                link(dve.tensor_scalar(tmp, tmp, magic, None, ADD))
                link(dve.tensor_scalar(tmp, tmp, -magic, None, ADD))
                link(dve.scalar_tensor_tensor(dst, tmp, -c1, arg, MUL, ADD))
                link(dve.scalar_tensor_tensor(dst, tmp, -c2, dst, MUL, ADD))
                link(dve.scalar_tensor_tensor(dst, tmp, -c3, dst, MUL, ADD))
                if shift:
                    link(dve.tensor_scalar(dst, dst, shift, None, ADD))
                lim = 3.1415925
                return dve.tensor_scalar(dst, dst, lim, -lim, ALU.min, MAX)

            def norm(i, gain, at, dst=None):
                dst = H if dst is None else dst
                n = N_NORM[i]
                dve.wait_ge(sem("norm_rms"), i + 1)
                link(dve.reciprocal(rstd[:, 0:n], rstd[:, 0:n]))
                for k in range(KD):
                    ins = dve.scalar_tensor_tensor(dst[:, k, 0:n], X[:, k, 0:n], PR(gain, at + k), rstd[:, 0:n], MUL, MUL)
                ins.then_inc(sem("norm_h"), 1)

            def norm_mod(i, which):
                n = N_NORM[i]
                dve.wait_ge(sem("norm_rms"), i + 1)
                link(dve.reciprocal(rstd[:, 0:n], rstd[:, 0:n]))
                link(dve.tensor_tensor(H[:, :, 0:n], X[:, :, 0:n], rep(rstd[:, 0:n], KD), MUL))
                for k in range(KD):
                    for s in range(n // T):
                        ins = dve.tensor_scalar(H[:, k, s * T:(s + 1) * T], H[:, k, s * T:(s + 1) * T],
                                                gains[:, which, k, s:s + 1], mod[:, 3 * which * KD + k, s:s + 1], MUL, ADD)
                ins.then_inc(sem("norm_h"), 1)

            def head_norm(i, dst, gain):
                a, b = dst.shape[1], dst.shape[2]
                dve.wait_ge(sem("hn_rms"), i + 1)
                link(dve.reciprocal(hn[:, 0:a * b], hn[:, 0:a * b]))
                dve.scalar_tensor_tensor(dst, dst, gain, hn[:, 0:a * b].rearrange("p (a b) -> p a b", a=a), MUL, MUL)\
                    .then_inc(sem("hn_done"), 1)

            def conv31(l, m):
                dve.wait_ge(sem("take_used"), TAKE["ag", l] + 2 * m + 2)
                dve.wait_ge(sem("conv_pad"), l + 1)
                w = (l * KD + m) * CONV_K
                link(dve.tensor_scalar(CV[:, m, :], U[:, m, 0:T], PR("conv_dw_w", w), PR("conv_dw_b", l * KD + m), MUL, ADD))
                for t in range(1, CONV_K):
                    ins = dve.scalar_tensor_tensor(CV[:, m, :], U[:, m, t:t + T], PR("conv_dw_w", w + t), CV[:, m, :], MUL, ADD)
                    if t < CONV_K - 1:
                        link(ins)
                ins.then_inc(sem("conv_done"), 1)

            def sconv(l, j):
                dve.wait_ge(sem("drained"), CHUNK["dn", l] + j + 1)
                w = (l * 24 + j) * SHORT_K
                link(dve.tensor_scalar(DN[:, j, :], raw[:, j % 4, 0:T], PR("dn_conv_w", w), None, MUL))
                for t in range(1, SHORT_K):
                    ins = dve.scalar_tensor_tensor(DN[:, j, :], raw[:, j % 4, t:t + T], PR("dn_conv_w", w + t), DN[:, j, :], MUL, ADD)
                    if t < SHORT_K - 1:
                        link(ins)
                ins.then_inc(sem("sconv"), 1)

            def attention_scores(l, it):
                i = 2 * HEADS * l + it
                b = it % 2
                e = P * (b + 1)
                dve.wait_ge(sem("att_scores"), i + 1)
                s = AT_S[:, i % 2, :].rearrange("p (m k) -> p m k", m=2)[:, :, 0:e]
                mask = C("causal1", P, P) if b == 0 else C("causal1")
                dve.scalar_tensor_tensor(s, ps[:, 0:2, 0:e], QK_S,
                                         rep(mask, 2), MUL, ADD).then_inc(sem("att_masked"), 1)
                dve.wait_ge(sem("att_masked"), i + 1)
                dve.tensor_reduce(at_m[:, i % 2, :], s, AX.X, MAX, negate=True).then_inc(sem("att_max"), 1)

            def attention_weights(l, it):
                i = 2 * HEADS * l + it
                e = P * (it % 2 + 1)
                dve.wait_ge(sem("att_exp"), i + 1)
                if i >= 2:
                    dve.wait_ge(sem("att_turn"), i - 1)
                r = at_l[:, i % 2, :]
                link(dve.reciprocal(r, r))
                link(dve.tensor_scalar(r[:, 1:2], r[:, 1:2], lam[:, 4 + l:5 + l], None, MUL))
                link(dve.tensor_scalar(AT_A[:, i % 2, 0:e], AT_S[:, i % 2, 0:e], r[:, 0:1], None, MUL))
                dve.scalar_tensor_tensor(AT_A[:, i % 2, 0:e], AT_S[:, i % 2, T:T + e], r[:, 1:2], AT_A[:, i % 2, 0:e], MUL, ADD)\
                    .then_inc(sem("att_weights"), 1)

            def attention_out(l, it):
                i = 2 * HEADS * l + it
                dve.wait_ge(sem("att_o"), i + 1)
                dve.tensor_copy(QK[:, it // 2, (it % 2) * P:(it % 2 + 1) * P], ps[:, 3, 0:P]).then_inc(sem("att_out"), 1)

            def delta_gates(l):
                dve.wait_ge(sem("beta"), l + 1)
                both = ps[:, 0, 0:32].rearrange("p (c n) -> p c n", c=NT)
                link(dve.tensor_tensor(B0, both[:, :, HEADS:], rep(PR("dn_dt_bias", l * HEADS, HEADS), NT), ADD))
                dve.scalar_tensor_tensor(B1, B0, -1.0, B0, MUL, MAX).then_inc(sem("abs_a"), 1)
                dve.wait_ge(sem("ln_abs"), l + 1)
                link(dve.tensor_scalar(GC, B1, 1.0, None, ADD))
                link(dve.tensor_scalar(NGC, GC, -1.0, None, ADD))
                link(dve.tensor_tensor(NGC, B1, NGC, SUB))
                link(dve.reciprocal(GC, GC))
                link(dve.tensor_tensor(NGC, NGC, GC, MUL))
                link(dve.tensor_tensor(B2, B2, NGC, ADD))
                link(dve.scalar_tensor_tensor(B0, B0, 0.0, B2, MAX, ADD))
                dve.wait_ge(sem("exp_a"), l + 1)
                dve.scalar_tensor_tensor(G, B0, -1.0, rep(EXA, NT), MUL, MUL).then_inc(sem("g_done"), 1)
                dve.wait_ge(sem("exp_gc"), l + 1)
                link(dve.tensor_scalar(NGC, ps[:, 1, 0:16].rearrange("p (c h) -> p c h", c=NT), -1.0, None, MUL))
                dve.tensor_tensor(BEG, BEG, BETA, MUL).then_inc(sem("gates_done"), 1)
                dve.wait_ge(sem("gates_done"), l + 1)

            def delta(l, u):
                i = 4 * l + u
                q4 = lambda ap: ap.rearrange("p (a b) -> p a b", a=4)
                for p in range(4):
                    h, c = 2 * u + p // 2, p % 2
                    dve.tensor_scalar(UG[:, p * P:(p + 1) * P], C("until"), G[:, c, h:h + 1], None, MUL)
                    ins = dve.tensor_scalar(IB[:, p * P:(p + 1) * P], ident, BETA[:, c, h:h + 1], None, MUL)
                ins.then_inc(sem("d_ugib"), 1)
                dve.wait_ge(sem("d_pre"), 4 * i + 1)
                dve.tensor_tensor(q4(DT), q4(ps[:, 0, :]), rep(C("later"), 4), ADD).then_inc(sem("d_dt"), 1)
                dve.wait_ge(sem("d_pre"), 4 * i + 4)
                dve.wait_ge(sem("d_exp"), i + 1)
                link(dve.tensor_tensor(LT, ps[:, 2, :], DT, MUL))
                dve.tensor_tensor(IN, ps[:, 3, :], DT, MUL)
                dve.tensor_tensor(LT, LT, ps[:, 1, :], MUL).then_inc(sem("d_lt"), 1)
                dve.tensor_tensor(QG, DN[:, 2 * u:2 * u + 2, P:T], EXR, MUL).then_inc(sem("d_qg"), 1)
                dve.wait_ge(sem("d_lm"), 7 * i + 1)
                dve.scalar_tensor_tensor(q4(TT), q4(LM[0]), -1.0, rep(ident, 4), MUL, ADD).then_inc(sem("d_tt"), 1)
                dve.wait_ge(sem("d_tt"), i + 1)
                for s in range(1, 7):
                    dve.wait_ge(sem("d_bc"), 6 * i + s)
                    if s < 6:
                        if s == 1:
                            dve.wait_ge(sem("d_tm"), i + 1)
                        dve.tensor_tensor(TM, TM, ps[:, 3, :], SUB)
                    dve.tensor_tensor(TT, TT, ps[:, 2, :], SUB).then_inc(sem("d_upd"), 1)
                    dve.wait_ge(sem("d_upd"), 6 * i + s)
                dve.wait_ge(sem("d_kv"), i + 1)
                for p in range(4):
                    h, c = 2 * u + p // 2, p % 2
                    dve.tensor_scalar(VB[:, p * P:(p + 1) * P], ps[:, 1, p * P:(p + 1) * P], BETA[:, c, h:h + 1], None, MUL)
                    if c:
                        ins = dve.tensor_scalar(KBG[:, p // 2, :], ps[:, 0, p * P:(p + 1) * P], BEG[:, 1, h:h + 1], None, MUL)
                    else:
                        dve.tensor_scalar(KDEC[:, p // 2, :], ps[:, 0, p * P:(p + 1) * P],
                                          DT[:, (p + 1) * P - 1:(p + 1) * P], None, MUL)
                ins.then_inc(sem("d_vb"), 1)

            dve.wait_ge(sem("loaded"), 64)
            link(dve.tensor_copy(POSF, ANGI))
            link(dve.tensor_scalar(RR[:, 1, :], POSF, C("inv1"), None, MUL))
            within_pi(POSF, RR[:, 1, :], T, RR[:, 2, :]).then_inc(sem("ang"), 1)
            within_pi(RR[:, 0, :], RR[:, 1, :], T, RR[:, 2, :], math.pi / 2).then_inc(sem("ang"), 1)
            lqp = RR[:, 1:3, :].rearrange("p a b -> p (a b)")[:, 0:4 * QK_DIM]
            lq = PR("lam_qk", 0, DEPTH * 4 * QK_DIM).rearrange("p (l a d) -> p l a d", a=4, d=QK_DIM)
            for l in range(DEPTH):
                for a in range(2):
                    link(dve.tensor_tensor(lqp[:, (2 * l + a) * QK_DIM:(2 * l + a + 1) * QK_DIM], lq[:, l, 2 * a, :], lq[:, l, 2 * a + 1, :], MUL))
            dve.tensor_reduce(lam[:, 0:4], lqp.rearrange("p (a d) -> p a d", a=4), AX.X, ADD).then_inc(sem("lam_dots"), 1)
            dve.wait_ge(sem("lam_exp"), 1)
            for l in range(DEPTH):
                link(dve.tensor_tensor(lam[:, 4 + l:5 + l], lam[:, 2 * l + 1:2 * l + 2], lam[:, 2 * l:2 * l + 1], SUB))
                link(dve.tensor_tensor(lam[:, 4 + l:5 + l], lam[:, 4 + l:5 + l], C("lam_init", l, 1), SUB))
            for l in range(DEPTH):
                link(dve.tensor_scalar(lam[:, 6 + l:7 + l], PR("attn_subln_w", l), 1.0 - (0.8 - 0.6 * math.exp(-0.3 * l)), None, MUL))
            dve.wait_ge(sem("rope_table"), 1)
            for l in range(DEPTH):
                norm(l, "norm_w", l * KD)
                for m in range(KD):
                    conv31(l, m)
                dve.wait_ge(sem("ln_mean"), l + 1)
                dve.scalar_tensor_tensor(CV, rep(ps[:, 0, 0:T], KD), -1.0 / D, CV, MUL, ADD).then_inc(sem("ln_centered"), 1)
                dve.wait_ge(sem("ln_centered"), l + 1)
                dve.wait_ge(sem("ln_rms"), l + 1)
                link(dve.reciprocal(rstd[:, 0:T], rstd[:, 0:T]))
                dve.tensor_tensor(CV, CV, rep(rstd[:, 0:T], KD), MUL).then_inc(sem("ln_normed"), 1)
                for jj in range(8):
                    rope1 = QK[:, 2 * jj:2 * jj + 2, :]
                    i = 8 * l + jj
                    if i:
                        dve.wait_ge(sem("rope"), i)
                    dve.wait_ge(sem("rot"), i + 1)
                    link(dve.tensor_tensor(cut(at_buf, 0, 2, T), rope1, rep(tab[:, 0, :], 2), MUL))
                    link(dve.tensor_tensor(cut(at_buf, 512, 2, T), ps[:, 2 + i % 2, :].rearrange("p (a b) -> p a b", a=2),
                                           rep(tab[:, 1, :], 2), MUL))
                    dve.tensor_tensor(rope1, cut(at_buf, 0, 2, T), cut(at_buf, 512, 2, T), ADD).then_inc(sem("rope"), 1)
                for j in range(24):
                    sconv(l, j)
                for it in range(18):
                    if it < 16:
                        attention_scores(l, it)
                    if 1 <= it <= 16:
                        attention_weights(l, it - 1)
                    if it >= 2:
                        attention_out(l, it - 2)
                head_norm(HN_BASE1(l), QK[:, 0:8, :], lam[:, 6 + l:7 + l])
                head_norm(HN_BASE1(l) + 1, DN[:, 0:8, :], DN_S)
                head_norm(HN_BASE1(l) + 2, DN[:, 8:16, :], 1.0)
                delta_gates(l)
                for u in range(4):
                    delta(l, u)
                head_norm(HN_BASE1(l) + 3, DN[:, 0:8, :], PR("dn_norm_w", l))
            norm(2, "final_norm_w", 0, X)

            def attention2_max(i, s):
                n = 2 * T if s == 0 else T
                dve.wait_ge(sem("a2_scores"), i + 1)
                link(dve.tensor_reduce(at_m[:, i % 2, 0:1], ps[:, i % 2, 0:n], AX.X, MAX, negate=True))
                dve.tensor_scalar(at_m[:, i % 2, 0:1], at_m[:, i % 2, 0:1], P ** -0.5, None, MUL).then_inc(sem("a2_max"), 1)

            def attention2_weights(i, s):
                n = 2 * T if s == 0 else T
                dve.wait_ge(sem("a2_exp"), i + 1)
                if i >= 2:
                    dve.wait_ge(sem("a2_turn"), i - 1)
                link(dve.reciprocal(at_l[:, i % 2, 0:1], at_l[:, i % 2, 0:1]))
                dve.tensor_scalar(AT_A[:, i % 2, 0:n], AT_S[:, i % 2, 0:n], at_l[:, i % 2, 0:1], None, MUL)\
                    .then_inc(sem("a2_weights"), 1)

            def attention2_out(i, step):
                h, s, b = step
                dve.wait_ge(sem("a2_o"), i + 1)
                dve.tensor_copy(Q2_[:, h, s * T + b * P:s * T + (b + 1) * P], ps[:, 3, 0:P]).then_inc(sem("a2_out"), 1)

            for l in range(DEPTH):
                n, ns = N_TOK[l], N_SEQ[l]
                dve.wait_ge(sem("mod_ready"), l + 1)
                if l:
                    dve.wait_ge(sem("drained"), CHUNK["down", l - 1] + KD)
                link(dve.tensor_tensor(mod[:, :, :], ps[:, 0, 0:2 * N_MOD * KD].rearrange("p (a b) -> p a b", b=2),
                                       wide(PR("b_mod", l * N_MOD * KD, N_MOD * KD), 2), ADD))
                for which, gain in ((0, "norm_mix"), (1, "norm_ffn")):
                    at = (3 * which + 1) * KD
                    ins = dve.scalar_tensor_tensor(gains[:, which, :, :], mod[:, at:at + KD, :], 1.0,
                                                   wide(PR(gain, l * KD, KD), 2), ADD, MUL)
                ins.then_inc(sem("mod_done"), 1)
                dve.wait_ge(sem("mod_done"), l + 1)
                for k in range(3):
                    dve.wait_ge(sem("f_ready"), 3 * l + k + 1)
                    link(dve.tensor_scalar(RR[0:64, 1, :], ps[0:64, 1, 0:T], PR("filt_b", 3 * l + k)[0:64], PR("filt_freq", 3 * l + k)[0:64], ADD, MUL))
                    within_pi(RR[0:64, 0, :], RR[0:64, 1, :], T, RR[0:64, 2, :]).then_inc(sem("f_arg"), 1)
                dve.wait_ge(sem("h4_ready"), l + 1)
                for half in range(2):
                    ins = dve.tensor_tensor(VTK[:, 2 * half:2 * half + 2, :], ps[:, 2 * half:2 * half + 2, :],
                                            C("decay").rearrange("p (a b) -> p a b", a=NT), MUL)
                ins.then_inc(sem("h4_done"), 1)
                norm_mod(mix_norm[l], 0)
                i = HN_BASE2[l]
                if l == 0:
                    head_norm(i, Q2_[:, 0:4, :], PR("q_norm", l))
                    head_norm(i + 1, Q2_[:, 4:8, :], PR("q_norm", l))
                    head_norm(i + 2, K2_, PR("k_norm", l))
                else:
                    head_norm(i, Q2_[:, :, 0:T], PR("q_norm", l))
                    head_norm(i + 1, K2_, PR("k_norm", l))
                for j in range(12):
                    dve.wait_ge(sem("drained"), CHUNK["hy2", l] + j + 1)
                    s0 = (j % 2) * 2
                    dst = (X0, X1, VX)[j // 4][:, j % 4, 0:n].rearrange("p (s t) -> p s t", s=ns)
                    w = (l * 12 + j) * HY_TAPS
                    link(dve.tensor_scalar(dst, hraw[:, s0:s0 + ns, 0:T], PR("conv_w", w), PR("conv_b", l * 12 + j), MUL, ADD))
                    link(dve.scalar_tensor_tensor(dst, hraw[:, s0:s0 + ns, 1:T + 1], PR("conv_w", w + 1), dst, MUL, ADD))
                    ins = dve.scalar_tensor_tensor(dst, hraw[:, s0:s0 + ns, 2:T + 2], PR("conv_w", w + 2), dst, MUL, ADD)
                    if j >= 8:
                        link(ins)
                        ins = dve.tensor_tensor(VX[:, j - 8, 0:n], VX[:, j - 8, 0:n], X1[:, j - 8, 0:n], MUL)
                    ins.then_inc(sem("hconv"), 1)
                for s in range(ns):
                    k = 2 * l + s
                    re, im = slice(0, 2), slice(2, 4)
                    dve.wait_ge(sem("vf_done"), k + 1)
                    dve.wait_ge(sem("kf_done"), l + 1)
                    dve.tensor_tensor(YFT[:, re, :], VFT[:, re, :], KFT[:, re, :], MUL)
                    link(dve.tensor_tensor(PROD, VFT[:, im, :], KFT[:, im, :], MUL))
                    dve.tensor_tensor(YFT[:, im, :], VFT[:, re, :], KFT[:, im, :], MUL)
                    link(dve.tensor_tensor(YFT[:, re, :], YFT[:, re, :], PROD, SUB))
                    link(dve.tensor_tensor(PROD, VFT[:, im, :], KFT[:, re, :], MUL))
                    link(dve.tensor_tensor(YFT[:, im, :], YFT[:, im, :], PROD, ADD))
                    dve.tensor_tensor(YFT[0:1, 0, :], VFT[0:1, 0, :], KFT[0:1, 0, :], MUL)
                    dve.tensor_tensor(YFT[0:1, 2, :], VFT[0:1, 2, :], KFT[0:1, 2, :], MUL).then_inc(sem("y_done"), 1)
                    dve.wait_ge(sem("yi_ready"), k + 1)
                    for m in range(KH):
                        link(dve.scalar_tensor_tensor(VX[:, m, s * T:(s + 1) * T], VX[:, m, s * T:(s + 1) * T], PR("hyena_bias", l * KH + m),
                                                      ps[:, m // 2, (m % 2) * T:(m % 2 + 1) * T], MUL, ADD))
                    dve.tensor_tensor(X0[:, :, s * T:(s + 1) * T], X0[:, :, s * T:(s + 1) * T], VX[:, :, s * T:(s + 1) * T], MUL)\
                        .then_inc(sem("hyena"), 1)
                for jj in range(5):
                    qk = Q2_[:, 2 * jj:2 * jj + 2, 0:T] if jj < 4 else K2_[:, :, 0:T]
                    i = ROPE2[l] + jj
                    dve.wait_ge(sem("rope"), i)
                    dve.wait_ge(sem("rot"), i + 1)
                    link(dve.tensor_tensor(cut(at_buf, 0, 2, T), qk, rep(C("cos2"), 2), MUL))
                    link(dve.tensor_tensor(cut(at_buf, 512, 2, T), ps[:, 2 + i % 2, :].rearrange("p (a b) -> p a b", a=2),
                                           rep(C("sin2"), 2), MUL))
                    dve.tensor_tensor(qk, cut(at_buf, 0, 2, T), cut(at_buf, 512, 2, T), ADD).then_inc(sem("rope"), 1)
                steps = IT2[l]
                for k in range(len(steps) + 2):
                    i = IT2_BASE[l] + k
                    if k < len(steps):
                        attention2_max(i, steps[k][1])
                    if 1 <= k <= len(steps):
                        attention2_weights(i - 1, steps[k - 1][1])
                    if k >= 2:
                        attention2_out(i - 2, steps[k - 2])
                norm_mod(ffn_norm[l], 1)
            norm(7, "norm_final", 0)
        @block.tensor
        def _(pe):
            at = {"tile": 0, "free": 0, "chunk": 0}

            def tile(n=1):
                t = at["tile"]
                at["tile"] += n
                load, off = divmod(t, TILES)
                if off == 0:
                    pe.wait_ge(sem(f"weights{load % RING}"), 16 * (load // RING + 1))
                assert off + n <= TILES
                if off + n == TILES:
                    at["free"] += 1
                return ring[:, load % RING, off * P:(off + n) * P]

            def chunk(name, l, i, k, rhs, n):
                j = CHUNK[name, l] + i
                assert j == at["chunk"], (name, l, i)
                at["chunk"] += 1
                if j >= 4:
                    pe.wait_ge(sem("drained"), j - 3)
                for c in range(k):
                    freed = at["free"]
                    ins = pe.matmul(pg[:, j % 4, 0:n], tile(), rhs(c), start=c == 0, stop=c == k - 1)
                    if freed and c < k - 1:
                        ins.then_inc(sem("slot_free"), freed)
                        at["free"] -= freed
                ins.then_inc(sem("chunk_ready"), 1)

            def rows_of(buf, n):
                return lambda c: buf[:, c, 0:n]

            def norm(i):
                n = N_NORM[i]
                pe.wait_ge(sem("norm_sq"), i + 1)
                for k in range(KD):
                    ins = pe.matmul(ps[:, 0, 0:n], ones, H[:, k, 0:n], start=k == 0, stop=k == KD - 1)
                ins.then_inc(sem("norm_ss"), 1)

            def head_norm(i, cols):
                pe.wait_ge(sem("hn_sq"), i + 1)
                for b in range(cols // 512):
                    ins = pe.matmul(ps[:, b, :], ones, sq[:, b * 512:(b + 1) * 512], start=True, stop=True)
                ins.then_inc(sem("hn_ss"), 1)

            def rot(i, table, qk):
                if i >= 2:
                    pe.wait_ge(sem("rope"), i - 1)
                pe.matmul(ps[:, 2 + i % 2, :], table, qk, start=True, stop=True).then_inc(sem("rot"), 1)

            def tokens_first(name, l, i, w, tt, n, freed=0):
                j = CHUNK[name, l] + i
                assert j == at["chunk"]
                at["chunk"] += 1
                if j >= 4:
                    pe.wait_ge(sem("drained"), j - 3)
                for k in range(KD):
                    ins = pe.matmul(pg[:, j % 4, 0:n], H[:, k, tt * P:(tt + 1) * P], w[k], start=k == 0, stop=k == KD - 1)
                    if freed and k == 0:
                        ins.then_inc(sem("slot_free"), freed)
                        at["free"] -= freed
                ins.then_inc(sem("chunk_ready"), 1)

            def attention_scores(l, it):
                i = 2 * HEADS * l + it
                h, b = it // 2, it % 2
                e = P * (b + 1)
                if i >= 1:
                    pe.wait_ge(sem("att_masked"), i)
                for m in range(2):
                    r = slice(m * QK_DIM, (m + 1) * QK_DIM)
                    ins = pe.matmul(ps[:, m, 0:e], QK[r, h, b * P:(b + 1) * P], QK[r, HEADS + h, 0:e],
                                    start=True, stop=True)
                ins.then_inc(sem("att_scores"), 1)

            def attention_turn(l, it):
                i = 2 * HEADS * l + it
                pe.wait_ge(sem("att_weights"), i + 1)
                if i >= 1:
                    pe.wait_ge(sem("att_turned"), i)
                for kb in range(it % 2 + 1):
                    ins = pe.transpose(ps[:, 2, kb * P:(kb + 1) * P], AT_A[:, i % 2, kb * P:(kb + 1) * P], ident)
                ins.then_inc(sem("att_turn"), 1)

            def attention_out(l, it):
                i = 2 * HEADS * l + it
                h, b = it // 2, it % 2
                pe.wait_ge(sem("att_turned"), i + 1)
                if i >= 1:
                    pe.wait_ge(sem("att_out"), i)
                for kb in range(b + 1):
                    ins = pe.matmul(ps[:, 3, 0:P], V[:, kb, h * P:(h + 1) * P], AT_T[:, i % 2, kb * P:(kb + 1) * P],
                                    start=kb == 0, stop=kb == b)
                ins.then_inc(sem("att_o"), 1)

            def delta_gates(l):
                pe.wait_ge(sem("hn_rms"), HN_BASE1(l) + 3)
                for c in range(NT):
                    for k in range(KD):
                        a = (l * KD + k) * 16
                        ins = pe.matmul(ps[:, 0, c * 16:(c + 1) * 16], H[:, k, c * P:(c + 1) * P], PR("w_ba", a, 16),
                                        start=k == 0, stop=k == KD - 1)
                ins.then_inc(sem("ba_ready"), 1)
                pe.wait_ge(sem("g_done"), l + 1)
                for c in range(NT):
                    ins = pe.matmul(ps[:, 1, c * HEADS:(c + 1) * HEADS], C("until"), G[:, c, :], start=True, stop=True)
                ins.then_inc(sem("gc_ready"), 1)

            def delta(l, u):
                i = 4 * l + u
                pair = [(2 * u + p // 2, p % 2, slice(p * P, (p + 1) * P)) for p in range(4)]
                kT = lambda h, c: DN[:, HEADS + h, c * P:(c + 1) * P]
                vT = lambda h, c: DN[:, 2 * HEADS + h, c * P:(c + 1) * P]
                pe.wait_ge(sem("d_ugib"), i + 1)
                if u == 0:
                    pe.wait_ge(sem("gates_done"), l + 1)
                else:
                    pe.wait_ge(sem("d_out"), i)
                pe.matmul(ps[:, 0, :], ones, UG, start=True, stop=True).then_inc(sem("d_pre"), 1)
                pe.matmul(ps[:, 1, :], ones, IB, start=True, stop=True).then_inc(sem("d_pre"), 1)
                pe.wait_ge(sem("hn_done"), HN_BASE1(l) + 3)
                for h, c, s in pair:
                    ins = pe.matmul(ps[:, 2, s], kT(h, c), kT(h, c), start=True, stop=True)
                ins.then_inc(sem("d_pre"), 1)
                for h, c, s in pair:
                    ins = pe.matmul(ps[:, 3, s], kT(h, c), DN[:, h, c * P:(c + 1) * P], start=True, stop=True)
                ins.then_inc(sem("d_pre"), 1)
                pe.wait_ge(sem("d_tt"), i + 1)
                for h, c, s in pair:
                    ins = pe.transpose(ps[:, 0, s], TT[:, s], ident)
                ins.then_inc(sem("d_t0"), 1)
                pe.wait_ge(sem("d_tm"), i + 1)
                for v in range(1, 7):
                    pe.wait_ge(sem("d_lm"), 7 * i + v + 1)
                    if v > 1:
                        pe.wait_ge(sem("d_upd"), 6 * i + v - 1)
                    for h, c, s in pair:
                        ins = pe.matmul(ps[:, 1, s], LM[v % 2][:, s], TM[:, s], start=True, stop=True)
                    ins.then_inc(sem("d_x"), 1)
                    pe.wait_ge(sem("d_xs"), 6 * i + v)
                    if v < 6:
                        for h, c, s in pair:
                            pe.matmul(ps[:, 3, s], TT[:, s], XS[:, s], start=True, stop=True)
                    for h, c, s in pair:
                        ins = pe.matmul(ps[:, 2, s], XS[:, s], TT[:, s], start=True, stop=True)
                    ins.then_inc(sem("d_bc"), 1)
                for h, c, s in pair:
                    pe.transpose(ps[:, 0, s], kT(h, c), ident)
                for h, c, s in pair:
                    ins = pe.transpose(ps[:, 1, s], vT(h, c), ident)
                ins.then_inc(sem("d_kv"), 1)
                pe.wait_ge(sem("d_vb"), i + 1)
                for hh in range(2):
                    pe.matmul(ps[:, 2, hh * P:(hh + 1) * P], KBG[:, hh, :], TT[:, pair[2 * hh + 1][2]], start=True, stop=True)
                for hh in range(2):
                    s = pair[2 * hh][2]
                    ins = pe.matmul(ps[:, 2, (2 + hh) * P:(3 + hh) * P], TT[:, s], VB[:, s], start=True, stop=True)
                ins.then_inc(sem("d_w"), 1)
                pe.wait_ge(sem("d_vn0"), i + 1)
                for hh in range(2):
                    ins = pe.matmul(ps[:, 3, hh * P:(hh + 1) * P], KDEC[:, hh, :], VN[:, hh * P:(hh + 1) * P], start=True, stop=True)
                ins.then_inc(sem("d_s"), 1)
                pe.wait_ge(sem("d_s1"), i + 1)
                for hh in range(2):
                    s = pair[2 * hh + 1][2]
                    pe.matmul(ps[:, 0, hh * P:(hh + 1) * P], TT[:, s], VB[:, s], start=True, stop=False)
                    ins = pe.matmul(ps[:, 0, hh * P:(hh + 1) * P], NW[:, hh, :], S1[:, hh, :], start=False, stop=True)
                ins.then_inc(sem("d_v1"), 1)
                pe.wait_ge(sem("d_vn1"), i + 1)
                pe.wait_ge(sem("d_qg"), i + 1)
                for hh in range(2):
                    o = hh * T
                    pe.matmul(ps[:, 1, o:o + P], VN[:, hh * P:(hh + 1) * P], IN[:, pair[2 * hh][2]], start=True, stop=True)
                    pe.matmul(ps[:, 1, o + P:o + T], S1[:, hh, :], QG[:, hh, :], start=True, stop=False)
                    ins = pe.matmul(ps[:, 1, o + P:o + T], VN[:, (2 + hh) * P:(3 + hh) * P], IN[:, pair[2 * hh + 1][2]],
                                    start=False, stop=True)
                ins.then_inc(sem("d_o"), 1)

            pe.wait_ge(sem("loaded"), 64)
            for l in range(DEPTH):
                norm(l)
                pe.wait_ge(sem("norm_h"), l + 1)
                hx = rows_of(H, T)
                for i in range(16):
                    chunk("ag", l, i, KD, hx, T)
                for i in range(16):
                    chunk("qk", l, i, KD, hx, T)
                pe.wait_ge(sem("conv_done"), KD * (l + 1))
                for m in range(KD):
                    ins = pe.matmul(ps[:, 0, 0:T], ones, CV[:, m, :], start=m == 0, stop=m == KD - 1)
                ins.then_inc(sem("ln_mean"), 1)
                for half in range(2):
                    freed = at["free"]
                    w = [tile(4) for k in range(KD)]
                    for tt in range(NT):
                        tokens_first("v", l, 2 * half + tt, w, tt, 512, freed if tt == 0 else 0)
                pe.wait_ge(sem("ln_sq"), l + 1)
                for m in range(KD):
                    ins = pe.matmul(ps[:, 1, 0:T], ones, sq[:, m * T:(m + 1) * T], start=m == 0, stop=m == KD - 1)
                ins.then_inc(sem("ln_ss"), 1)
                pe.wait_ge(sem("drained"), CHUNK["qk", l] + 16)
                if l == 0:
                    pe.wait_ge(sem("rope_table"), 1)
                for jj in range(8):
                    rot(8 * l + jj, C("rot1"), QK[:, 2 * jj:2 * jj + 2, :])
                for i in range(24):
                    chunk("dn", l, i, KD, hx, T)
                pe.wait_ge(sem("rope"), 8 * (l + 1))
                pe.wait_ge(sem("ln_rms"), l + 1)
                fill = [("cz", m) for m in range(KD)] + [("c_out", i) for i in range(2 * KD)]
                for it in range(18):
                    if it < 16:
                        attention_scores(l, it)
                    if 1 <= it <= 16:
                        attention_turn(l, it - 1)
                    if it >= 2:
                        attention_out(l, it - 2)
                    for name, i in fill[24 * it // 18:24 * (it + 1) // 18]:
                        if (name, i) == ("c_out", 1):
                            pe.wait_ge(sem("take_used"), TAKE["cz", l] + KD)
                        chunk(name, l, i, KD, rows_of(CV, T) if name == "c_out" and i % 2 else hx, T)
                for k in range(3):
                    head_norm(HN_BASE1(l) + k, 2048)
                for m in range(KD):
                    chunk("az", l, m, KD, hx, T)
                for i in range(2 * KD):
                    if i == 1:
                        pe.wait_ge(sem("take_used"), TAKE["az", l] + KD)
                    chunk("a_out", l, i, KD, rows_of(QK, T) if i % 2 else hx, T)
                delta_gates(l)
                for u in range(4):
                    delta(l, u)
                head_norm(HN_BASE1(l) + 3, 2048)
                for m in range(KD):
                    chunk("dz", l, m, KD, hx, T)
                for i in range(2 * KD):
                    if i == 1:
                        pe.wait_ge(sem("take_used"), TAKE["dz", l] + KD)
                    chunk("d_out", l, i, KD, rows_of(DN, T) if i % 2 else hx, T)
                pe.wait_ge(sem("take_used"), TAKE["d_out", l] + 2 * KD)
                for m in range(KD):
                    chunk("w_out", l, m, KD, rows_of(MG, T), T)
            norm(2)

            def attention2_scores(i, step):
                h, s, b = step
                keys = slice(0, 2 * T) if s == 0 else slice(T, 2 * T)
                if i >= 2:
                    pe.wait_ge(sem("a2_exp"), i - 1)
                pe.matmul(ps[:, i % 2, 0:keys.stop - keys.start], Q2_[:, h, s * T + b * P:s * T + (b + 1) * P],
                          K2_[:, h // 4, keys], start=True, stop=True).then_inc(sem("a2_scores"), 1)

            def attention2_turn(i, step):
                pe.wait_ge(sem("a2_weights"), i + 1)
                if i >= 1:
                    pe.wait_ge(sem("a2_turned"), i)
                for kb in range(4 if step[1] == 0 else 2):
                    ins = pe.transpose(ps[:, 2, kb * P:(kb + 1) * P], AT_A[:, i % 2, kb * P:(kb + 1) * P], ident)
                ins.then_inc(sem("a2_turn"), 1)

            def attention2_out(i, step):
                h, s, b = step
                blocks = [0, 1, 2, 3] if s == 0 else [2, 3]
                g = h // 4
                pe.wait_ge(sem("a2_turned"), i + 1)
                if i >= 1:
                    pe.wait_ge(sem("a2_out"), i)
                for n, kb in enumerate(blocks):
                    ins = pe.matmul(ps[:, 3, 0:P], V2_[:, kb, g * P:(g + 1) * P], AT_T[:, i % 2, n * P:(n + 1) * P],
                                    start=n == 0, stop=n == len(blocks) - 1)
                ins.then_inc(sem("a2_o"), 1)

            for l in range(DEPTH):
                n, ns = N_TOK[l], N_SEQ[l]
                if l == 0:
                    pe.wait_ge(sem("norm_rms"), 3)
                    pe.wait_ge(sem("silu_c"), 1)
                for m in range(N_MOD * KD):
                    for k in range(KD):
                        freed = at["free"] if (m, k) != (N_MOD * KD - 1, KD - 1) else 0
                        ins = pe.matmul(ps[:, 0, 2 * m:2 * m + 2], tile(), sc[:, k, :], start=k == 0, stop=k == KD - 1)
                        if freed:
                            ins.then_inc(sem("slot_free"), freed)
                            at["free"] -= freed
                ins.then_inc(sem("mod_ready"), 1)
                for k in range(3):
                    if k == 0:
                        lhsT, rhs = PR("filt_w1", l * 64, 64)[0:33], C("zT")[0:33]
                        pe.wait_ge(sem("norm_rms"), 3 + 2 * l)
                    else:
                        lhsT, rhs = PR(f"filt_w{k + 1}", l * 64, 64)[0:64], HQ[0:64, :]
                        pe.wait_ge(sem("f_sin"), 3 * l + k)
                    pe.matmul(ps[0:64, 1, 0:T], lhsT, rhs, start=True, stop=True).then_inc(sem("f_ready"), 1)
                pe.wait_ge(sem("f_sin"), 3 * l + 3)
                pe.wait_ge(sem("w4_loaded"), 16 * (l + 1))
                pe.wait_ge(sem("mod_done"), l + 1)
                for half in range(2):
                    for tt in range(NT):
                        ins = pe.matmul(ps[:, 2 * half + tt, :], HQ[0:64, tt * P:(tt + 1) * P],
                                        W4[0:64, half * HY:(half + 1) * HY], start=True, stop=True)
                ins.then_inc(sem("h4_ready"), 1)
                pe.wait_ge(sem("h4_done"), l + 1)
                for ft in range(4):
                    for q in range(4):
                        table = "dft_fwd" if q < 2 else "dft_bwd"
                        ins = pe.matmul(ps[:, ft, :], C(table, (q % 2) * N_FFT + ft * P, P), VTK[:, q, :], start=q == 0, stop=q == 3)
                ins.then_inc(sem("kf_ready"), 1)
                pe.wait_ge(sem("kf_done"), l + 1)
                norm(mix_norm[l])
                pe.wait_ge(sem("norm_h"), mix_norm[l] + 1)
                hx = rows_of(H, n)
                for i in range(8):
                    chunk("q2", l, i, KD, hx, n)
                for i in range(2):
                    chunk("k2", l, i, KD, rows_of(H, 2 * T), 2 * T)
                w = [tile(2) for k in range(KD)]
                for tt in range(4):
                    tokens_first("v2", l, tt, w, tt, 2 * P)
                i = HN_BASE2[l]
                if l == 0:
                    head_norm(i, 2048)
                    head_norm(i + 1, 2048)
                    head_norm(i + 2, 1024)
                else:
                    head_norm(i, 2048)
                    head_norm(i + 1, 1024)
                for i in range(12):
                    chunk("hy2", l, i, KD, hx, n)
                pe.wait_ge(sem("hconv"), 12 * (l + 1))
                pe.wait_ge(sem("hn_rms"), HN_BASE2[l] + (3 if l == 0 else 2))
                for s in range(ns):
                    for tt in range(NT):
                        for m in range(KH):
                            ins = pe.transpose(ps[:, 2 * s + tt, m * P:(m + 1) * P],
                                               VX[:, m, s * T + tt * P:s * T + (tt + 1) * P], ident)
                ins.then_inc(sem("vt_ready"), 1)
                pe.wait_ge(sem("vt_done"), l + 1)
                for s in range(ns):
                    k = 2 * l + s
                    if s:
                        pe.wait_ge(sem("hyena"), k)
                    for ft in range(4):
                        for tt in range(NT):
                            ins = pe.matmul(ps[:, ft, :], C("dft_fwd", tt * N_FFT + ft * P, P), VTK[:, 2 * s + tt, :],
                                            start=tt == 0, stop=tt == NT - 1)
                    ins.then_inc(sem("vf_ready"), 1)
                    pe.wait_ge(sem("y_done"), k + 1)
                    for m in range(KH):
                        for ft in range(4):
                            ins = pe.matmul(ps[:, m // 2, (m % 2) * T:(m % 2 + 1) * T], YFT[:, ft, m * P:(m + 1) * P],
                                            C("idft", ft * T, T), start=ft == 0, stop=ft == 3)
                    ins.then_inc(sem("yi_ready"), 1)
                pe.wait_ge(sem("hn_done"), HN_BASE2[l] + (3 if l == 0 else 2))
                for jj in range(5):
                    rot(ROPE2[l] + jj, C("rot2"), Q2_[:, 2 * jj:2 * jj + 2, 0:T] if jj < 4 else K2_[:, :, 0:T])
                pe.wait_ge(sem("rope"), ROPE2[l] + 5)
                pe.wait_ge(sem("hyena"), 2 * l + ns)
                steps = IT2[l]
                for k in range(len(steps) + 2):
                    i = IT2_BASE[l] + k
                    if k < len(steps):
                        attention2_scores(i, steps[k])
                    if 1 <= k <= len(steps):
                        attention2_turn(i - 1, steps[k - 1])
                    if k >= 2:
                        attention2_out(i - 2, steps[k - 2])
                pe.wait_ge(sem("a2_out"), IT2_BASE[l] + len(steps))
                for m in range(KD):
                    chunk("o2", l, 4 * m, KD, hx, n)
                    chunk("o2", l, 4 * m + 1, KD, rows_of(Q2_, n), n)
                    chunk("o2", l, 4 * m + 2, KD, hx, n)
                    chunk("o2", l, 4 * m + 3, KH, rows_of(X0, n), n)
                pe.wait_ge(sem("take_used"), TAKE["o2", l] + 32)
                for m in range(KD):
                    chunk("w_out2", l, m, KD, rows_of(MG2, n), n)
                norm(ffn_norm[l])
                pe.wait_ge(sem("norm_h"), ffn_norm[l] + 1)
                for i in range(2 * KF):
                    chunk("gu", l, i, KD, hx, n)
                pe.wait_ge(sem("take_used"), TAKE["gu", l] + KF)
                for m in range(KD):
                    chunk("down", l, m, KF, rows_of(AF, n), n)
            norm(7)




def lay_out(inp):
    a = {k: np.asarray(v) for k, v in inp.items()}

    def tiles(w):
        k, m = w.shape
        return w.reshape(k // P, P, m // P, P).transpose(2, 0, 1, 3)

    def woven(*ws):
        return [t for group in zip(*ws) for w in group for t in w]

    stream = []
    for l in range(DEPTH):
        w = a["w_in"][l]
        cols = lambda at, n=D: w[:, at:at + n]
        flat = lambda m: list(tiles(m).reshape(-1, P, P))
        stream += woven(tiles(cols(GLU)), tiles(cols(GLU + D)))
        stream += flat(cols(AQ, 2 * D))
        for half in range(2):
            stream += list(tiles(cols(AV + half * 512, 512)).transpose(1, 0, 2, 3).reshape(-1, P, P))
        stream += flat(cols(DQ, 3 * D))
        stream += flat(cols(CZ))
        stream += woven(tiles(cols(GATE + D)), tiles(a["w_conv_out"][l]))
        stream += flat(cols(AZ))
        stream += woven(tiles(cols(GATE)), tiles(a["w_attn_out"][l]))
        stream += flat(cols(DZ))
        stream += woven(tiles(cols(GATE + 2 * D)), tiles(a["w_dn_out"][l]))
        stream += flat(a["w_out"][l])
        assert len(stream) == TILES_1 * (l + 1)
    for l in range(DEPTH):
        w = a["w_in_2"][l]
        cols = lambda at, n: w[:, at:at + n]
        flat = lambda m: list(tiles(m).reshape(-1, P, P))
        stream += flat(a["w_mod_2"][l])
        stream += flat(cols(Q2, D + 2 * P))
        stream += list(tiles(cols(V2, 2 * P)).transpose(1, 0, 2, 3).reshape(-1, P, P))
        stream += flat(cols(HY2, 3 * HY))
        stream += woven(tiles(cols(G2, D)), tiles(a["w_o_attn_2"][l]), tiles(cols(G2 + D, D)), tiles(a["w_o_hyena_2"][l]))
        stream += flat(a["w_out_2"][l])
        g = a["w_gate_up_2"][l]
        stream += woven(tiles(g[:, :D_FF]), tiles(g[:, D_FF:]))
        stream += flat(a["w_down_2"][l])
    assert len(stream) == N_TILES
    nothing = np.zeros((P, P), np.float32)
    stream += [nothing] * (N_LOADS * TILES - len(stream))
    w_stream = np.empty((N_LOADS, P, TILES, P), np.float32)
    for i, t in enumerate(stream):
        w_stream[i // TILES, :, i % TILES, :] = t

    prm = np.zeros((P, N_PARAM), np.float32)

    def put(name, at, cols):
        cols = np.asarray(cols)
        s = PARAM_AT[name] + at
        prm[:cols.shape[0], s:s + cols.shape[1]] = cols

    by_p = lambda v: v.reshape(-1, P).T
    rows = lambda v: np.broadcast_to(v.reshape(1, -1), (P, v.size))
    for l in range(DEPTH):
        put("norm_w", l * KD, by_p(a["norm_w"][l]))
        put("attn_subln_w", l, by_p(a["attn_subln_w"][l]))
        put("conv_dw_w", l * KD * CONV_K, a["conv_dw_w"][l].reshape(CONV_K, KD, P).transpose(2, 1, 0).reshape(P, -1))
        put("conv_dw_b", l * KD, by_p(a["conv_dw_b"][l]))
        put("conv_ln_w", l * KD, by_p(a["conv_ln_w"][l]))
        put("conv_ln_b", l * KD, by_p(a["conv_ln_b"][l]))
        put("dn_conv_w", l * 24 * SHORT_K, a["dn_conv_w"][l].reshape(SHORT_K, 24, P).transpose(2, 1, 0).reshape(P, -1))
        put("dn_a_log", l * HEADS, rows(a["dn_a_log"][l]))
        put("dn_dt_bias", l * HEADS, rows(a["dn_dt_bias"][l]))
        put("dn_norm_w", l, by_p(a["dn_norm_w"][l]))
        put("lam_qk", l * 4 * QK_DIM, rows(a["lam_qk"][l]))
        put("w_ba", l * KD * 16, a["w_in"][l][:, DB:DB + 16].reshape(KD, P, 16).transpose(1, 0, 2).reshape(P, -1))
        put("b_mod", l * N_MOD * KD, by_p(a["b_mod_2"][l]))
        put("norm_mix", l * KD, by_p(a["norm_mix_2"][l]))
        put("q_norm", l, by_p(a["q_norm_2"][l]))
        put("k_norm", l, by_p(a["k_norm_2"][l]))
        put("conv_w", l * 12 * HY_TAPS, a["conv_w_2"][l].reshape(HY_TAPS, 12, P).transpose(2, 1, 0).reshape(P, -1))
        put("conv_b", l * 12, by_p(a["conv_b_2"][l]))
        for k in (1, 2, 3):
            put(f"filt_w{k}", l * 64, a[f"filt_w{k}_2"][l])
            put("filt_b", 3 * l + k - 1, a[f"filt_b{k}_2"][l][:, None])
            put("filt_freq", 3 * l + k - 1, a["filt_freq_2"][l][k - 1][:, None])
        put("hyena_bias", l * KH, by_p(a["hyena_bias_2"][l]))
        put("norm_ffn", l * KD, by_p(a["norm_ffn_2"][l]))
    put("final_norm_w", 0, by_p(a["final_norm_w"]))
    put("norm_final", 0, by_p(a["norm_final_2"]))
    conds = np.stack([a["c_2"].reshape(-1), a["c_ctx_2"].reshape(-1)], 1)
    put("c", 0, conds.reshape(KD, P, 2).transpose(1, 0, 2).reshape(P, -1))

    made = constants()
    cst = np.zeros((P, N_CONST), np.float32)
    for name, n in CONST_W.items():
        assert made[name].shape == (P, n), (name, made[name].shape)
        cst[:, CONST_AT[name]:CONST_AT[name] + n] = made[name].astype(np.float32)

    turned = lambda x: np.ascontiguousarray(x.reshape(T, KD, P).transpose(2, 1, 0))
    return {
        "w_stream": w_stream.reshape(N_LOADS, P, TILES * P),
        "params": prm,
        "fw4": np.ascontiguousarray(a["filt_w4_2"]),
        "pos": np.ascontiguousarray(np.broadcast_to(a["positions"].reshape(1, T), (P, T))),
        "xT": turned(a["x"]),
        "ctxT": turned(a["ctx_2"]),
        "consts": cst,
    }




def kernel(**inputs):
    import concourse.bacc as _bacc
    from concourse.bass_utils import run_bass_kernel_spmd as _run

    arrays = lay_out(inputs)
    nc = _bacc.Bacc("TRN2", target_bir_lowering=False, num_devices=1, dynamic_dma_scratch_size=1024)
    args = [nc.dram_tensor(f"in_{n}_dram", v.shape, mybir.dt.from_np(v.dtype), kind="ExternalInput").ap()
            for n, v in arrays.items()]
    args.append(nc.dram_tensor("out_0_dram", (P, KD, T), mybir.dt.float32, kind="ExternalOutput").ap())
    build(nc, *args)
    r = _run(nc, [{f"in_{n}_dram": v for n, v in arrays.items()}], core_ids=[0])
    got = r.results[0]["out_0_dram"]
    return np.ascontiguousarray(np.asarray(got).transpose(2, 1, 0)).reshape(1, T, D)
```

```python
import math
import numpy as np
import concourse.bass as bass
from concourse import mybir
from contextlib import ExitStack

P = 128
D = 1024
KD = D // P
T = 256
NT = T // P
DEPTH = 2
HEADS = 8
QK_DIM = 64
CONV_K = 31
SHORT_K = 4
HY = 512
KH = HY // P
HY_TAPS = 3
D_FF = 2816
KF = D_FF // P
N_MOD = 6
N_FFT = 2 * T
NEG = -1.0e30
TWO_PI = 2.0 * math.pi
TILES = 16
RING = 4
HIGHS = 32
PIECE = 8
LEAD = 16

AQ, AK, AV, AZ, GLU, CZ, DQ, DK, DV, DZ, DB, GATE = (
    0, 1024, 2048, 3072, 4096, 6144, 7168, 8192, 9216, 10240, 11264, 11280)
Q2, K2, V2, HY2, G2 = 0, 1024, 1280, 1536, 3072



def constants():
    f = np.float64
    i = np.arange(P)
    c = {}
    c["ident"] = np.eye(P)
    c["ones"] = np.ones((P, P))
    c["until"] = (i[:, None] <= i[None, :]) * 1.0
    c["later"] = np.where(i[:, None] <= i[None, :], 0.0, NEG)
    causal = np.where(i[:, None] >= i[None, :], 0.0, NEG)
    c["causal1"] = np.concatenate([np.zeros((P, P)), causal], 1)
    lv = []
    for s in (1, 2, 4, 8, 16, 32, 64):
        lv.append(((i[:, None] // (2 * s) == i[None, :] // (2 * s))
                   & (i[:, None] % (2 * s) < s) & (i[None, :] % (2 * s) >= s)) * 1.0)
    c["levels"] = np.concatenate(lv, 1)
    rot1 = np.zeros((P, P))
    for d in range(P):
        if d % QK_DIM < QK_DIM // 2:
            rot1[d + QK_DIM // 2, d] = -1.0
        else:
            rot1[d - QK_DIM // 2, d] = 1.0
    c["rot1"] = rot1
    c["tab1"] = np.zeros((P, 2 * T))
    rot2 = np.zeros((P, P))
    for d in range(0, P, 2):
        rot2[d + 1, d] = -1.0
        rot2[d, d + 1] = 1.0
    c["rot2"] = rot2
    t = np.arange(T)
    half = P // 2
    inv2 = (10000.0 ** (-np.arange(0, half, 2, dtype=f) / half)).astype(np.float32)
    ang = np.concatenate([(t // 64)[:, None].astype(np.float32) * inv2,
                          (t % 64)[:, None].astype(np.float32) * inv2], 1).astype(f)
    c["cos2"] = np.repeat(np.cos(ang).T, 2, 0)
    c["sin2"] = np.repeat(np.sin(ang).T, 2, 0)
    inv1 = 10000.0 ** (-np.arange(0, QK_DIM, 2, dtype=f) / QK_DIM)
    c["inv1"] = np.tile(inv1, 4)[:, None]
    tt = np.linspace(0.0, 1.0, T)[:, None]
    w = (TWO_PI / T) * np.arange(T)[:, None]
    fr = np.linspace(1e-4, 15, 16)[None, :]
    z = np.concatenate([tt, np.cos(fr * w), -np.sin(fr * w)], 1)
    c["zT"] = np.concatenate([z.T, np.zeros((P - 33, T))], 0)
    deltas = np.abs(np.linspace(math.log(1e-2) / 1.5, math.log(1e-2) / 0.3, HY))
    dec = np.exp(-tt * deltas)
    rows = lambda a: a.reshape(-1, P, a.shape[1]).transpose(1, 0, 2).reshape(P, -1)
    c["decay"] = rows(dec)
    ph = TWO_PI * np.outer(t, np.arange(T)) / N_FFT
    re, im = np.cos(ph), -np.sin(ph)
    im_n = im.copy()
    im_n[:, 0] = np.cos(math.pi * t)
    c["dft_fwd"] = rows(np.concatenate([re, im_n], 1))
    bre, bim = re.copy(), -im
    bim[:, 0] = np.cos(math.pi * t)
    bre[0], bim[0] = 0.0, 0.0
    c["dft_bwd"] = rows(np.concatenate([bre, bim], 1))
    ire, iim = 2.0 * np.cos(ph.T) / N_FFT, -2.0 * np.sin(ph.T) / N_FFT
    ire[0] *= 0.5
    iim[0] = np.cos(math.pi * t) / N_FFT
    c["idft"] = rows(np.concatenate([ire, iim], 0))
    for name, v in (("eps6", 1e-6), ("eps5", 1e-5), ("half_pi", math.pi / 2)):
        c[name] = np.full((P, 1), v)
    for name, v in (("lam_init", [0.8 - 0.6 * math.exp(-0.3 * l) for l in range(DEPTH)]),):
        c[name] = np.tile(np.array(v)[None], (P, 1))
    return c


CONST_W = {"until": P, "later": P, "causal1": T, "levels": 7 * P, "rot1": P, "tab1": 2 * T,
           "ident": P, "ones": P, "eps6": 1, "eps5": 1, "half_pi": 1, "lam_init": DEPTH, "inv1": 1,
           "rot2": P, "cos2": T, "sin2": T, "zT": T, "dft_fwd": NT * N_FFT, "idft": 4 * T,
           "decay": NT * HY, "dft_bwd": NT * N_FFT}
EARLY = ("ident", "rot2")

PARAM_W = {"norm_w": DEPTH * KD, "attn_subln_w": DEPTH, "conv_dw_w": DEPTH * KD * CONV_K,
           "conv_dw_b": DEPTH * KD, "conv_ln_w": DEPTH * KD, "conv_ln_b": DEPTH * KD,
           "dn_conv_w": DEPTH * 24 * SHORT_K, "dn_a_log": DEPTH * HEADS, "dn_dt_bias": DEPTH * HEADS,
           "dn_norm_w": DEPTH, "final_norm_w": KD, "lam_qk": DEPTH * 4 * QK_DIM, "w_ba": DEPTH * KD * 16,
           "c": KD * 2, "b_mod": DEPTH * N_MOD * KD, "norm_mix": DEPTH * KD, "q_norm": DEPTH, "k_norm": DEPTH,
           "conv_w": DEPTH * 12 * HY_TAPS, "conv_b": DEPTH * 12, "filt_w1": DEPTH * 64, "filt_w2": DEPTH * 64,
           "filt_w3": DEPTH * 64, "filt_b": DEPTH * 3, "filt_freq": DEPTH * 3,
           "hyena_bias": DEPTH * KH, "norm_ffn": DEPTH * KD, "norm_final": KD}


def starts(widths):
    at, out = 0, {}
    for k, n in widths.items():
        out[k] = at
        at += n
    return out, at


CONST_AT, N_CONST = starts(CONST_W)
N_KEPT = CONST_AT["decay"]
PARAM_AT, N_PARAM = starts(PARAM_W)



def spread(items, points):
    return [items[len(items) * k // points:len(items) * (k + 1) // points] for k in range(points)]


LAG = 2
ATT_STEPS = 2 * HEADS
STEPS2 = [2 * 2 * HEADS, 2 * HEADS]
DELTA_POINTS = 18
UNITS = HEADS // 2
EARLY_CZ = 4
EARLY_HY = 4

MODS = N_MOD * D // 512
MOD_AT = [{"gates": (0, 1), "att": (1, 2), "delta": (2, 10), "n1a": (10, 11), "n1b": (11, 12)},
          {"gates": (0, 1), "att": (1, 2), "delta": (2, 8), "n2a": (8, 9), "n2b": (9, 10), "n3a": (10, 11), "n3b": (11, 12)}]


def mods(l, place):
    return [(name, l, m) for m in range(*MOD_AT[l].get(place, (0, 0))) for name in ("mod", "modt")]


def norm_mods(i, side):
    return mods(0, f"n{i}{side}") + mods(1, f"n{i}{side}")


def att_fill(l):
    return spread([("cz", l, m) for m in range(EARLY_CZ, KD)] + [("c_out", l, i) for i in range(2 * KD)], ATT_STEPS + LAG + 1)


def delta_fill(l):
    rows, turns = mods(l, "delta")[::2], mods(l, "delta")[1::2]
    outs = [("az", l, m) for m in range(KD)] + [("a_out", l, i) for i in range(2 * KD)]
    both = []
    for row, turn, out in zip(spread(rows, len(outs)), spread([None] + turns[:-1], len(outs)), outs):
        both += turn + row + [out]
    both = [x for x in both if x] + turns[-1:]
    halves = []
    for x in both:
        halves += [x] if x[0] == "modt" else [("half", x), x]
    return spread(halves, UNITS * DELTA_POINTS)


def whole(items):
    return [x for x in items if x[0] != "half"]


def att2_fill(l):
    return spread([("hy2", l, j) for j in range(EARLY_HY, 12)], STEPS2[l] + LAG + 1)


def hyena_fill(l):
    return spread([("oa", l, i) for i in range(2 * KD)], 5 if l == 0 else 3)


def chunk_order():
    out = []
    for l in range(DEPTH):
        add = lambda name, a, b: out.extend((name, l, i) for i in range(a, b))
        add("ag", 0, 16)
        add("qk", 0, 16)
        add("v", 0, 8)
        add("dn", 0, 24)
        add("cz", 0, EARLY_CZ // 2)
        out += mods(l, "gates")
        add("cz", EARLY_CZ // 2, EARLY_CZ)
        out += sum(att_fill(l), []) + mods(l, "att") + whole(sum(delta_fill(l), []))
        add("dz", 0, 8)
        add("d_out", 0, 16)
        add("w_out", 0, 8)
        out += norm_mods(l + 1, "a") + norm_mods(l + 1, "b")
    for l in range(DEPTH):
        add = lambda name, a, b: out.extend((name, l, i) for i in range(a, b))
        out += norm_mods(2 * l + 3, "a") + norm_mods(2 * l + 3, "b")
        add("q2", 0, 8)
        add("k2", 0, 2)
        add("v2", 0, 4)
        add("hy2", 0, EARLY_HY)
        out += sum(att2_fill(l), []) + sum(hyena_fill(l), [])
        add("oh", 0, 16)
        add("w_out2", 0, 8)
        out += norm_mods(2 * l + 4, "a") + norm_mods(2 * l + 4, "b")
        add("gu", 0, 2 * KF)
        add("down", 0, 8)
    return out


ORDER = chunk_order()
MOD_TURNS = [("modt", l, i) for l in range(DEPTH) for i in range(MODS)]
CHUNK = {x: j for j, x in enumerate(ORDER)}
TAKEN = [x for x in ORDER if x[0] in ("ag", "cz", "c_out", "az", "a_out", "dz", "d_out", "w_out", "oa", "oh", "w_out2", "down")
         or (x[0] == "gu" and x[2] % 2)]
TAKE = {x: q for q, x in enumerate(TAKEN)}


def n_tiles(name, i):
    if name == "v":
        return 2 * KD if i % 2 == 0 else 0
    if name == "v2":
        return 2 * KD if i == 0 else 0
    if name == "oh" and i % 2:
        return KH
    return {"down": KF, "mod": 4 * KD, "modt": 0}.get(name, KD)


def is_split(name, i):
    if name in ("c_out", "a_out", "d_out", "oa", "oh"):
        return i % 2 == 0
    return name not in ("mod", "modt", "w_out", "w_out2", "down")


def piece_table():
    ends, readers, pieces, stream = [], [], [], []
    t = s = 0
    for j, (name, l, i) in enumerate(ORDER):
        n = n_tiles(name, i)
        last = j + {"v": 1, "v2": 3}.get(name, 0)
        stream += [last] * n
        if is_split(name, i):
            a = 0
            while a < n:
                m = min(PIECE, n - a, TILES - (t + a) % TILES, HIGHS - (s + a) % HIGHS)
                end = s + a + m - HIGHS
                pieces.append((t + a, m, (s + a) % HIGHS, readers[end - 1] if end > 0 else None, s + a, j))
                a += m
            readers += [last] * n
            s += n
        t += n
        ends.append(s)
    out, j = [], 0
    for t, m, place, reader, at, own in pieces:
        before = (t // TILES - RING + 1) * TILES
        while at >= ends[j] + LEAD or (reader is not None and reader >= j) or (before > 0 and stream[before - 1] > j - 2):
            j += 1
        assert j <= own
        out.append((t, m, place, reader, j))
    return out


PIECES = piece_table()
PIECE_OF = {t: p for p, (t, m, place, reader, j) in enumerate(PIECES)}
N_TILES = sum(n_tiles(name, i) for name, l, i in ORDER)
N_LOADS = -(-N_TILES // (TILES * RING)) * RING


def build(nc, w_stream, params, fw4, pos, xT, ctxT, consts, out):
    F32 = mybir.dt.float32
    F32R = mybir.dt.float32r
    I32 = mybir.dt.int32
    ALU = mybir.AluOpType
    ACT = mybir.ActivationFunctionType
    AX = mybir.AxisListType
    MUL, ADD, SUB, MAX = ALU.mult, ALU.add, ALU.subtract, ALU.max
    ctx = ExitStack()
    with ctx:
        START = {}

        def sb(name, *shape, dt=F32):
            START[name] = -(-nc.sbuf_base // 32) * 32
            return ctx.enter_context(nc.sbuf_tensor(name, [P, *shape], dt))

        made = {}

        def sem(name):
            if name not in made:
                made[name] = ctx.enter_context(nc.semaphore(name))
            return made[name]

        def typed(name, other, *shape):
            return nc.alloc_sbuf_tensor_at(name, [P, *shape], F32R, offset=other)

        ring = sb("ring", RING, TILES * P)
        ring_lo = typed("ring_lo", START["ring"], RING, TILES * P)
        ring_hi = sb("ring_hi", HIGHS * P, dt=F32R)
        cst = sb("cst", N_KEPT)
        prm = sb("prm", N_PARAM)
        X = sb("X", KD, 2 * T)
        H = sb("H", KD, 2 * T)
        HL = typed("HL", START["H"], KD, 2 * T)
        HH = sb("HH", KD, 2 * T, dt=F32R)
        rstd = sb("rstd", 2 * T)
        take = sb("take", 4, 2 * T)
        hn = sb("hn", 2048)
        at_buf = sb("at_buf", 3072)
        sq = at_buf[:, 1024:3072]
        big = sb("big", 15616)
        ba = sb("ba", 9, 2 * HEADS)
        at_m = sb("at_m", 2, 2)
        at_l = sb("at_l", 2, 2)
        lam = sb("lam", 8)
        mod = sb("mod", DEPTH, N_MOD * KD, 2)
        mod_rows = sb("mod_rows", 2, 512)
        gains = sb("gains", 2, KD, 2)
        sc = sb("sc", KD, 2)

        def cut(buf, at, *shape):
            n = 1
            for s in shape:
                n *= s
            v = buf[:, at:at + n]
            if len(shape) == 2:
                v = v.rearrange("p (a b) -> p a b", a=shape[0])
            if len(shape) == 3:
                v = v.rearrange("p (a b c) -> p a b c", a=shape[0], b=shape[1])
            return v

        pg = ctx.enter_context(nc.psum_tensor("pg", [P, 4, 512], F32))
        ps = ctx.enter_context(nc.psum_tensor("ps", [P, 4, 512], F32))
        ps_flat = ps[:, :, :].rearrange("p a b -> p (a b)")

        def C(name, at=0, n=None):
            a = CONST_AT[name] + at
            return cst[:, a:a + (n or CONST_W[name])]

        DECAY, DFT_BWD = hn[:, 0:NT * HY], hn[:, NT * HY:NT * (HY + N_FFT)]

        def PR(name, at=0, n=1):
            a = PARAM_AT[name] + at
            return prm[:, a:a + n]

        ident, ones, eps6, eps5 = C("ident"), C("ones"), C("eps6"), C("eps5")

        tab = C("tab1").rearrange("p (a b) -> p a b", a=2)
        assert CONST_AT["ident"] >= 4 * HY

        def rep(ap, n):
            return ap.unsqueeze(1).broadcast_to([P, n, ap.shape[1]])

        def wide(ap, n):
            return ap.unsqueeze(2).broadcast_to([P, ap.shape[1], n])

        QK = cut(big, 0, 16, T)
        V = cut(big, 4096, NT, D)
        U = cut(big, 6144, KD, CONV_K - 1 + T)
        DN = cut(big, 8432, 24, T)
        raw = cut(big, 14576, 4, SHORT_K - 1 + T)
        CV = X[:, :, T:2 * T]
        MG = H[:, :, T:2 * T]
        AT_S = cut(at_buf, 0, 2, 2 * T)
        AT_A = cut(at_buf, 1024, 2, 2 * T)
        AT_T = cut(at_buf, 2048, 2, 2 * T)
        RT = cut(at_buf, 0, 2, 2 * T)
        PAIRS = 4 * P
        DT, LT, IN, LM0, LM1, TT, TM, XS = (cut(big, 2048 + j * PAIRS, PAIRS) for j in range(8))
        VB, UG, IB, VN = (cut(big, 6144 + j * PAIRS, PAIRS) for j in range(4))
        LM = [LM0, LM1]
        KBG, KDEC, NW, S1, QG, EXR = (cut(at_buf, j * 2 * P, 2, P) for j in range(6))
        BETA, G, GC, NGC, BEG, B0, B1, B2 = (ba[:, j, :].rearrange("p (c h) -> p c h", c=NT) for j in range(8))
        EXA = ba[:, 8, 0:HEADS]
        QK_S = QK_DIM ** -0.5
        DN_S = P ** -0.5

        Q2_ = cut(big, 0, HEADS, 2 * T)
        K2_ = cut(big, 4096, 2, 2 * T)
        V2_ = cut(big, 5120, 4, 2 * P)
        X0 = cut(big, 6144, KH, 2 * T)
        X1 = cut(big, 8192, KH, 2 * T)
        VX = cut(big, 10240, KH, 2 * T)
        hraw = cut(big, 12288, 4, T + 2)
        VTK = cut(big, 13320, 4, HY)
        AF = cut(big, 0, KF, 2 * T)
        MG2 = [cut(big, at, KH, 2 * T)[:, m, :] for at in (4096, 8192) for m in range(KH)]
        W4 = cut(at_buf, 0, 2 * HY)
        HQ = cut(at_buf, 1024, T)
        RR = cut(at_buf, 1280, 3, T)
        KFT = cut(cst, 0, 4, HY)
        PROD = cut(at_buf, 0, 2, HY)
        VFT = hn[:, :].rearrange("p (a b) -> p a b", a=4)
        YFT = sq.rearrange("p (a b) -> p a b", a=4)
        ANGI = cut(at_buf, 0, T).bitcast(I32)
        POSF = cut(at_buf, 256, T)

        N_TOK = [2 * T, T]
        N_SEQ = [2, 1]
        N_NORM = [T, T, T, 2 * T, 2 * T, 2 * T, T, T]
        SPLIT_NORMS = [0, 1, 3, 4, 5, 6]
        mix_norm = [3, 5]
        ffn_norm = [4, 6]
        HN_BASE1 = lambda l: 4 * l
        HN_BASE2 = [8, 11]
        ROPE2 = [16, 21]
        IT2 = [[(h, s, b) for h in range(HEADS) for s in range(n) for b in range(NT)] for n in N_SEQ]
        IT2_BASE = [0, len(IT2[0])]
        DQ_N, DK_N, ATT_N, DO_N = range(4)
        ROPES_AFTER = [[0, 1], [2, 3], [4], []]
        FILTER_1 = [1, 4, 7, 10, 13]
        FILTER_2 = [0, 1, 2, 3, 4]

        def x_done(i, m=KD - 1):
            name, l = {1: ("w_out", 0), 2: ("w_out", 1), 4: ("w_out2", 0), 5: ("down", 0), 6: ("w_out2", 1), 7: ("down", 1)}[i]
            return TAKE[name, l, m] + 1

        early = slice(CONST_AT[EARLY[0]], CONST_AT[EARLY[1]])

        block = ctx.enter_context(nc.Block())

        @block.sync
        def _(sp):
            sp.dma_start(X[:, :, 0:T], xT).then_inc(sem("x_loaded"), 16)
            for s in range(RING):
                sp.dma_start(ring[:, s, :], w_stream[s]).then_inc(sem(f"weights{s}"), 16)
            first, after = slice(0, CONST_AT["tab1"]), slice(early.stop, N_KEPT)
            sp.dma_start(cst[:, first], consts[:, first]).then_inc(sem("tables"), 16)
            sp.dma_start(cst[:, after], consts[:, after]).then_inc(sem("tables"), 16)
            with sp.Fori(1, N_LOADS // RING) as r:
                for s in range(RING):
                    sp.wait_ge(sem("slot_free"), (r - 1) * RING + (s + 1))
                    sp.dma_start(ring[:, s, :], w_stream[bass.ds(r * RING + s, 1), :, :].rearrange("o p n -> p (o n)"))\
                        .then_inc(sem(f"weights{s}"), 16)
            for s in range(RING):
                sp.wait_ge(sem(f"weights{s}"), 16 * (N_LOADS // RING))

        @block.gpsimd
        def _(pool):
            links = [0]

            def link(ins):
                links[0] += 1
                ins.then_inc(sem("pool_link"), 1)
                pool.wait_ge(sem("pool_link"), links[0])

            def taken(name, l, i):
                return TAKE[name, l, i] % 4

            split = [0]

            def ahead(j):
                while split[0] < len(PIECES) and PIECES[split[0]][4] <= j:
                    t, n, place, reader, step = PIECES[split[0]]
                    split[0] += 1
                    cols = slice(t % TILES * P, (t % TILES + n) * P)
                    slot = t // TILES % RING
                    pool.wait_ge(sem("high_ready"), split[0])
                    pool.tensor_tensor(ring_lo[:, slot, cols], ring[:, slot, cols],
                                       ring_hi[:, place * P:(place + n) * P].bitcast(F32), SUB).then_inc(sem("low_ready"), 1)

            def drained(name, l, i):
                ahead(CHUNK[name, l, i])
                pool.wait_ge(sem("drained"), CHUNK[name, l, i] + 1)

            def zero_conv_pad():
                pool.memset(U[:, :, 0:CONV_K - 1], 0.0).then_inc(sem("conv_pad"), 1)

            def conv_gate(l):
                for m in range(KD):
                    a, g = taken("ag", l, 2 * m), taken("ag", l, 2 * m + 1)
                    drained("ag", l, 2 * m + 1)
                    pool.tensor_tensor(U[:, m, CONV_K - 1:], take[:, a, 0:T], take[:, g, 0:T], MUL)\
                        .then_inc(sem("take_used"), 2)

            def times_z(name, l, m, branch):
                drained(name, l, m)
                pool.tensor_tensor(branch[:, m, :], branch[:, m, :], take[:, taken(name, l, m), 0:T], MUL)\
                    .then_inc(sem("take_used"), 1)

            def merge(name, l, m, first):
                g, y = taken(name, l, 2 * m), taken(name, l, 2 * m + 1)
                drained(name, l, 2 * m + 1)
                if first:
                    pool.tensor_tensor(MG[:, m, :], take[:, g, 0:T], take[:, y, 0:T], MUL).then_inc(sem("take_used"), 2)
                else:
                    link(pool.tensor_tensor(take[:, y, 0:T], take[:, g, 0:T], take[:, y, 0:T], MUL))
                    pool.tensor_tensor(MG[:, m, :], MG[:, m, :], take[:, y, 0:T], ADD).then_inc(sem("take_used"), 2)

            def add_to_x(name, l, n):
                for m in range(KD):
                    drained(name, l, m)
                    pool.tensor_tensor(X[:, m, 0:n], X[:, m, 0:n], take[:, taken(name, l, m), 0:n], ADD)\
                        .then_inc(sem("take_used"), 1)

            pool.memset(raw[:, :, 0:SHORT_K - 1], 0.0).then_inc(sem("raw_pad"), 1)
            for l in range(DEPTH):
                if l:
                    pool.wait_ge(sem("take_used"), x_done(l))
                zero_conv_pad()
                conv_gate(l)
                for m in range(KD):
                    times_z("cz", l, m, CV)
                for m in range(KD):
                    merge("c_out", l, m, True)
                ahead(CHUNK["az", l, 2])
                pool.wait_ge(sem("hn_done"), HN_BASE1(l) + ATT_N + 1)
                for m in range(KD):
                    times_z("az", l, m, QK)
                for m in range(KD):
                    merge("a_out", l, m, False)
                ahead(CHUNK["dz", l, 3])
                pool.wait_ge(sem("hn_done"), HN_BASE1(l) + DO_N + 1)
                for m in range(KD):
                    times_z("dz", l, m, DN)
                for m in range(KD):
                    merge("d_out", l, m, False)
                add_to_x("w_out", l, T)
            pool.wait_ge(sem("norm_h"), 3 * KD)
            pool.memset(hraw[:, :, 0:1], 0.0)
            pool.memset(hraw[:, :, T + 1:T + 2], 0.0).then_inc(sem("hraw_pad"), 1)
            for l in range(DEPTH):
                n = N_TOK[l]
                for m in range(KD):
                    g, y = taken("oa", l, 2 * m), taken("oa", l, 2 * m + 1)
                    drained("oa", l, 2 * m + 1)
                    pool.tensor_tensor(MG2[m][:, 0:n], take[:, g, 0:n], take[:, y, 0:n], MUL).then_inc(sem("take_used"), 2)
                for m in range(KD):
                    g, y = taken("oh", l, 2 * m), taken("oh", l, 2 * m + 1)
                    drained("oh", l, 2 * m + 1)
                    link(pool.tensor_tensor(take[:, y, 0:n], take[:, g, 0:n], take[:, y, 0:n], MUL))
                    pool.tensor_tensor(MG2[m][:, 0:n], MG2[m][:, 0:n], take[:, y, 0:n], ADD).then_inc(sem("take_used"), 2)
                add_to_x("w_out2", l, n)
                for i in range(KF):
                    drained("gu", l, 2 * i + 1)
                    pool.tensor_tensor(AF[:, i, 0:n], AF[:, i, 0:n], take[:, taken("gu", l, 2 * i + 1), 0:n], MUL)\
                        .then_inc(sem("take_used"), 1)
                add_to_x("down", l, n)

        @block.scalar
        def _(act):
            split = [0]

            def ahead(j):
                while split[0] < len(PIECES) and PIECES[split[0]][4] <= j:
                    t, n, place, reader, step = PIECES[split[0]]
                    split[0] += 1
                    cols = slice(t % TILES * P, (t % TILES + n) * P)
                    slot = t // TILES % RING
                    act.wait_ge(sem(f"weights{slot}"), 16 * (t // TILES // RING + 1))
                    if reader is not None:
                        act.wait_ge(sem("chunk_ready"), reader + 1)
                    act.activation(ring_hi[:, place * P:(place + n) * P], ring[:, slot, cols], ACT.Copy)\
                        .then_inc(sem("high_ready"), 1)

            def ready(j):
                ahead(j)
                act.wait_ge(sem("chunk_ready"), j + 1)
                return pg[:, j % 4, :]

            def drain(j, dst, func=ACT.Copy, n=T):
                act.activation(dst, ready(j)[:, 0:n], func).then_inc(sem("drained"), 1)

            def to_take(name, l, i, func=ACT.Copy, n=T):
                q = TAKE[name, l, i]
                ahead(CHUNK[name, l, i])
                if q >= 4:
                    act.wait_ge(sem("take_used"), q - 3)
                drain(CHUNK[name, l, i], take[:, q % 4, 0:n], func, n)

            def drain_fill(items):
                for name, l, i in items:
                    if name == "mod":
                        k = MODS * l + i
                        if k >= 2:
                            act.wait_ge(sem("drained"), CHUNK[MOD_TURNS[k - 2]] + 1)
                        act.activation(mod_rows[0:2, i % 2, :], ready(CHUNK[name, l, i])[0:2, :], ACT.Copy).then_inc(sem("drained"), 1)
                    elif name == "modt":
                        drain(CHUNK[name, l, i], mod[:, l, 4 * i:4 * i + 4, :].rearrange("p a b -> p (a b)"), n=8)
                    elif name in ("cz", "az", "dz"):
                        to_take(name, l, i, ACT.Silu)
                    elif name == "hy2":
                        hyena_in(l, i)
                    else:
                        to_take(name, l, i, ACT.Copy if i % 2 else ACT.Sigmoid, N_TOK[l] if name in ("oa", "oh") else T)

            def hyena_in(l, j):
                n, ns = N_TOK[l], N_SEQ[l]
                ahead(CHUNK["hy2", l, j])
                if 12 * l + j >= 2:
                    act.wait_ge(sem("hconv"), 12 * l + j - 1)
                s0 = (j % 2) * 2
                act.activation(hraw[:, s0:s0 + ns, 1:T + 1],
                               ready(CHUNK["hy2", l, j])[:, 0:n].rearrange("p (s t) -> p s t", s=ns), ACT.Copy)\
                    .then_inc(sem("drained"), 1)

            def norm_square(i, m):
                n = N_NORM[i]
                if i == 0 and m == 0:
                    act.wait_ge(sem("x_loaded"), 16)
                if i == 3:
                    act.wait_ge(sem("norm_h"), 2 * KD + m + 1)
                    act.wait_ge(sem("ctx_loaded"), 16)
                elif i:
                    act.wait_ge(sem("take_used"), x_done(i, m))
                act.activation(H[:, m, 0:n], X[:, m, 0:n], ACT.Square).then_inc(sem("norm_sq"), 1)

            def norm_root(i):
                n = N_NORM[i]
                drain_fill(norm_mods(i, "a"))
                act.wait_ge(sem("norm_ss"), i + 1)
                act.activation(rstd[:, 0:n], ps[:, 0, 0:n], ACT.Sqrt, bias=eps6, scale=1.0 / D)\
                    .then_inc(sem("norm_rms"), 1)
                drain_fill(norm_mods(i, "b"))

            def updates(i, put):
                for m in range(KD + 2):
                    if m < KD:
                        put(m)
                    if m >= 2:
                        norm_square(i, m - 2)
                norm_root(i)

            def modulate(i, l, which):
                n = N_NORM[i]
                act.wait_ge(sem("mod_done"), l + 1)
                for k in range(KD + 1):
                    if k < KD:
                        act.wait_ge(sem("normed"), KD * (i - 3) + k + 1)
                        for s in range(n // T):
                            ins = act.activation(H[:, k, s * T:(s + 1) * T], H[:, k, s * T:(s + 1) * T], ACT.Identity,
                                                 bias=mod[:, l, 3 * which * KD + k, s:s + 1], scale=gains[:, which, k, s:s + 1])
                        ins.then_inc(sem("h_whole"), 1)
                    if k:
                        high_part(i, k - 1)

            def high_part(i, k):
                act.wait_ge(sem("h_whole"), KD * SPLIT_NORMS.index(i) + k + 1)
                act.activation(HH[:, k, 0:N_NORM[i]], H[:, k, 0:N_NORM[i]], ACT.Copy).then_inc(sem("h_high"), 1)

            def hn_square(src):
                a, b = src.shape[1], src.shape[2]
                act.activation(sq[:, 0:a * b].rearrange("p (a b) -> p a b", a=a), src, ACT.Square)\
                    .then_inc(sem("hn_sq"), 1)

            def hn_root(i, cols, scale):
                act.wait_ge(sem("hn_ss"), i + 1)
                if i >= 1:
                    act.wait_ge(sem("hn_done"), i)
                act.activation(hn[:, 0:cols], ps_flat[:, 0:cols], ACT.Sqrt, bias=eps6, scale=scale)\
                    .then_inc(sem("hn_rms"), 1)

            def filter_sin(l, k):
                act.wait_ge(sem("f_arg"), 3 * l + k + 1)
                act.activation(HQ[0:64, :], RR[0:64, 0, :], ACT.Sin).then_inc(sem("f_sin"), 1)

            def filter_spectrum(l):
                act.wait_ge(sem("kf_ready"), l + 1)
                act.activation(KFT, ps[:, :, :], ACT.Copy).then_inc(sem("kf_done"), 1)

            def attention_exp(l, it):
                i = 2 * HEADS * l + it
                e = P * (it % 2 + 1)
                act.wait_ge(sem("att_max"), i + 1)
                for m in range(2):
                    ins = act.activation(AT_S[:, i % 2, m * T:m * T + e], AT_S[:, i % 2, m * T:m * T + e], ACT.Exp,
                                         bias=at_m[:, i % 2, m:m + 1], accum_out=at_l[:, i % 2, m:m + 1])
                ins.then_inc(sem("att_exp"), 1)

            def attention_turned(l, it):
                i = 2 * HEADS * l + it
                e = P * (it % 2 + 1)
                act.wait_ge(sem("att_turn"), i + 1)
                if i >= 2:
                    act.wait_ge(sem("att_o"), i - 1)
                act.activation(AT_T[:, i % 2, 0:e], ps[:, 2, 0:e], ACT.Copy).then_inc(sem("att_turned"), 1)

            def delta_gates(l):
                act.wait_ge(sem("ba_ready"), l + 1)
                both = ps[:, 0, 0:32].rearrange("p (c n) -> p c n", c=NT)
                act.activation(BETA, both[:, :, 0:HEADS], ACT.Sigmoid).then_inc(sem("beta"), 1)
                act.activation(EXA, PR("dn_a_log", l * HEADS, HEADS), ACT.Exp).then_inc(sem("exp_a"), 1)
                act.wait_ge(sem("abs_a"), l + 1)
                act.activation(B1, B1, ACT.Exp, scale=-1.0).then_inc(sem("exp_abs"), 1)
                act.wait_ge(sem("exp_abs"), l + 1)
                act.activation(B2, B1, ACT.Ln, bias=1.0).then_inc(sem("ln_abs"), 1)
                drain_fill([("cz", l, m) for m in range(EARLY_CZ // 2)])
                drain_fill(mods(l, "gates"))
                act.wait_ge(sem("gc_ready"), l + 1)
                act.activation(BEG, ps[:, 1, 0:16].rearrange("p (c h) -> p c h", c=NT), ACT.Exp)\
                    .then_inc(sem("exp_gc"), 1)
                drain_fill([("cz", l, m) for m in range(EARLY_CZ // 2, EARLY_CZ)])

            def delta(l, u):
                i = 4 * l + u
                gaps = iter(delta_fill(l)[u * DELTA_POINTS:(u + 1) * DELTA_POINTS])

                def fill():
                    drain_fill(whole(next(gaps)))

                sums = ps[:, 0, :].rearrange("p (h c n) -> p h c n", h=2, c=NT)
                fill()
                act.wait_ge(sem("d_dt"), i + 1)
                act.activation(EXR, sums[:, :, 1, :], ACT.Exp)
                for p in range(4):
                    h, c = 2 * u + p // 2, p % 2
                    ins = act.activation(DT[:, p * P:(p + 1) * P], DT[:, p * P:(p + 1) * P], ACT.Exp,
                                         bias=NGC[:, c, h:h + 1])
                ins.then_inc(sem("d_exp"), 1)
                fill()
                act.wait_ge(sem("d_t0"), i + 1)
                act.activation(TM, ps[:, 0, :], ACT.Copy).then_inc(sem("d_tm"), 1)
                for s in range(1, 7):
                    fill()
                    act.wait_ge(sem("d_x"), 6 * i + s)
                    act.activation(XS, ps[:, 1, :], ACT.Copy).then_inc(sem("d_xs"), 1)
                    fill()
                fill()
                act.wait_ge(sem("d_w"), i + 1)
                act.activation(NW, ps[:, 2, 0:2 * P].rearrange("p (a b) -> p a b", a=2), ACT.Copy, scale=-1.0)
                act.activation(VN[:, 0:2 * P], ps[:, 2, 2 * P:4 * P], ACT.Copy).then_inc(sem("d_vn0"), 1)
                fill()
                act.wait_ge(sem("d_s"), i + 1)
                act.activation(S1, ps[:, 3, 0:2 * P].rearrange("p (a b) -> p a b", a=2), ACT.Copy).then_inc(sem("d_s1"), 1)
                fill()
                act.wait_ge(sem("d_v1"), i + 1)
                act.activation(VN[:, 2 * P:4 * P], ps[:, 0, 0:2 * P], ACT.Copy).then_inc(sem("d_vn1"), 1)
                fill()
                act.wait_ge(sem("d_o"), i + 1)
                act.activation(DN[:, 2 * u:2 * u + 2, :], ps[:, 1, :].rearrange("p (a b) -> p a b", a=2), ACT.Copy).then_inc(sem("d_out"), 1)

            act.dma_start(cst[:, early], consts[:, early]).then_inc(sem("loaded"), 16)
            act.dma_start(prm[:, :], params).then_inc(sem("loaded"), 16)
            act.dma_start(ANGI, pos).then_inc(sem("loaded"), 16)
            for m in range(KD):
                norm_square(0, m)
            act.wait_ge(sem("loaded"), 48)
            norm_root(0)
            ahead(0)
            for k in range(KD):
                high_part(0, k)
            act.activation(sc[:, :, :], PR("c", 0, 2 * KD), ACT.Silu).then_inc(sem("silu_c"), 1)
            act.wait_ge(sem("ang"), 1)
            act.activation(tab[:, 1, :], POSF, ACT.Sin)
            act.wait_ge(sem("ang"), 2)
            act.activation(tab[:, 0, :], RR[:, 0, :], ACT.Sin).then_inc(sem("rope_table"), 1)
            act.wait_ge(sem("lam_dots"), 1)
            act.activation(lam[:, 0:4], lam[:, 0:4], ACT.Exp).then_inc(sem("lam_exp"), 1)
            for l in range(DEPTH):
                for m in range(KD):
                    to_take("ag", l, 2 * m)
                    to_take("ag", l, 2 * m + 1, ACT.Sigmoid)
                for j in range(16):
                    drain(CHUNK["qk", l, j], QK[:, j, :])
                for j in range(8):
                    drain(CHUNK["v", l, j], V[:, j % 2, (j // 2) * T:(j // 2 + 1) * T])
                act.wait_ge(sem("ln_centered"), l + 1)
                act.activation(sq.rearrange("p (a b) -> p a b", a=KD), CV, ACT.Square).then_inc(sem("ln_sq"), 1)

                def dn_silu(j):
                    act.wait_ge(sem("sconv"), 24 * l + j + 1)
                    act.activation(DN[:, j, :], DN[:, j, :], ACT.Silu).then_inc(sem("dn_silu"), 1)

                for j in range(24):
                    if 24 * l + j >= 4:
                        act.wait_ge(sem("sconv"), 24 * l + j - 3)
                    if l == 0 and j == 0:
                        act.wait_ge(sem("raw_pad"), 1)
                    drain(CHUNK["dn", l, j], raw[:, j % 4, SHORT_K - 1:])
                    if j >= 2:
                        dn_silu(j - 2)
                    if j == 1:
                        act.wait_ge(sem("ln_ss"), l + 1)
                        act.activation(rstd[:, 0:T], ps[:, 1, 0:T], ACT.Sqrt, bias=eps5, scale=1.0 / D).then_inc(sem("ln_rms"), 1)
                    if j == 7:
                        act.wait_ge(sem("ln_normed"), l + 1)
                        for m in range(KD):
                            act.activation(CV[:, m, :], CV[:, m, :], ACT.Silu, bias=PR("conv_ln_b", l * KD + m),
                                           scale=PR("conv_ln_w", l * KD + m)).then_inc(sem("ln_silu"), 1)
                    if j == 9:
                        act.wait_ge(sem("dn_silu"), 24 * l + 8)
                        hn_square(DN[:, 0:8, :])
                    if j == 11:
                        hn_root(HN_BASE1(l) + DQ_N, 2048, 1.0)
                    if j == 17:
                        act.wait_ge(sem("dn_silu"), 24 * l + 16)
                        hn_square(DN[:, 8:16, :])
                    if j == 20:
                        hn_root(HN_BASE1(l) + DK_N, 2048, 1.0)
                dn_silu(22)
                dn_silu(23)
                act.wait_ge(sem("ln_silu"), KD * (l + 1))
                delta_gates(l)
                for it, items in enumerate(att_fill(l)):
                    if it < ATT_STEPS:
                        attention_exp(l, it)
                    drain_fill(items)
                    if LAG <= it < ATT_STEPS + LAG:
                        attention_turned(l, it - LAG)
                act.wait_ge(sem("att_out"), 16 * (l + 1))
                hn_square(QK[:, 0:8, :])
                drain_fill(mods(l, "att"))
                hn_root(HN_BASE1(l) + ATT_N, 2048, 1.0 / P)
                for u in range(UNITS):
                    delta(l, u)
                act.wait_ge(sem("d_out"), 4 * (l + 1))
                if l == DEPTH - 1:
                    act.dma_start(X[:, :, T:2 * T], ctxT).then_inc(sem("ctx_loaded"), 16)
                    act.dma_start(W4[0:64, :], fw4[0]).then_inc(sem("w4_loaded"), 16)
                hn_square(DN[:, 0:8, :])
                drain_fill([("dz", l, m) for m in range(2)])
                hn_root(HN_BASE1(l) + DO_N, 2048, 1.0 / P)
                drain_fill([("dz", l, m) for m in range(2, KD)])
                if l == DEPTH - 1:
                    act.wait_ge(sem("hn_done"), HN_BASE1(l) + DO_N + 1)
                    act.dma_start(hn[:, :], consts[:, N_KEPT:]).then_inc(sem("filter_tables"), 16)
                for i in range(2 * KD):
                    drain_fill([("d_out", l, i)])
                    if l == DEPTH - 1 and i in FILTER_1[1:4]:
                        filter_sin(0, FILTER_1.index(i) - 1)
                    if l == DEPTH - 1 and i == 14:
                        filter_spectrum(0)
                updates(l + 1, lambda m: to_take("w_out", l, m))
                if l == 0:
                    for k in range(KD):
                        high_part(1, k)
            for m in range(KD):
                norm_square(3, m)
            norm_root(3)

            def attention2_exp(i, s):
                n = 2 * T if s == 0 else T
                act.wait_ge(sem("a2_max"), i + 1)
                act.activation(AT_S[:, i % 2, 0:n], ps[:, i % 2, 0:n], ACT.Exp, bias=at_m[:, i % 2, 0:1],
                               scale=P ** -0.5, accum_out=at_l[:, i % 2, 0:1]).then_inc(sem("a2_exp"), 1)

            def attention2_turned(i, s):
                n = 2 * T if s == 0 else T
                act.wait_ge(sem("a2_turn"), i + 1)
                if i >= 2:
                    act.wait_ge(sem("a2_o"), i - 1)
                act.activation(AT_T[:, i % 2, 0:n], ps[:, 2, 0:n], ACT.Copy).then_inc(sem("a2_turned"), 1)

            def gated(name, l, m, which):
                q = TAKE[name, l, m]
                ahead(CHUNK[name, l, m])
                act.wait_ge(sem("take_used"), q - 3)
                src = ready(CHUNK[name, l, m])
                for s in range(N_SEQ[l]):
                    ins = act.activation(take[:, q % 4, s * T:(s + 1) * T], src[:, s * T:(s + 1) * T], ACT.Copy,
                                         scale=mod[:, l, which * KD + m, s:s + 1])
                ins.then_inc(sem("drained"), 1)

            for l in range(DEPTH):
                n, ns = N_TOK[l], N_SEQ[l]
                modulate(mix_norm[l], l, 0)
                i = HN_BASE2[l]
                for j in range(8):
                    drain(CHUNK["q2", l, j], Q2_[:, j, 0:n], n=n)
                    if l == 0 and j == 3:
                        act.wait_ge(sem("drained"), CHUNK["q2", l, j] + 1)
                        hn_square(Q2_[:, 0:4, :])
                    if l == 0 and j == 6:
                        hn_root(i, 2048, 1.0 / P)
                        i += 1
                act.wait_ge(sem("drained"), CHUNK["q2", l, 7] + 1)
                hn_square(Q2_[:, 4:8, :] if l == 0 else Q2_[:, :, 0:T])
                for j in range(2):
                    drain(CHUNK["k2", l, j], K2_[:, j, :], n=2 * T)
                hn_root(i, 2048, 1.0 / P)
                act.wait_ge(sem("drained"), CHUNK["k2", l, 1] + 1)
                hn_square(K2_)
                for j in range(4):
                    drain(CHUNK["v2", l, j], V2_[:, j, :], n=2 * P)
                    if j == 1:
                        hn_root(i + 1, 1024, 1.0 / P)
                if l == 0:
                    act.wait_ge(sem("hraw_pad"), 1)
                drain_fill([("hy2", l, j) for j in range(EARLY_HY)])
                steps = IT2[l]
                for k, items in enumerate(att2_fill(l)):
                    if k < len(steps):
                        attention2_exp(IT2_BASE[l] + k, steps[k][1])
                    drain_fill(items)
                    if LAG <= k < len(steps) + LAG:
                        attention2_turned(IT2_BASE[l] + k - LAG, steps[k - LAG][1])
                gaps = iter(hyena_fill(l))
                drain_fill(next(gaps))
                act.wait_ge(sem("vt_ready"), l + 1)
                act.activation(VTK[:, 0:2 * ns, :], ps[:, 0:2 * ns, :], ACT.Copy).then_inc(sem("vt_done"), 1)
                drain_fill(next(gaps))
                for s in range(ns):
                    act.wait_ge(sem("vf_ready"), 2 * l + s + 1)
                    act.activation(VFT, ps[:, :, :], ACT.Copy).then_inc(sem("vf_done"), 1)
                    drain_fill(next(gaps))
                    if s < ns - 1:
                        drain_fill(next(gaps))
                drain_fill([("oh", l, i) for i in range(2 * KD)])
                updates(ffn_norm[l], lambda m: gated("w_out2", l, m, 2))
                modulate(ffn_norm[l], l, 1)
                if l == 0:
                    act.wait_ge(sem("hyena"), N_SEQ[0])
                    act.dma_start(W4[0:64, :], fw4[1]).then_inc(sem("w4_loaded"), 16)
                    act.dma_start(hn[:, :], consts[:, N_KEPT:]).then_inc(sem("filter_tables"), 16)
                for i in range(KF):
                    drain(CHUNK["gu", l, 2 * i], AF[:, i, 0:n], ACT.Silu, n)
                    to_take("gu", l, 2 * i + 1, n=n)
                    if l == 0 and i in FILTER_2[1:4]:
                        filter_sin(1, FILTER_2.index(i) - 1)
                    if l == 0 and i == FILTER_2[4] + 1:
                        filter_spectrum(1)
                updates(mix_norm[1] if l == 0 else 7, lambda m: gated("down", l, m, 5))
            act.wait_ge(sem("norm_h"), 8 * KD)
            act.dma_start(out, H[:, :, 0:T]).then_inc(sem("stored"), 16)
            act.wait_ge(sem("stored"), 16)

        @block.vector
        def _(dve):
            links = [0]

            def link(ins):
                links[0] += 1
                ins.then_inc(sem("dve_link"), 1)
                dve.wait_ge(sem("dve_link"), links[0])

            def within_pi(dst, arg, n, tmp, shift=0.0):
                magic = 1.5 * 2.0 ** 23
                c1 = 6.28125
                c2 = math.floor((TWO_PI - c1) * 2.0 ** 22) / 2.0 ** 22
                c3 = TWO_PI - c1 - c2
                link(dve.tensor_scalar(tmp, arg, 1.0 / TWO_PI, shift / TWO_PI, MUL, ADD))
                link(dve.tensor_scalar(tmp, tmp, magic, None, ADD))
                link(dve.tensor_scalar(tmp, tmp, -magic, None, ADD))
                link(dve.scalar_tensor_tensor(dst, tmp, -c1, arg, MUL, ADD))
                link(dve.scalar_tensor_tensor(dst, tmp, -c2, dst, MUL, ADD))
                link(dve.scalar_tensor_tensor(dst, tmp, -c3, dst, MUL, ADD))
                if shift:
                    link(dve.tensor_scalar(dst, dst, shift, None, ADD))
                lim = 3.1415925
                return dve.tensor_scalar(dst, dst, lim, -lim, ALU.min, MAX)

            def norm(i, gain, at, dst=None):
                n = N_NORM[i]
                dve.wait_ge(sem("norm_rms"), i + 1)
                link(dve.reciprocal(rstd[:, 0:n], rstd[:, 0:n]))
                for k in range(KD):
                    dve.scalar_tensor_tensor((H if dst is None else dst)[:, k, 0:n], X[:, k, 0:n], PR(gain, at + k),
                                             rstd[:, 0:n], MUL, MUL).then_inc(sem("h_whole" if i in SPLIT_NORMS else "norm_h"), 1)
                if i in SPLIT_NORMS:
                    low_part(i)

            def low_part(i):
                n = N_NORM[i]
                for k in range(KD):
                    dve.wait_ge(sem("h_high"), KD * SPLIT_NORMS.index(i) + k + 1)
                    dve.tensor_tensor(HL[:, k, 0:n], H[:, k, 0:n], HH[:, k, 0:n].bitcast(F32), SUB).then_inc(sem("norm_h"), 1)

            def norm_over(i):
                n = N_NORM[i]
                dve.wait_ge(sem("norm_rms"), i + 1)
                link(dve.reciprocal(rstd[:, 0:n], rstd[:, 0:n]))
                for k in range(KD):
                    dve.tensor_tensor(H[:, k, 0:n], X[:, k, 0:n], rstd[:, 0:n], MUL).then_inc(sem("normed"), 1)
                low_part(i)

            def head_norm(i, dst, gain):
                a, b = dst.shape[1], dst.shape[2]
                dve.wait_ge(sem("hn_rms"), i + 1)
                link(dve.reciprocal(hn[:, 0:a * b], hn[:, 0:a * b]))
                dve.scalar_tensor_tensor(dst, dst, gain, hn[:, 0:a * b].rearrange("p (a b) -> p a b", a=a), MUL, MUL)\
                    .then_inc(sem("hn_done"), 1)

            def conv31(l, m):
                dve.wait_ge(sem("take_used"), TAKE["ag", l, 2 * m + 1] + 1)
                dve.wait_ge(sem("conv_pad"), l + 1)
                w = (l * KD + m) * CONV_K
                link(dve.tensor_scalar(CV[:, m, :], U[:, m, 0:T], PR("conv_dw_w", w), PR("conv_dw_b", l * KD + m), MUL, ADD))
                for t in range(1, CONV_K):
                    ins = dve.scalar_tensor_tensor(CV[:, m, :], U[:, m, t:t + T], PR("conv_dw_w", w + t), CV[:, m, :], MUL, ADD)
                    if t < CONV_K - 1:
                        link(ins)
                ins.then_inc(sem("conv_done"), 1)

            def sconv(l, j):
                dve.wait_ge(sem("drained"), CHUNK["dn", l, j] + 1)
                w = (l * 24 + j) * SHORT_K
                link(dve.tensor_scalar(DN[:, j, :], raw[:, j % 4, 0:T], PR("dn_conv_w", w), None, MUL))
                for t in range(1, SHORT_K):
                    ins = dve.scalar_tensor_tensor(DN[:, j, :], raw[:, j % 4, t:t + T], PR("dn_conv_w", w + t), DN[:, j, :], MUL, ADD)
                    if t < SHORT_K - 1:
                        link(ins)
                ins.then_inc(sem("sconv"), 1)

            def attention_scores(l, it):
                i = 2 * HEADS * l + it
                b = it % 2
                e = P * (b + 1)
                dve.wait_ge(sem("att_scores"), i + 1)
                if i >= 2:
                    dve.wait_ge(sem("att_weights"), i - 1)
                s = AT_S[:, i % 2, :].rearrange("p (m k) -> p m k", m=2)[:, :, 0:e]
                mask = C("causal1", P, P) if b == 0 else C("causal1")
                dve.scalar_tensor_tensor(s, ps[:, 0:2, 0:e], QK_S,
                                         rep(mask, 2), MUL, ADD).then_inc(sem("att_masked"), 1)
                dve.wait_ge(sem("att_masked"), i + 1)
                dve.tensor_reduce(at_m[:, i % 2, :], s, AX.X, MAX, negate=True).then_inc(sem("att_max"), 1)

            def attention_weights(l, it):
                i = 2 * HEADS * l + it
                e = P * (it % 2 + 1)
                dve.wait_ge(sem("att_exp"), i + 1)
                if i >= 2:
                    dve.wait_ge(sem("att_turn"), i - 1)
                r = at_l[:, i % 2, :]
                link(dve.reciprocal(r, r))
                link(dve.tensor_scalar(r[:, 1:2], r[:, 1:2], lam[:, 4 + l:5 + l], None, MUL))
                link(dve.tensor_scalar(AT_A[:, i % 2, 0:e], AT_S[:, i % 2, 0:e], r[:, 0:1], None, MUL))
                dve.scalar_tensor_tensor(AT_A[:, i % 2, 0:e], AT_S[:, i % 2, T:T + e], r[:, 1:2], AT_A[:, i % 2, 0:e], MUL, ADD)\
                    .then_inc(sem("att_weights"), 1)

            def attention_out(l, it):
                i = 2 * HEADS * l + it
                dve.wait_ge(sem("att_o"), i + 1)
                dve.tensor_copy(QK[:, it // 2, (it % 2) * P:(it % 2 + 1) * P], ps[:, 3, 0:P]).then_inc(sem("att_out"), 1)

            def delta_gates(l):
                dve.wait_ge(sem("beta"), l + 1)
                both = ps[:, 0, 0:32].rearrange("p (c n) -> p c n", c=NT)
                link(dve.tensor_tensor(B0, both[:, :, HEADS:], rep(PR("dn_dt_bias", l * HEADS, HEADS), NT), ADD))
                dve.scalar_tensor_tensor(B1, B0, -1.0, B0, MUL, MAX).then_inc(sem("abs_a"), 1)
                dve.wait_ge(sem("ln_abs"), l + 1)
                link(dve.tensor_scalar(GC, B1, 1.0, None, ADD))
                link(dve.tensor_scalar(NGC, GC, -1.0, None, ADD))
                link(dve.tensor_tensor(NGC, B1, NGC, SUB))
                link(dve.reciprocal(GC, GC))
                link(dve.tensor_tensor(NGC, NGC, GC, MUL))
                link(dve.tensor_tensor(B2, B2, NGC, ADD))
                link(dve.scalar_tensor_tensor(B0, B0, 0.0, B2, MAX, ADD))
                dve.wait_ge(sem("exp_a"), l + 1)
                dve.scalar_tensor_tensor(G, B0, -1.0, rep(EXA, NT), MUL, MUL).then_inc(sem("g_done"), 1)
                head_norm(HN_BASE1(l) + DK_N, DN[:, 8:16, :], 1.0)
                dve.wait_ge(sem("exp_gc"), l + 1)
                link(dve.tensor_scalar(NGC, ps[:, 1, 0:16].rearrange("p (c h) -> p c h", c=NT), -1.0, None, MUL))
                dve.tensor_tensor(BEG, BEG, BETA, MUL).then_inc(sem("gates_done"), 1)
                dve.wait_ge(sem("gates_done"), l + 1)

            def level(i, s):
                dve.tensor_tensor(LM[s % 2].rearrange("p (a b) -> p a b", a=4), LT.rearrange("p (a b) -> p a b", a=4),
                                  rep(C("levels", s * P, P), 4), MUL).then_inc(sem("d_lm"), 1)

            def delta(l, u):
                i = 4 * l + u
                q4 = lambda ap: ap.rearrange("p (a b) -> p a b", a=4)
                for p in range(4):
                    h, c = 2 * u + p // 2, p % 2
                    dve.tensor_scalar(UG[:, p * P:(p + 1) * P], C("until"), G[:, c, h:h + 1], None, MUL)
                    ins = dve.tensor_scalar(IB[:, p * P:(p + 1) * P], ident, BETA[:, c, h:h + 1], None, MUL)
                ins.then_inc(sem("d_ugib"), 1)
                dve.wait_ge(sem("d_pre"), 4 * i + 1)
                dve.tensor_tensor(q4(DT), q4(ps[:, 0, :]), rep(C("later"), 4), ADD).then_inc(sem("d_dt"), 1)
                dve.wait_ge(sem("d_pre"), 4 * i + 4)
                dve.wait_ge(sem("d_exp"), i + 1)
                link(dve.tensor_tensor(LT, ps[:, 2, :], DT, MUL))
                dve.tensor_tensor(IN, ps[:, 3, :], DT, MUL)
                dve.tensor_tensor(LT, LT, ps[:, 1, :], MUL).then_inc(sem("d_lt"), 1)
                dve.tensor_tensor(QG, DN[:, 2 * u:2 * u + 2, P:T], EXR, MUL).then_inc(sem("d_qg"), 1)
                dve.wait_ge(sem("d_lt"), i + 1)
                level(i, 0)
                level(i, 1)
                dve.wait_ge(sem("d_lm"), 7 * i + 1)
                dve.scalar_tensor_tensor(q4(TT), q4(LM[0]), -1.0, rep(ident, 4), MUL, ADD).then_inc(sem("d_tt"), 1)
                dve.wait_ge(sem("d_tt"), i + 1)
                for s in range(1, 7):
                    if s < 6:
                        if s > 1:
                            dve.wait_ge(sem("d_x"), 6 * i + s - 1)
                        level(i, s + 1)
                    dve.wait_ge(sem("d_bc"), 6 * i + s)
                    if s < 6:
                        if s == 1:
                            dve.wait_ge(sem("d_tm"), i + 1)
                        dve.tensor_tensor(TM, TM, ps[:, 3, :], SUB)
                    dve.tensor_tensor(TT, TT, ps[:, 2, :], SUB).then_inc(sem("d_upd"), 1)
                    dve.wait_ge(sem("d_upd"), 6 * i + s)
                dve.wait_ge(sem("d_kv"), i + 1)
                for p in range(4):
                    h, c = 2 * u + p // 2, p % 2
                    dve.tensor_scalar(VB[:, p * P:(p + 1) * P], ps[:, 1, p * P:(p + 1) * P], BETA[:, c, h:h + 1], None, MUL)
                    if c:
                        ins = dve.tensor_scalar(KBG[:, p // 2, :], ps[:, 0, p * P:(p + 1) * P], BEG[:, 1, h:h + 1], None, MUL)
                    else:
                        dve.tensor_scalar(KDEC[:, p // 2, :], ps[:, 0, p * P:(p + 1) * P],
                                          DT[:, (p + 1) * P - 1:(p + 1) * P], None, MUL)
                ins.then_inc(sem("d_vb"), 1)

            dve.wait_ge(sem("loaded"), 48)
            dve.wait_ge(sem("x_loaded"), 16)
            norm(0, "norm_w", 0)
            link(dve.tensor_copy(POSF, ANGI))
            link(dve.tensor_scalar(RR[:, 1, :], POSF, C("inv1"), None, MUL))
            within_pi(POSF, RR[:, 1, :], T, RR[:, 2, :]).then_inc(sem("ang"), 1)
            within_pi(RR[:, 0, :], RR[:, 1, :], T, RR[:, 2, :], math.pi / 2).then_inc(sem("ang"), 1)
            lqp = RR[:, 1:3, :].rearrange("p a b -> p (a b)")[:, 0:4 * QK_DIM]
            lq = PR("lam_qk", 0, DEPTH * 4 * QK_DIM).rearrange("p (l a d) -> p l a d", a=4, d=QK_DIM)
            for l in range(DEPTH):
                for a in range(2):
                    link(dve.tensor_tensor(lqp[:, (2 * l + a) * QK_DIM:(2 * l + a + 1) * QK_DIM], lq[:, l, 2 * a, :], lq[:, l, 2 * a + 1, :], MUL))
            dve.tensor_reduce(lam[:, 0:4], lqp.rearrange("p (a d) -> p a d", a=4), AX.X, ADD).then_inc(sem("lam_dots"), 1)
            dve.wait_ge(sem("lam_exp"), 1)
            for l in range(DEPTH):
                link(dve.tensor_tensor(lam[:, 4 + l:5 + l], lam[:, 2 * l + 1:2 * l + 2], lam[:, 2 * l:2 * l + 1], SUB))
                link(dve.tensor_tensor(lam[:, 4 + l:5 + l], lam[:, 4 + l:5 + l], C("lam_init", l, 1), SUB))
            for l in range(DEPTH):
                link(dve.tensor_scalar(lam[:, 6 + l:7 + l], PR("attn_subln_w", l), 1.0 - (0.8 - 0.6 * math.exp(-0.3 * l)), None, MUL))
            dve.wait_ge(sem("rope_table"), 1)
            def rope(i, qk, cos, sin):
                if i:
                    dve.wait_ge(sem("rope"), i)
                dve.wait_ge(sem("rot"), i + 1)
                link(dve.tensor_tensor(cut(at_buf, 0, 2, T), qk, rep(cos, 2), MUL))
                link(dve.tensor_tensor(cut(at_buf, 512, 2, T), ps[:, 2 + i % 2, :].rearrange("p (a b) -> p a b", a=2),
                                       rep(sin, 2), MUL))
                dve.tensor_tensor(qk, cut(at_buf, 0, 2, T), cut(at_buf, 512, 2, T), ADD).then_inc(sem("rope"), 1)

            def modulation(l):
                dve.wait_ge(sem("drained"), CHUNK["modt", l, MODS - 1] + 1)
                link(dve.tensor_tensor(mod[:, l, :, :], mod[:, l, :, :], wide(PR("b_mod", l * N_MOD * KD, N_MOD * KD), 2), ADD))
                for which, gain in ((0, "norm_mix"), (1, "norm_ffn")):
                    at = (3 * which + 1) * KD
                    ins = dve.scalar_tensor_tensor(gains[:, which, :, :], mod[:, l, at:at + KD, :], 1.0,
                                                   wide(PR(gain, l * KD, KD), 2), ADD, MUL)
                ins.then_inc(sem("mod_done"), 1)

            def filters(l):
                for k in range(3):
                    dve.wait_ge(sem("f_ready"), 3 * l + k + 1)
                    link(dve.tensor_scalar(RR[0:64, 1, :], ps[0:64, 1, 0:T], PR("filt_b", 3 * l + k)[0:64],
                                           PR("filt_freq", 3 * l + k)[0:64], ADD, MUL))
                    within_pi(RR[0:64, 0, :], RR[0:64, 1, :], T, RR[0:64, 2, :]).then_inc(sem("f_arg"), 1)
                dve.wait_ge(sem("h4_ready"), l + 1)
                dve.wait_ge(sem("filter_tables"), 16 * (l + 1))
                for half in range(2):
                    ins = dve.tensor_tensor(VTK[:, 2 * half:2 * half + 2, :], ps[:, 2 * half:2 * half + 2, :],
                                            DECAY.rearrange("p (a b) -> p a b", a=NT), MUL)
                ins.then_inc(sem("h4_done"), 1)

            for l in range(DEPTH):
                if l:
                    norm(l, "norm_w", l * KD)
                for m in range(KD):
                    conv31(l, m)
                dve.wait_ge(sem("ln_mean"), l + 1)
                dve.scalar_tensor_tensor(CV, rep(ps[:, 0, 0:T], KD), -1.0 / D, CV, MUL, ADD).then_inc(sem("ln_centered"), 1)
                for j in range(24):
                    if j < 8:
                        rope(8 * l + j, QK[:, 2 * j:2 * j + 2, :], tab[:, 0, :], tab[:, 1, :])
                    sconv(l, j)
                    if j == 1:
                        dve.wait_ge(sem("ln_centered"), l + 1)
                        dve.wait_ge(sem("ln_rms"), l + 1)
                        link(dve.reciprocal(rstd[:, 0:T], rstd[:, 0:T]))
                        dve.tensor_tensor(CV, CV, rep(rstd[:, 0:T], KD), MUL).then_inc(sem("ln_normed"), 1)
                    if j == 11:
                        head_norm(HN_BASE1(l) + DQ_N, DN[:, 0:8, :], DN_S)
                dve.wait_ge(sem("tables"), 32)
                delta_gates(l)
                for it in range(ATT_STEPS + LAG + 1):
                    if it < ATT_STEPS:
                        attention_scores(l, it)
                    if 1 <= it <= ATT_STEPS:
                        attention_weights(l, it - 1)
                    if it > LAG:
                        attention_out(l, it - LAG - 1)
                head_norm(HN_BASE1(l) + ATT_N, QK[:, 0:8, :], lam[:, 6 + l:7 + l])
                for u in range(UNITS):
                    delta(l, u)
                head_norm(HN_BASE1(l) + DO_N, DN[:, 0:8, :], PR("dn_norm_w", l))
            modulation(0)
            filters(0)
            norm(2, "final_norm_w", 0, X)

            def attention2_max(i, s):
                n = 2 * T if s == 0 else T
                dve.wait_ge(sem("a2_scores"), i + 1)
                link(dve.tensor_reduce(at_m[:, i % 2, 0:1], ps[:, i % 2, 0:n], AX.X, MAX, negate=True))
                dve.tensor_scalar(at_m[:, i % 2, 0:1], at_m[:, i % 2, 0:1], P ** -0.5, None, MUL).then_inc(sem("a2_max"), 1)

            def attention2_weights(i, s):
                n = 2 * T if s == 0 else T
                dve.wait_ge(sem("a2_exp"), i + 1)
                if i >= 2:
                    dve.wait_ge(sem("a2_turn"), i - 1)
                link(dve.reciprocal(at_l[:, i % 2, 0:1], at_l[:, i % 2, 0:1]))
                dve.tensor_scalar(AT_A[:, i % 2, 0:n], AT_S[:, i % 2, 0:n], at_l[:, i % 2, 0:1], None, MUL)\
                    .then_inc(sem("a2_weights"), 1)

            def attention2_out(i, step):
                h, s, b = step
                dve.wait_ge(sem("a2_o"), i + 1)
                dve.tensor_copy(Q2_[:, h, s * T + b * P:s * T + (b + 1) * P], ps[:, 3, 0:P]).then_inc(sem("a2_out"), 1)

            def hyena_conv(l, j):
                n, ns = N_TOK[l], N_SEQ[l]
                dve.wait_ge(sem("drained"), CHUNK["hy2", l, j] + 1)
                s0 = (j % 2) * 2
                dst = (X0, X1, VX)[j // 4][:, j % 4, 0:n].rearrange("p (s t) -> p s t", s=ns)
                w = (l * 12 + j) * HY_TAPS
                link(dve.tensor_scalar(dst, hraw[:, s0:s0 + ns, 0:T], PR("conv_w", w), PR("conv_b", l * 12 + j), MUL, ADD))
                link(dve.scalar_tensor_tensor(dst, hraw[:, s0:s0 + ns, 1:T + 1], PR("conv_w", w + 1), dst, MUL, ADD))
                ins = dve.scalar_tensor_tensor(dst, hraw[:, s0:s0 + ns, 2:T + 2], PR("conv_w", w + 2), dst, MUL, ADD)
                if j >= 8:
                    link(ins)
                    ins = dve.tensor_tensor(VX[:, j - 8, 0:n], VX[:, j - 8, 0:n], X1[:, j - 8, 0:n], MUL)
                ins.then_inc(sem("hconv"), 1)

            def rope2(l, jj):
                rope(ROPE2[l] + jj, Q2_[:, 2 * jj - 2:2 * jj, 0:T] if jj else K2_[:, :, 0:T], C("cos2"), C("sin2"))

            for l in range(DEPTH):
                n, ns = N_TOK[l], N_SEQ[l]
                norm_over(mix_norm[l])
                i = HN_BASE2[l]
                if l == 0:
                    head_norm(i, Q2_[:, 0:4, :], PR("q_norm", l))
                    head_norm(i + 1, Q2_[:, 4:8, :], PR("q_norm", l))
                    head_norm(i + 2, K2_, PR("k_norm", l))
                else:
                    head_norm(i, Q2_[:, :, 0:T], PR("q_norm", l))
                    head_norm(i + 1, K2_, PR("k_norm", l))
                for j in range(EARLY_HY):
                    hyena_conv(l, j)
                    for jj in ROPES_AFTER[j]:
                        rope2(l, jj)
                steps = IT2[l]
                for k, items in enumerate(att2_fill(l)):
                    i = IT2_BASE[l] + k
                    if k < len(steps):
                        attention2_max(i, steps[k][1])
                    if 1 <= k <= len(steps):
                        attention2_weights(i - 1, steps[k - 1][1])
                    if k > LAG:
                        attention2_out(i - LAG - 1, steps[k - LAG - 1])
                    for name, l_, j in items:
                        hyena_conv(l, j)
                for s in range(ns):
                    k = 2 * l + s
                    re, im = slice(0, 2), slice(2, 4)
                    dve.wait_ge(sem("vf_done"), k + 1)
                    dve.wait_ge(sem("kf_done"), l + 1)
                    dve.tensor_tensor(YFT[:, re, :], VFT[:, re, :], KFT[:, re, :], MUL)
                    link(dve.tensor_tensor(PROD, VFT[:, im, :], KFT[:, im, :], MUL))
                    dve.tensor_tensor(YFT[:, im, :], VFT[:, re, :], KFT[:, im, :], MUL)
                    link(dve.tensor_tensor(YFT[:, re, :], YFT[:, re, :], PROD, SUB))
                    link(dve.tensor_tensor(PROD, VFT[:, im, :], KFT[:, re, :], MUL))
                    link(dve.tensor_tensor(YFT[:, im, :], YFT[:, im, :], PROD, ADD))
                    dve.tensor_tensor(YFT[0:1, 0, :], VFT[0:1, 0, :], KFT[0:1, 0, :], MUL)
                    dve.tensor_tensor(YFT[0:1, 2, :], VFT[0:1, 2, :], KFT[0:1, 2, :], MUL).then_inc(sem("y_done"), 1)
                    dve.wait_ge(sem("yi_ready"), k + 1)
                    for m in range(KH):
                        link(dve.scalar_tensor_tensor(VX[:, m, s * T:(s + 1) * T], VX[:, m, s * T:(s + 1) * T], PR("hyena_bias", l * KH + m),
                                                      ps[:, m // 2, (m % 2) * T:(m % 2 + 1) * T], MUL, ADD))
                    dve.tensor_tensor(X0[:, :, s * T:(s + 1) * T], X0[:, :, s * T:(s + 1) * T], VX[:, :, s * T:(s + 1) * T], MUL)\
                        .then_inc(sem("hyena"), 1)
                norm_over(ffn_norm[l])
                if l == 0:
                    dve.wait_ge(sem("norm_h"), KD * (ffn_norm[0] + 1))
                    modulation(1)
                    filters(1)
            norm(7, "norm_final", 0)

        @block.tensor
        def _(pe):
            at = {"tile": 0, "free": 0, "chunk": 0, "split": 0, "raw": False}

            def tile(n=1, split=False):
                t = at["tile"]
                at["tile"] += n
                load, off = divmod(t, TILES)
                if not split and (off == 0 or not at["raw"]):
                    pe.wait_ge(sem(f"weights{load % RING}"), 16 * (load // RING + 1))
                assert off + n <= TILES
                if t in PIECE_OF:
                    pe.wait_ge(sem("low_ready"), PIECE_OF[t] + 1)
                if off + n == TILES:
                    at["free"] += 1
                at["raw"] = not split
                cols = slice(off * P, (off + n) * P)
                if not split:
                    return ring[:, load % RING, cols]
                place = at["split"] % HIGHS
                at["split"] += n
                return ring_hi[:, place * P:(place + n) * P], ring_lo[:, load % RING, cols]

            def parts(out, a, b, start, stop):
                first = pe.matmul(out, a[0], b[0], start=start, stop=False)
                pe.matmul(out, a[1], b[0], start=False, stop=False)
                return first, pe.matmul(out, a[0], b[1], start=False, stop=stop)

            def chunk(name, l, i, k, rhs, n, arrived=None):
                for half in chunk_halves(name, l, i, k, rhs, n, arrived):
                    pass

            def chunk_halves(name, l, i, k, rhs, n, arrived=None):
                j = CHUNK[name, l, i]
                assert j == at["chunk"], (name, l, i)
                at["chunk"] += 1
                if j >= 4:
                    pe.wait_ge(sem("drained"), j - 3)
                for c in range(k):
                    freed = at["free"]
                    if arrived:
                        arrived(c)
                    first = None
                    if is_split(name, i):
                        first, ins = parts(pg[:, j % 4, 0:n], tile(split=True), (HH[:, c, 0:n], HL[:, c, 0:n]), c == 0, c == k - 1)
                    elif name == "mod":
                        ins = pe.matmul(pg[0:2, j % 4, :], sc[:, c, :], tile(4), start=c == 0, stop=c == k - 1)
                    else:
                        ins = pe.matmul(pg[:, j % 4, 0:n], tile(), rhs(c), start=c == 0, stop=c == k - 1)
                    if freed and (first or c < k - 1):
                        (first or ins).then_inc(sem("slot_free"), freed)
                        at["free"] -= freed
                    if c == k // 2 - 1:
                        yield
                ins.then_inc(sem("chunk_ready"), 1)

            def turn_rows(l, i):
                j = CHUNK["modt", l, i]
                assert j == at["chunk"]
                at["chunk"] += 1
                pe.wait_ge(sem("drained"), max(CHUNK["mod", l, i] + 1, j - 3))
                for q in range(4):
                    ins = pe.transpose(pg[:, j % 4, 2 * q:2 * q + 2], mod_rows[0:2, i % 2, q * P:(q + 1) * P], ident[0:2, 0:2])
                ins.then_inc(sem("chunk_ready"), 1)

            def normed(i):
                def wait(c):
                    pe.wait_ge(sem("norm_h"), KD * i + c + 1)
                return wait

            def joined(name, l, step):
                def wait(c):
                    pe.wait_ge(sem("take_used"), TAKE[name, l, step * c + 1] + 1)
                return wait

            started = []

            def fill(items):
                for item in items:
                    if item[0] == "half":
                        started.append(halves_of(*item[1]))
                        next(started[0])
                    elif item[0] == "modt":
                        turn_rows(*item[1:])
                    else:
                        for half in started or [halves_of(*item)]:
                            for step in half:
                                pass
                        started.clear()

            def halves_of(name, l, i):
                if name == "mod":
                    return chunk_halves(name, l, i, KD, None, 512)
                if name in ("cz", "az", "dz"):
                    return chunk_halves(name, l, i, KD, rows_of(H, T), T)
                if name == "hy2":
                    return chunk_halves(name, l, i, KD, rows_of(H, N_TOK[l]), N_TOK[l])
                if name in ("c_out", "a_out", "d_out"):
                    z, branch = {"c_out": ("cz", CV), "a_out": ("az", QK), "d_out": ("dz", DN)}[name]

                    def multiplied(c):
                        pe.wait_ge(sem("take_used"), TAKE[z, l, c] + 1)
                    return chunk_halves(name, l, i, KD, rows_of(branch if i % 2 else H, T), T, multiplied if i == 1 else None)
                k, src = {"oa": (KD, Q2_), "oh": (KH, X0)}[name] if i % 2 else (KD, H)
                return chunk_halves(name, l, i, k, rows_of(src, N_TOK[l]), N_TOK[l])

            def filter_step(l, step):
                if step < 3:
                    if step == 0:
                        lhsT, rhs = PR("filt_w1", l * 64, 64)[0:33], C("zT")[0:33]
                        if l == 0:
                            pe.wait_ge(sem("hn_rms"), HN_BASE1(1) + DO_N + 1)
                        else:
                            pe.wait_ge(sem("norm_rms"), ffn_norm[0] + 1)
                    else:
                        lhsT, rhs = PR(f"filt_w{step + 1}", l * 64, 64)[0:64], HQ[0:64, :]
                        pe.wait_ge(sem("f_sin"), 3 * l + step)
                    pe.matmul(ps[0:64, 1, 0:T], lhsT, rhs, start=True, stop=True).then_inc(sem("f_ready"), 1)
                elif step == 3:
                    pe.wait_ge(sem("f_sin"), 3 * l + 3)
                    pe.wait_ge(sem("w4_loaded"), 16 * (l + 1))
                    for half in range(2):
                        for tt in range(NT):
                            ins = pe.matmul(ps[:, 2 * half + tt, :], HQ[0:64, tt * P:(tt + 1) * P],
                                            W4[0:64, half * HY:(half + 1) * HY], start=True, stop=True)
                    ins.then_inc(sem("h4_ready"), 1)
                else:
                    pe.wait_ge(sem("h4_done"), l + 1)
                    for ft in range(4):
                        for q in range(4):
                            table = C("dft_fwd") if q < 2 else DFT_BWD
                            ins = pe.matmul(ps[:, ft, :], table[:, (q % 2) * N_FFT + ft * P:(q % 2) * N_FFT + (ft + 1) * P], VTK[:, q, :], start=q == 0, stop=q == 3)
                    ins.then_inc(sem("kf_ready"), 1)

            def rows_of(buf, n):
                return lambda c: buf[:, c, 0:n]

            def norm(i):
                n = N_NORM[i]
                fill(norm_mods(i, "a"))
                for k in range(KD):
                    pe.wait_ge(sem("norm_sq"), KD * i + k + 1)
                    ins = pe.matmul(ps[:, 0, 0:n], ones, H[:, k, 0:n], start=k == 0, stop=k == KD - 1)
                ins.then_inc(sem("norm_ss"), 1)
                fill(norm_mods(i, "b"))

            def head_norm(i, cols):
                pe.wait_ge(sem("hn_sq"), i + 1)
                for b in range(cols // 512):
                    ins = pe.matmul(ps[:, b, :], ones, sq[:, b * 512:(b + 1) * 512], start=True, stop=True)
                ins.then_inc(sem("hn_ss"), 1)

            def rot(i, table, qk):
                if i >= 2:
                    pe.wait_ge(sem("rope"), i - 1)
                pe.matmul(ps[:, 2 + i % 2, :], table, qk, start=True, stop=True).then_inc(sem("rot"), 1)

            def tokens_first(name, l, i, w, tt, n, freed=0):
                j = CHUNK[name, l, i]
                assert j == at["chunk"]
                at["chunk"] += 1
                if j >= 4:
                    pe.wait_ge(sem("drained"), j - 3)
                for k in range(KD):
                    t = slice(tt * P, (tt + 1) * P)
                    first, ins = parts(pg[:, j % 4, 0:n], (HH[:, k, t], HL[:, k, t]), w[k], k == 0, k == KD - 1)
                    if freed and k == 0:
                        first.then_inc(sem("slot_free"), freed)
                        at["free"] -= freed
                ins.then_inc(sem("chunk_ready"), 1)

            def attention_scores(l, it):
                i = 2 * HEADS * l + it
                h, b = it // 2, it % 2
                e = P * (b + 1)
                if i >= 1:
                    pe.wait_ge(sem("att_masked"), i)
                for m in range(2):
                    r = slice(m * QK_DIM, (m + 1) * QK_DIM)
                    ins = pe.matmul(ps[:, m, 0:e], QK[r, h, b * P:(b + 1) * P], QK[r, HEADS + h, 0:e],
                                    start=True, stop=True)
                ins.then_inc(sem("att_scores"), 1)

            def attention_turn(l, it):
                i = 2 * HEADS * l + it
                pe.wait_ge(sem("att_weights"), i + 1)
                if i >= 1:
                    pe.wait_ge(sem("att_turned"), i)
                for kb in range(it % 2 + 1):
                    ins = pe.transpose(ps[:, 2, kb * P:(kb + 1) * P], AT_A[:, i % 2, kb * P:(kb + 1) * P], ident)
                ins.then_inc(sem("att_turn"), 1)

            def attention_out(l, it):
                i = 2 * HEADS * l + it
                h, b = it // 2, it % 2
                pe.wait_ge(sem("att_turned"), i + 1)
                if i >= 1:
                    pe.wait_ge(sem("att_out"), i)
                for kb in range(b + 1):
                    ins = pe.matmul(ps[:, 3, 0:P], V[:, kb, h * P:(h + 1) * P], AT_T[:, i % 2, kb * P:(kb + 1) * P],
                                    start=kb == 0, stop=kb == b)
                ins.then_inc(sem("att_o"), 1)

            def delta_gates(l):
                pe.wait_ge(sem("hn_rms"), HN_BASE1(l) + DK_N + 1)
                for c in range(NT):
                    for k in range(KD):
                        a = (l * KD + k) * 16
                        for part, src in enumerate((HH, HL)):
                            ins = pe.matmul(ps[:, 0, c * 16:(c + 1) * 16], src[:, k, c * P:(c + 1) * P].bitcast(F32), PR("w_ba", a, 16),
                                            start=k + part == 0, stop=k + part == KD)
                ins.then_inc(sem("ba_ready"), 1)
                fill([("cz", l, m) for m in range(EARLY_CZ // 2)] + mods(l, "gates"))
                pe.wait_ge(sem("g_done"), l + 1)
                for c in range(NT):
                    ins = pe.matmul(ps[:, 1, c * HEADS:(c + 1) * HEADS], C("until"), G[:, c, :], start=True, stop=True)
                ins.then_inc(sem("gc_ready"), 1)
                fill([("cz", l, m) for m in range(EARLY_CZ // 2, EARLY_CZ)])
                pe.wait_ge(sem("gates_done"), l + 1)

            def delta(l, u):
                i = 4 * l + u
                pair = [(2 * u + p // 2, p % 2, slice(p * P, (p + 1) * P)) for p in range(4)]
                kT = lambda h, c: DN[:, HEADS + h, c * P:(c + 1) * P]
                vT = lambda h, c: DN[:, 2 * HEADS + h, c * P:(c + 1) * P]
                gaps = iter(delta_fill(l)[u * DELTA_POINTS:(u + 1) * DELTA_POINTS])
                fill(next(gaps))
                pe.wait_ge(sem("d_ugib"), i + 1)
                if u == 0:
                    pe.wait_ge(sem("hn_rms"), HN_BASE1(l) + ATT_N + 1)
                else:
                    pe.wait_ge(sem("d_out"), i)
                pe.matmul(ps[:, 0, :], ones, UG, start=True, stop=True).then_inc(sem("d_pre"), 1)
                pe.matmul(ps[:, 1, :], ones, IB, start=True, stop=True).then_inc(sem("d_pre"), 1)
                for h, c, s in pair:
                    ins = pe.matmul(ps[:, 2, s], kT(h, c), kT(h, c), start=True, stop=True)
                ins.then_inc(sem("d_pre"), 1)
                for h, c, s in pair:
                    ins = pe.matmul(ps[:, 3, s], kT(h, c), DN[:, h, c * P:(c + 1) * P], start=True, stop=True)
                ins.then_inc(sem("d_pre"), 1)
                fill(next(gaps))
                pe.wait_ge(sem("d_tt"), i + 1)
                for h, c, s in pair:
                    ins = pe.transpose(ps[:, 0, s], TT[:, s], ident)
                ins.then_inc(sem("d_t0"), 1)
                for v in range(1, 7):
                    fill(next(gaps))
                    if v == 1:
                        pe.wait_ge(sem("d_tm"), i + 1)
                    pe.wait_ge(sem("d_lm"), 7 * i + v + 1)
                    if v > 1:
                        pe.wait_ge(sem("d_upd"), 6 * i + v - 1)
                    for h, c, s in pair:
                        ins = pe.matmul(ps[:, 1, s], LM[v % 2][:, s], TM[:, s], start=True, stop=True)
                    ins.then_inc(sem("d_x"), 1)
                    fill(next(gaps))
                    pe.wait_ge(sem("d_xs"), 6 * i + v)
                    if v < 6:
                        for h, c, s in pair:
                            pe.matmul(ps[:, 3, s], TT[:, s], XS[:, s], start=True, stop=True)
                    for h, c, s in pair:
                        ins = pe.matmul(ps[:, 2, s], XS[:, s], TT[:, s], start=True, stop=True)
                    ins.then_inc(sem("d_bc"), 1)
                for h, c, s in pair:
                    pe.transpose(ps[:, 0, s], kT(h, c), ident)
                for h, c, s in pair:
                    ins = pe.transpose(ps[:, 1, s], vT(h, c), ident)
                ins.then_inc(sem("d_kv"), 1)
                fill(next(gaps))
                pe.wait_ge(sem("d_vb"), i + 1)
                for hh in range(2):
                    pe.matmul(ps[:, 2, hh * P:(hh + 1) * P], KBG[:, hh, :], TT[:, pair[2 * hh + 1][2]], start=True, stop=True)
                for hh in range(2):
                    s = pair[2 * hh][2]
                    ins = pe.matmul(ps[:, 2, (2 + hh) * P:(3 + hh) * P], TT[:, s], VB[:, s], start=True, stop=True)
                ins.then_inc(sem("d_w"), 1)
                fill(next(gaps))
                pe.wait_ge(sem("d_vn0"), i + 1)
                for hh in range(2):
                    ins = pe.matmul(ps[:, 3, hh * P:(hh + 1) * P], KDEC[:, hh, :], VN[:, hh * P:(hh + 1) * P], start=True, stop=True)
                ins.then_inc(sem("d_s"), 1)
                fill(next(gaps))
                pe.wait_ge(sem("d_s1"), i + 1)
                for hh in range(2):
                    s = pair[2 * hh + 1][2]
                    pe.matmul(ps[:, 0, hh * P:(hh + 1) * P], TT[:, s], VB[:, s], start=True, stop=False)
                    ins = pe.matmul(ps[:, 0, hh * P:(hh + 1) * P], NW[:, hh, :], S1[:, hh, :], start=False, stop=True)
                ins.then_inc(sem("d_v1"), 1)
                fill(next(gaps))
                pe.wait_ge(sem("d_vn1"), i + 1)
                pe.wait_ge(sem("d_qg"), i + 1)
                for hh in range(2):
                    o = hh * T
                    pe.matmul(ps[:, 1, o:o + P], VN[:, hh * P:(hh + 1) * P], IN[:, pair[2 * hh][2]], start=True, stop=True)
                    pe.matmul(ps[:, 1, o + P:o + T], S1[:, hh, :], QG[:, hh, :], start=True, stop=False)
                    ins = pe.matmul(ps[:, 1, o + P:o + T], VN[:, (2 + hh) * P:(3 + hh) * P], IN[:, pair[2 * hh + 1][2]],
                                    start=False, stop=True)
                ins.then_inc(sem("d_o"), 1)

            pe.wait_ge(sem("loaded"), 48)
            norm(0)
            for l in range(DEPTH):
                hx = rows_of(H, T)
                for i in range(16):
                    chunk("ag", l, i, KD, hx, T, normed(l) if i == 0 else None)
                for i in range(16):
                    chunk("qk", l, i, KD, hx, T)
                for part in range(4):
                    freed = at["free"]
                    w = [tile(2, split=True) for k in range(KD)]
                    for tt in range(NT):
                        tokens_first("v", l, 2 * part + tt, w, tt, T, freed if tt == 0 else 0)
                pe.wait_ge(sem("conv_done"), KD * (l + 1))
                for m in range(KD):
                    ins = pe.matmul(ps[:, 0, 0:T], ones, CV[:, m, :], start=m == 0, stop=m == KD - 1)
                ins.then_inc(sem("ln_mean"), 1)
                pe.wait_ge(sem("drained"), CHUNK["qk", l, 15] + 1)
                if l == 0:
                    pe.wait_ge(sem("rope_table"), 1)
                    pe.wait_ge(sem("tables"), 32)
                for i in range(24):
                    if i < 8:
                        rot(8 * l + i, C("rot1"), QK[:, 2 * i:2 * i + 2, :])
                    if i == 11:
                        pe.wait_ge(sem("rope"), 8 * (l + 1))
                        head_norm(HN_BASE1(l) + DQ_N, 2048)
                    if i == 20:
                        pe.wait_ge(sem("hn_rms"), HN_BASE1(l) + DQ_N + 1)
                        head_norm(HN_BASE1(l) + DK_N, 2048)
                    chunk("dn", l, i, KD, hx, T)
                    if i == 1:
                        pe.wait_ge(sem("ln_sq"), l + 1)
                        for m in range(KD):
                            ins = pe.matmul(ps[:, 1, 0:T], ones, sq[:, m * T:(m + 1) * T], start=m == 0, stop=m == KD - 1)
                        ins.then_inc(sem("ln_ss"), 1)
                if l == 0:
                    pe.wait_ge(sem("silu_c"), 1)
                delta_gates(l)
                for it, items in enumerate(att_fill(l)):
                    if it < ATT_STEPS:
                        attention_scores(l, it)
                    fill(items)
                    if LAG <= it < ATT_STEPS + LAG:
                        attention_turn(l, it - LAG)
                    if it > LAG:
                        attention_out(l, it - LAG - 1)
                fill(mods(l, "att"))
                head_norm(HN_BASE1(l) + ATT_N, 2048)
                for u in range(UNITS):
                    delta(l, u)
                fill([("dz", l, m) for m in range(2)])
                head_norm(HN_BASE1(l) + DO_N, 2048)
                fill([("dz", l, m) for m in range(2, KD)])
                for i in range(2 * KD):
                    fill([("d_out", l, i)])
                    if l == DEPTH - 1 and i in FILTER_1:
                        filter_step(0, FILTER_1.index(i))
                for m in range(KD):
                    chunk("w_out", l, m, KD, rows_of(MG, T), T, joined("d_out", l, 2) if m == 0 else None)
                norm(l + 1)
            norm(3)

            def attention2_scores(i, step):
                h, s, b = step
                keys = slice(0, 2 * T) if s == 0 else slice(T, 2 * T)
                if i >= 2:
                    pe.wait_ge(sem("a2_exp"), i - 1)
                pe.matmul(ps[:, i % 2, 0:keys.stop - keys.start], Q2_[:, h, s * T + b * P:s * T + (b + 1) * P],
                          K2_[:, h // 4, keys], start=True, stop=True).then_inc(sem("a2_scores"), 1)

            def attention2_turn(i, step):
                pe.wait_ge(sem("a2_weights"), i + 1)
                if i >= 1:
                    pe.wait_ge(sem("a2_turned"), i)
                for kb in range(4 if step[1] == 0 else 2):
                    ins = pe.transpose(ps[:, 2, kb * P:(kb + 1) * P], AT_A[:, i % 2, kb * P:(kb + 1) * P], ident)
                ins.then_inc(sem("a2_turn"), 1)

            def attention2_out(i, step):
                h, s, b = step
                blocks = [0, 1, 2, 3] if s == 0 else [2, 3]
                g = h // 4
                pe.wait_ge(sem("a2_turned"), i + 1)
                if i >= 1:
                    pe.wait_ge(sem("a2_out"), i)
                for n, kb in enumerate(blocks):
                    ins = pe.matmul(ps[:, 3, 0:P], V2_[:, kb, g * P:(g + 1) * P], AT_T[:, i % 2, n * P:(n + 1) * P],
                                    start=n == 0, stop=n == len(blocks) - 1)
                ins.then_inc(sem("a2_o"), 1)

            for l in range(DEPTH):
                n, ns = N_TOK[l], N_SEQ[l]
                hx = rows_of(H, n)
                i = HN_BASE2[l]
                for j in range(8):
                    chunk("q2", l, j, KD, hx, n, normed(mix_norm[l]) if j == 0 else None)
                    if l == 0 and j == 5:
                        head_norm(i, 2048)
                        i += 1
                chunk("k2", l, 0, KD, rows_of(H, 2 * T), 2 * T)
                if l == 0:
                    pe.wait_ge(sem("hn_rms"), i)
                head_norm(i, 2048)
                chunk("k2", l, 1, KD, rows_of(H, 2 * T), 2 * T)
                freed = at["free"]
                w = [tile(2, split=True) for k in range(KD)]
                for tt in range(4):
                    tokens_first("v2", l, tt, w, tt, 2 * P, freed if tt == 0 else 0)
                    if tt == 1:
                        pe.wait_ge(sem("hn_rms"), i + 1)
                        head_norm(i + 1, 1024)
                for j in range(EARLY_HY):
                    fill([("hy2", l, j)])
                    for jj in ROPES_AFTER[j]:
                        if jj == 0:
                            pe.wait_ge(sem("hn_done"), i + 2)
                        rot(ROPE2[l] + jj, C("rot2"), Q2_[:, 2 * jj - 2:2 * jj, 0:T] if jj else K2_[:, :, 0:T])
                pe.wait_ge(sem("rope"), ROPE2[l] + 5)
                steps = IT2[l]
                for k, items in enumerate(att2_fill(l)):
                    i = IT2_BASE[l] + k
                    if k < len(steps):
                        attention2_scores(i, steps[k])
                    fill(items)
                    if LAG <= k < len(steps) + LAG:
                        attention2_turn(i - LAG, steps[k - LAG])
                    if k > LAG:
                        attention2_out(i - LAG - 1, steps[k - LAG - 1])
                pe.wait_ge(sem("a2_out"), IT2_BASE[l] + len(steps))
                gaps = iter(hyena_fill(l))
                fill(next(gaps))
                pe.wait_ge(sem("hconv"), 12 * (l + 1))
                for s in range(ns):
                    for tt in range(NT):
                        for m in range(KH):
                            ins = pe.transpose(ps[:, 2 * s + tt, m * P:(m + 1) * P],
                                               VX[:, m, s * T + tt * P:s * T + (tt + 1) * P], ident)
                ins.then_inc(sem("vt_ready"), 1)
                fill(next(gaps))
                pe.wait_ge(sem("vt_done"), l + 1)
                for s in range(ns):
                    k = 2 * l + s
                    if s:
                        fill(next(gaps))
                        pe.wait_ge(sem("hyena"), k)
                    for ft in range(4):
                        for tt in range(NT):
                            ins = pe.matmul(ps[:, ft, :], C("dft_fwd", tt * N_FFT + ft * P, P), VTK[:, 2 * s + tt, :],
                                            start=tt == 0, stop=tt == NT - 1)
                    ins.then_inc(sem("vf_ready"), 1)
                    fill(next(gaps))
                    pe.wait_ge(sem("y_done"), k + 1)
                    for m in range(KH):
                        for ft in range(4):
                            ins = pe.matmul(ps[:, m // 2, (m % 2) * T:(m % 2 + 1) * T], YFT[:, ft, m * P:(m + 1) * P],
                                            C("idft", ft * T, T), start=ft == 0, stop=ft == 3)
                    ins.then_inc(sem("yi_ready"), 1)
                fill([("oh", l, 0)])
                pe.wait_ge(sem("hyena"), 2 * l + ns)
                fill([("oh", l, i) for i in range(1, 2 * KD)])
                for m in range(KD):
                    chunk("w_out2", l, m, KD, lambda c: MG2[c][:, 0:n], n, joined("oh", l, 2) if m == 0 else None)
                norm(ffn_norm[l])
                for i in range(KF):
                    for half in range(2):
                        chunk("gu", l, 2 * i + half, KD, hx, n, normed(ffn_norm[l]) if i + half == 0 else None)
                    if l == 0 and i in FILTER_2:
                        filter_step(1, FILTER_2.index(i))
                for m in range(KD):
                    chunk("down", l, m, KF, rows_of(AF, n), n, joined("gu", l, 2) if m == 0 else None)
                norm(mix_norm[1] if l == 0 else 7)




def lay_out(inp):
    a = {k: np.asarray(v) for k, v in inp.items()}

    def tiles_of(w):
        return lambda col: [w[k:k + P, col:col + P] for k in range(0, w.shape[0], P)]

    w1, w2 = [tiles_of(w) for w in a["w_in"]], [tiles_of(w) for w in a["w_in_2"]]
    names = {"mod": "w_mod_2", "w_out": "w_out", "w_out2": "w_out_2", "down": "w_down_2", "c_out": "w_conv_out",
             "a_out": "w_attn_out", "d_out": "w_dn_out", "oa": "w_o_attn_2", "oh": "w_o_hyena_2"}
    single1 = {"qk": AQ, "dn": DQ, "cz": CZ, "az": AZ, "dz": DZ}
    single2 = {"q2": Q2, "k2": K2, "hy2": HY2}
    gates1 = {"c_out": GATE + D, "a_out": GATE, "d_out": GATE + 2 * D}
    gates2 = {"oa": G2, "oh": G2 + D}
    rest = {(name, l): tiles_of(a[key][l]) for name, key in names.items() for l in range(DEPTH)}
    gate_up = [tiles_of(w) for w in a["w_gate_up_2"]]

    def chunk_tiles(name, l, i):
        m = i // 2
        if name == "ag":
            return w1[l](GLU + D * (i % 2) + m * P)
        if name in single1:
            return w1[l](single1[name] + i * P)
        if name in single2:
            return w2[l](single2[name] + i * P)
        if name == "v":
            return [] if i % 2 else [t for k in zip(*(w1[l](AV + m * 2 * P + j * P) for j in range(2))) for t in k]
        if name == "mod":
            return [t for k in zip(*(rest[name, l](i * 512 + j * P) for j in range(4))) for t in k]
        if name == "modt":
            return []
        if name == "v2":
            return [] if i else [t for k in zip(*(w2[l](V2 + j * P) for j in range(2))) for t in k]
        if name in gates1:
            return rest[name, l](m * P) if i % 2 else w1[l](gates1[name] + m * P)
        if name in gates2:
            return rest[name, l](m * P) if i % 2 else w2[l](gates2[name] + m * P)
        if name == "gu":
            return gate_up[l](D_FF * (i % 2) + m * P)
        return rest[name, l](i * P)

    w_stream = np.zeros((N_LOADS, P, TILES, P), np.float32)
    at = 0
    for name, l, i in ORDER:
        own = chunk_tiles(name, l, i)
        assert len(own) == n_tiles(name, i)
        for t in own:
            w_stream[at // TILES, :, at % TILES, :] = t
            at += 1

    prm = np.zeros((P, N_PARAM), np.float32)

    def put(name, at, cols):
        cols = np.asarray(cols)
        s = PARAM_AT[name] + at
        prm[:cols.shape[0], s:s + cols.shape[1]] = cols

    by_p = lambda v: v.reshape(-1, P).T
    rows = lambda v: np.broadcast_to(v.reshape(1, -1), (P, v.size))
    for l in range(DEPTH):
        put("norm_w", l * KD, by_p(a["norm_w"][l]))
        put("attn_subln_w", l, by_p(a["attn_subln_w"][l]))
        put("conv_dw_w", l * KD * CONV_K, a["conv_dw_w"][l].reshape(CONV_K, KD, P).transpose(2, 1, 0).reshape(P, -1))
        put("conv_dw_b", l * KD, by_p(a["conv_dw_b"][l]))
        put("conv_ln_w", l * KD, by_p(a["conv_ln_w"][l]))
        put("conv_ln_b", l * KD, by_p(a["conv_ln_b"][l]))
        put("dn_conv_w", l * 24 * SHORT_K, a["dn_conv_w"][l].reshape(SHORT_K, 24, P).transpose(2, 1, 0).reshape(P, -1))
        put("dn_a_log", l * HEADS, rows(a["dn_a_log"][l]))
        put("dn_dt_bias", l * HEADS, rows(a["dn_dt_bias"][l]))
        put("dn_norm_w", l, by_p(a["dn_norm_w"][l]))
        put("lam_qk", l * 4 * QK_DIM, rows(a["lam_qk"][l]))
        put("w_ba", l * KD * 16, a["w_in"][l][:, DB:DB + 16].reshape(KD, P, 16).transpose(1, 0, 2).reshape(P, -1))
        put("b_mod", l * N_MOD * KD, by_p(a["b_mod_2"][l]))
        put("norm_mix", l * KD, by_p(a["norm_mix_2"][l]))
        put("q_norm", l, by_p(a["q_norm_2"][l]))
        put("k_norm", l, by_p(a["k_norm_2"][l]))
        put("conv_w", l * 12 * HY_TAPS, a["conv_w_2"][l].reshape(HY_TAPS, 12, P).transpose(2, 1, 0).reshape(P, -1))
        put("conv_b", l * 12, by_p(a["conv_b_2"][l]))
        for k in (1, 2, 3):
            put(f"filt_w{k}", l * 64, a[f"filt_w{k}_2"][l])
            put("filt_b", 3 * l + k - 1, a[f"filt_b{k}_2"][l][:, None])
            put("filt_freq", 3 * l + k - 1, a["filt_freq_2"][l][k - 1][:, None])
        put("hyena_bias", l * KH, by_p(a["hyena_bias_2"][l]))
        put("norm_ffn", l * KD, by_p(a["norm_ffn_2"][l]))
    put("final_norm_w", 0, by_p(a["final_norm_w"]))
    put("norm_final", 0, by_p(a["norm_final_2"]))
    conds = np.stack([a["c_2"].reshape(-1), a["c_ctx_2"].reshape(-1)], 1)
    put("c", 0, conds.reshape(KD, P, 2).transpose(1, 0, 2).reshape(P, -1))

    made = constants()
    cst = np.zeros((P, N_CONST), np.float32)
    for name, n in CONST_W.items():
        assert made[name].shape == (P, n), (name, made[name].shape)
        cst[:, CONST_AT[name]:CONST_AT[name] + n] = made[name].astype(np.float32)

    turned = lambda x: np.ascontiguousarray(x.reshape(T, KD, P).transpose(2, 1, 0))
    return {
        "w_stream": w_stream.reshape(N_LOADS, P, TILES * P),
        "params": prm,
        "fw4": np.ascontiguousarray(a["filt_w4_2"]),
        "pos": np.ascontiguousarray(np.broadcast_to(a["positions"].reshape(1, T), (P, T))),
        "xT": turned(a["x"]),
        "ctxT": turned(a["ctx_2"]),
        "consts": cst,
    }




def kernel(**inputs):
    import concourse.bacc as _bacc
    from concourse.bass_utils import run_bass_kernel_spmd as _run

    arrays = lay_out(inputs)
    nc = _bacc.Bacc("TRN2", target_bir_lowering=False, num_devices=1, dynamic_dma_scratch_size=1024)
    args = [nc.dram_tensor(f"in_{n}_dram", v.shape, mybir.dt.from_np(v.dtype), kind="ExternalInput").ap()
            for n, v in arrays.items()]
    args.append(nc.dram_tensor("out_0_dram", (P, KD, T), mybir.dt.float32, kind="ExternalOutput").ap())
    build(nc, *args)
    r = _run(nc, [{f"in_{n}_dram": v for n, v in arrays.items()}], core_ids=[0])
    got = r.results[0]["out_0_dram"]
    return np.ascontiguousarray(np.asarray(got).transpose(2, 1, 0)).reshape(1, T, D)
```

```python
import math
import numpy as np
import concourse.bass as bass
from concourse import mybir
from contextlib import ExitStack

P = 128
D = 1024
KD = D // P
T = 256
NT = T // P
DEPTH = 2
HEADS = 8
QK_DIM = 64
CONV_K = 31
SHORT_K = 4
HY = 512
KH = HY // P
HY_TAPS = 3
D_FF = 2816
KF = D_FF // P
N_MOD = 6
N_FFT = 2 * T
NEG = -1.0e30
TWO_PI = 2.0 * math.pi
TILES = 16
RING = 4
HIGHS = 32
PIECE = 8
LEAD = 24

AQ, AK, AV, AZ, GLU, CZ, DQ, DK, DV, DZ, DB, GATE = (
    0, 1024, 2048, 3072, 4096, 6144, 7168, 8192, 9216, 10240, 11264, 11280)
Q2, K2, V2, HY2, G2 = 0, 1024, 1280, 1536, 3072



def constants():
    f = np.float64
    i = np.arange(P)
    c = {}
    c["ident"] = np.eye(P)
    c["ones"] = np.ones((P, P))
    c["until"] = (i[:, None] <= i[None, :]) * 1.0
    c["later"] = np.where(i[:, None] <= i[None, :], 0.0, NEG)
    causal = np.where(i[:, None] >= i[None, :], 0.0, NEG)
    c["causal1"] = np.concatenate([np.zeros((P, P)), causal], 1)
    lv = []
    for s in (1, 2, 4, 8, 16, 32, 64):
        lv.append(((i[:, None] // (2 * s) == i[None, :] // (2 * s))
                   & (i[:, None] % (2 * s) < s) & (i[None, :] % (2 * s) >= s)) * 1.0)
    c["levels"] = np.concatenate(lv, 1)
    rot1 = np.zeros((P, P))
    for d in range(P):
        if d % QK_DIM < QK_DIM // 2:
            rot1[d + QK_DIM // 2, d] = -1.0
        else:
            rot1[d - QK_DIM // 2, d] = 1.0
    c["rot1"] = rot1
    c["tab1"] = np.zeros((P, 2 * T))
    rot2 = np.zeros((P, P))
    for d in range(0, P, 2):
        rot2[d + 1, d] = -1.0
        rot2[d, d + 1] = 1.0
    c["rot2"] = rot2
    t = np.arange(T)
    half = P // 2
    inv2 = (10000.0 ** (-np.arange(0, half, 2, dtype=f) / half)).astype(np.float32)
    ang = np.concatenate([(t // 64)[:, None].astype(np.float32) * inv2,
                          (t % 64)[:, None].astype(np.float32) * inv2], 1).astype(f)
    c["cos2"] = np.repeat(np.cos(ang).T, 2, 0)
    c["sin2"] = np.repeat(np.sin(ang).T, 2, 0)
    inv1 = 10000.0 ** (-np.arange(0, QK_DIM, 2, dtype=f) / QK_DIM)
    c["inv1"] = np.tile(inv1, 4)[:, None]
    tt = np.linspace(0.0, 1.0, T)[:, None]
    w = (TWO_PI / T) * np.arange(T)[:, None]
    fr = np.linspace(1e-4, 15, 16)[None, :]
    z = np.concatenate([tt, np.cos(fr * w), -np.sin(fr * w)], 1)
    c["zT"] = np.concatenate([z.T, np.zeros((P - 33, T))], 0)
    deltas = np.abs(np.linspace(math.log(1e-2) / 1.5, math.log(1e-2) / 0.3, HY))
    dec = np.exp(-tt * deltas)
    rows = lambda a: a.reshape(-1, P, a.shape[1]).transpose(1, 0, 2).reshape(P, -1)
    c["decay"] = rows(dec)
    ph = TWO_PI * np.outer(t, np.arange(T)) / N_FFT
    re, im = np.cos(ph), -np.sin(ph)
    im_n = im.copy()
    im_n[:, 0] = np.cos(math.pi * t)
    c["dft_fwd"] = rows(np.concatenate([re, im_n], 1))
    bre, bim = re.copy(), -im
    bim[:, 0] = np.cos(math.pi * t)
    bre[0], bim[0] = 0.0, 0.0
    c["dft_bwd"] = rows(np.concatenate([bre, bim], 1))
    ire, iim = 2.0 * np.cos(ph.T) / N_FFT, -2.0 * np.sin(ph.T) / N_FFT
    ire[0] *= 0.5
    iim[0] = np.cos(math.pi * t) / N_FFT
    c["idft"] = rows(np.concatenate([ire, iim], 0))
    for name, v in (("eps6", 1e-6), ("eps5", 1e-5), ("half_pi", math.pi / 2)):
        c[name] = np.full((P, 1), v)
    for name, v in (("lam_init", [0.8 - 0.6 * math.exp(-0.3 * l) for l in range(DEPTH)]),):
        c[name] = np.tile(np.array(v)[None], (P, 1))
    return c


CONST_W = {"until": P, "later": P, "causal1": T, "levels": 7 * P, "rot1": P, "tab1": 2 * T,
           "ident": P, "ones": P, "eps6": 1, "eps5": 1, "half_pi": 1, "lam_init": DEPTH, "inv1": 1,
           "rot2": P, "cos2": T, "sin2": T, "zT": T, "dft_fwd": NT * N_FFT, "idft": 4 * T,
           "decay": NT * HY, "dft_bwd": NT * N_FFT}
EARLY = ("ident", "rot2")

PARAM_W = {"norm_w": DEPTH * KD, "attn_subln_w": DEPTH, "conv_dw_w": DEPTH * KD * CONV_K,
           "conv_dw_b": DEPTH * KD, "conv_ln_w": DEPTH * KD, "conv_ln_b": DEPTH * KD,
           "dn_conv_w": DEPTH * 24 * SHORT_K, "dn_a_log": DEPTH * HEADS, "dn_dt_bias": DEPTH * HEADS,
           "dn_norm_w": DEPTH, "final_norm_w": KD, "lam_qk": DEPTH * 4 * QK_DIM, "w_ba": DEPTH * KD * 16,
           "c": KD * 2, "b_mod": DEPTH * N_MOD * KD, "norm_mix": DEPTH * KD, "q_norm": DEPTH, "k_norm": DEPTH,
           "conv_w": DEPTH * 12 * HY_TAPS, "conv_b": DEPTH * 12, "filt_w1": DEPTH * 64, "filt_w2": DEPTH * 64,
           "filt_w3": DEPTH * 64, "filt_b": DEPTH * 3, "filt_freq": DEPTH * 3,
           "hyena_bias": DEPTH * KH, "norm_ffn": DEPTH * KD, "norm_final": KD}


def starts(widths):
    at, out = 0, {}
    for k, n in widths.items():
        out[k] = at
        at += n
    return out, at


CONST_AT, N_CONST = starts(CONST_W)
N_KEPT = CONST_AT["decay"]
PARAM_AT, N_PARAM = starts(PARAM_W)



def spread(items, points):
    return [items[len(items) * k // points:len(items) * (k + 1) // points] for k in range(points)]


LAG = 2
ATT_STEPS = 2 * HEADS
STEPS2 = [2 * 2 * HEADS, 2 * HEADS]
UNITS = HEADS // 2
EARLY_CZ = 4
EARLY_HY = 4

MODS = N_MOD * D // 512
MOD_PLACES = [("gates", 0, 1), ("att", 0, 1), ("delta", 0, 6), ("do", 0, 1), ("norm", 1, 1),
              ("gates", 1, 1), ("att", 1, 1), ("delta", 1, 6), ("do", 1, 1)] + [("norm", i, 1) for i in range(2, 7)]


def mods_by_place():
    out, at = {}, 0
    for place, which, n in MOD_PLACES:
        out[place, which] = [divmod(at + k, MODS) for k in range(n)]
        at += n
    assert at == DEPTH * MODS
    return out


MOD_AT = mods_by_place()
MOD_PARTS = [(0, 3), (3, 5), (5, 6)]


def mods(l, place):
    names = ("mod",) if place == "att" else ("mod", "modt")
    return [(name, *x) for name in names for x in MOD_AT[place, l]]


def norm_mods(i, side):
    rows = [("mod", *x) for x in MOD_AT.get(("norm", i), [])]
    return {"before": [("part", x) for x in rows[:1]] * 2, "after": rows, "turns": [("modt", *x[1:]) for x in rows]}[side]


def att_fill(l):
    return spread([("cz", l, m) for m in range(EARLY_CZ, KD)] + [("c_out", l, i) for i in range(2 * KD)], ATT_STEPS + LAG + 1)


GAPS = [0.8, 5, 0.8] + [1, 1.5] * 5 + [0.6, 2, 0.64, 1, 0.8]
DELTA_POINTS = len(GAPS)


def n_parts(name):
    return {"mod": 4, "modt": 1}.get(name, 2)


def delta_fill(l):
    rows, turns = ([x for x in mods(l, "delta") if x[0] == name] for name in ("mod", "modt"))
    outs = [("az", l, m) for m in range(KD)]
    for m in range(KD):
        outs += [("a_out", l, 2 * m), ("a_out", l, 2 * m + 1), ("dz", l, m)]
    both = []
    for row, turn, out in zip(spread(rows, len(outs)), spread([None] + turns[:-1], len(outs)), outs):
        both += turn + row + [out]
    both = [x for x in both if x] + turns[-1:]
    parts = [("modt", *x) for x in MOD_AT["att", l]]
    for x in both:
        parts += [("part", x)] * (n_parts(x[0]) - 1) + [x]
    gaps = [1.08] + (GAPS * UNITS)[1:]
    out = [[] for _ in gaps]
    at, end = 0, gaps[0]
    for k, x in enumerate(parts):
        while sum(gaps) * (k + 0.5) / len(parts) > end:
            at += 1
            end += gaps[at]
        out[at].append(x)
    return out


def whole(items):
    return [x for x in items if x[0] != "part"]


def att2_fill(l):
    return spread([("hy2", l, j) for j in range(EARLY_HY, 12)], STEPS2[l] + LAG + 1)


FF_PARTS = [2, 1]


def hyena_fill(l):
    return spread([("oa", l, i) for i in range(2 * KD)], 5 if l == 0 else 3)


def chunk_order():
    out = []
    for l in range(DEPTH):
        add = lambda name, a, b: out.extend((name, l, i) for i in range(a, b))
        add("ag", 0, 2)
        if l:
            out += norm_mods(l, "turns")
        add("ag", 2, 16)
        add("qk", 0, 16)
        add("v", 0, 8)
        add("dn", 0, 24)
        add("cz", 0, EARLY_CZ // 2)
        out += mods(l, "gates")
        add("cz", EARLY_CZ // 2, EARLY_CZ)
        out += sum(att_fill(l), []) + mods(l, "att") + whole(sum(delta_fill(l), []))
        add("d_out", 0, 1)
        out += mods(l, "do")
        add("d_out", 1, 16)
        add("w_out", 0, 8)
        out += norm_mods(l + 1, "after")
    for l in range(DEPTH):
        add = lambda name, a, b: out.extend((name, l, i) for i in range(a, b))
        if l == 0:
            out += norm_mods(2, "turns") + norm_mods(3, "after")
        add("k2", 0, 2)
        out += norm_mods(2 * l + 3, "turns")
        add("q2", 0, 8)
        add("v2", 0, 4)
        add("hy2", 0, EARLY_HY)
        out += sum(att2_fill(l), []) + sum(hyena_fill(l), [])
        add("oh", 0, 16)
        add("w_out2", 0, 8)
        out += norm_mods(2 * l + 4, "after")
        add("gu", 0, 2)
        out += norm_mods(2 * l + 4, "turns")
        for half in range(FF_PARTS[l]):
            add("gu", max(2, 2 * KF * half // FF_PARTS[l]), 2 * KF * (half + 1) // FF_PARTS[l])
            add("down", KD * half, KD * (half + 1))
        if l == 0:
            out += norm_mods(5, "after")
    return out


ORDER = chunk_order()
MOD_TURNS = [("modt", l, i) for l in range(DEPTH) for i in range(MODS)]
CHUNK = {x: j for j, x in enumerate(ORDER)}
TAKEN = [x for x in ORDER if x[0] in ("ag", "cz", "c_out", "az", "a_out", "d_out", "w_out", "oa", "oh", "w_out2", "down")
         or (x[0] == "gu" and x[2] % 2)]
TAKE = {x: q for q, x in enumerate(TAKEN)}


def n_tiles(name, l, i):
    if name == "v":
        return 2 * KD if i % 2 == 0 else 0
    if name == "v2":
        return 2 * KD if i == 0 else 0
    if name == "oh" and i % 2:
        return KH
    return {"down": KF // FF_PARTS[l], "mod": 4 * KD, "modt": 0}.get(name, KD)


def is_split(name, l, i):
    if name == "oa" and l == 0:
        return i % 2 == 0
    return name not in ("mod", "modt")


def vector_splits(name, l, i):
    if name == "d_out":
        return i % 2 and i > 1
    return l == DEPTH - 1 and (name in ("w_out2", "down") or (name == "oh" and i >= 3))


def piece_table():
    ends, readers, pieces, stream = [], [], [], []
    t = s = 0
    for j, (name, l, i) in enumerate(ORDER):
        n = n_tiles(name, l, i)
        last = j + {"v": 1, "v2": 3}.get(name, 0)
        stream += [last] * n
        if is_split(name, l, i):
            a = 0
            while a < n:
                m = min(PIECE, n - a, TILES - (t + a) % TILES, HIGHS - (s + a) % HIGHS)
                end = s + a + m - HIGHS
                pieces.append((t + a, m, (s + a) % HIGHS, readers[end - 1] if end > 0 else None, s + a, j))
                a += m
            readers += [last] * n
            s += n
        t += n
        ends.append(s)
    out, j, counts = [], 0, [0, 0]
    for t, m, place, reader, at, own in pieces:
        before = (t // TILES - RING + 1) * TILES
        while at >= ends[j] + LEAD or (reader is not None and reader >= j) or (before > 0 and stream[before - 1] > j - 2):
            j += 1
        assert j <= own
        who = int(vector_splits(*ORDER[own]))
        counts[who] += 1
        out.append((t, m, place, reader, j, who, counts[who]))
    return out


PIECES = piece_table()
PIECE_OF = {piece[0]: piece for piece in PIECES}
N_TILES = sum(n_tiles(name, l, i) for name, l, i in ORDER)
N_LOADS = -(-N_TILES // (TILES * RING)) * RING


def build(nc, w_stream, params, fw4, pos, xT, ctxT, consts, out):
    F32 = mybir.dt.float32
    F32R = mybir.dt.float32r
    I32 = mybir.dt.int32
    ALU = mybir.AluOpType
    ACT = mybir.ActivationFunctionType
    AX = mybir.AxisListType
    MUL, ADD, SUB, MAX = ALU.mult, ALU.add, ALU.subtract, ALU.max
    ctx = ExitStack()
    with ctx:
        START = {}

        def sb(name, *shape, dt=F32):
            START[name] = -(-nc.sbuf_base // 32) * 32
            return ctx.enter_context(nc.sbuf_tensor(name, [P, *shape], dt))

        made = {}

        def sem(name):
            if name not in made:
                made[name] = ctx.enter_context(nc.semaphore(name))
            return made[name]

        def typed(name, other, *shape):
            return nc.alloc_sbuf_tensor_at(name, [P, *shape], F32R, offset=other)

        ring = sb("ring", RING, TILES * P)
        ring_lo = typed("ring_lo", START["ring"], RING, TILES * P)
        ring_hi = sb("ring_hi", HIGHS * P, dt=F32R)
        cst = sb("cst", N_KEPT)
        prm = sb("prm", N_PARAM)
        prm_r = typed("prm_r", START["prm"], N_PARAM)
        WB_HI = sb("wb_hi", PARAM_W["w_ba"], dt=F32R)
        WB_LO = prm_r[:, PARAM_AT["w_ba"]:PARAM_AT["w_ba"] + PARAM_W["w_ba"]]
        X = sb("X", KD, 2 * T)
        XL = typed("XL", START["X"], KD, 2 * T)
        H = sb("H", KD, 2 * T)
        HL = typed("HL", START["H"], KD, 2 * T)
        HH = sb("HH", KD, 2 * T, dt=F32R)
        rstd = sb("rstd", 2 * T)
        take = sb("take", 4, 2 * T)
        hn = sb("hn", 2048)
        at_buf = sb("at_buf", 3072)
        sq = at_buf[:, 1024:3072]
        big = sb("big", 15616)
        big_r = typed("big_r", START["big"], 15616)
        ba = sb("ba", 9, 2 * HEADS)
        at_m = sb("at_m", 2, 2)
        at_l = sb("at_l", 2, 2)
        lam = sb("lam", 8)
        mod = sb("mod", DEPTH, N_MOD * KD, 2)
        mod_rows = sb("mod_rows", 2, 512)
        gains = sb("gains", 2, KD, 2)
        sc = sb("sc", KD, 2)

        def cut(buf, at, *shape):
            n = 1
            for s in shape:
                n *= s
            v = buf[:, at:at + n]
            if len(shape) == 2:
                v = v.rearrange("p (a b) -> p a b", a=shape[0])
            if len(shape) == 3:
                v = v.rearrange("p (a b c) -> p a b c", a=shape[0], b=shape[1])
            return v

        pg = ctx.enter_context(nc.psum_tensor("pg", [P, 4, 512], F32))
        ps = ctx.enter_context(nc.psum_tensor("ps", [P, 4, 512], F32))
        ps_flat = ps[:, :, :].rearrange("p a b -> p (a b)")

        def C(name, at=0, n=None):
            a = CONST_AT[name] + at
            return cst[:, a:a + (n or CONST_W[name])]

        DECAY, DFT_BWD = hn[:, 0:NT * HY], hn[:, NT * HY:NT * (HY + N_FFT)]

        def PR(name, at=0, n=1):
            a = PARAM_AT[name] + at
            return prm[:, a:a + n]

        ident, ones, eps6, eps5 = C("ident"), C("ones"), C("eps6"), C("eps5")

        tab = C("tab1").rearrange("p (a b) -> p a b", a=2)
        assert CONST_AT["ident"] >= 4 * HY

        def rep(ap, n):
            return ap.unsqueeze(1).broadcast_to([P, n, ap.shape[1]])

        def wide(ap, n):
            return ap.unsqueeze(2).broadcast_to([P, ap.shape[1], n])

        QK = cut(big, 0, 16, T)
        V = cut(big, 4096, NT, D)
        U = cut(big, 6144, KD, CONV_K - 1 + T)
        DN = cut(big, 8432, 24, T)
        raw = cut(big, 14576, 4, SHORT_K - 1 + T)
        CV = X[:, :, T:2 * T]
        MG = H[:, :, T:2 * T]
        AT_S = cut(at_buf, 0, 2, 2 * T)
        AT_A = cut(at_buf, 1024, 2, 2 * T)
        AT_T = cut(at_buf, 2048, 2, 2 * T)
        CVH, CVL = HH[:, :, T:2 * T], XL[:, :, T:2 * T]
        AOH, AOL = HH[:, :, T:2 * T], cut(big_r, 0, 16, T)
        MGH, MGL = HH[:, :, T:2 * T], HL[:, :, T:2 * T]
        DNH = cut(big_r, 2048, KD, T)
        DNL = cut(big_r, 8432, 24, T)
        RT = cut(at_buf, 0, 2, 2 * T)
        PAIRS = 4 * P
        DT, LT, IN, LM0, LM1, TT, TM, XS = (cut(big, 2048 + j * PAIRS, PAIRS) for j in range(8))
        VB, UG, IB, VN = (cut(big, 6144 + j * PAIRS, PAIRS) for j in range(4))
        LM = [LM0, LM1]
        KBG, KDEC, NW, S1, QG, EXR = (cut(at_buf, j * 2 * P, 2, P) for j in range(6))
        BETA, G, GC, NGC, BEG, B0, B1, B2 = (ba[:, j, :].rearrange("p (c h) -> p c h", c=NT) for j in range(8))
        EXA = ba[:, 8, 0:HEADS]
        QK_S = QK_DIM ** -0.5
        DN_S = P ** -0.5

        N_TOK = [2 * T, T]
        Q2_ = cut(big, 0, HEADS, 2 * T)
        K2_ = cut(big, 4096, 2, 2 * T)
        V2_ = cut(big, 5120, 4, 2 * P)
        X0 = cut(big, 6144, KH, 2 * T)
        X1 = cut(big, 8192, KH, 2 * T)
        VX = cut(big, 10240, KH, 2 * T)
        hraw = cut(big, 12288, 4, T + 2)
        A2H, A2L = (cut(big_r, 0, HEADS, 2 * T)[:, :, s] for s in (slice(T, 2 * T), slice(0, T)))
        X0L, X0H = cut(big_r, 6144, KH, 2 * T), cut(big_r, 10240, KH, 2 * T)
        X0P = cut(at_buf, 0, KH, T)
        VTK = cut(big, 13320, 4, HY)
        AF, AFL, AFH = ([cut(b, at, KF // FF_PARTS[l], N_TOK[l]) for l in range(DEPTH)]
                        for b, at in ((big, 0), (big_r, 0), (big_r, KF * T)))
        MG2 = [cut(big, at, KH, 2 * T)[:, m, :] for at in (4096, 8192) for m in range(KH)]
        MG2L = [cut(big_r, at, KH, 2 * T)[:, m, :] for at in (4096, 8192) for m in range(KH)]
        MG2H = cut(big_r, 0, KD, 2 * T)
        W4 = cut(at_buf, 0, 2 * HY)
        HQ = cut(at_buf, 1024, T)
        RR = cut(at_buf, 1280, 3, T)
        KFT = cut(cst, 0, 4, HY)
        PROD = cut(at_buf, 0, 2, HY)
        VFT = hn[:, :].rearrange("p (a b) -> p a b", a=4)
        YFT = sq.rearrange("p (a b) -> p a b", a=4)
        ANGI = cut(at_buf, 0, T).bitcast(I32)
        POSF = cut(at_buf, 256, T)

        N_SEQ = [2, 1]
        N_NORM = [T, T, T, 2 * T, 2 * T, 2 * T, T, T]
        LOW_READY = ["low_ready", "low_ready_dve"]
        SPLIT_NORMS = [0, 1, 3, 4, 5, 6]
        NORM_USER = {1: ("ag", 1, 0), 3: ("k2", 0, 0), 4: ("gu", 0, 0), 5: ("k2", 1, 0), 6: ("gu", 1, 0)}
        mix_norm = [3, 5]
        ffn_norm = [4, 6]
        HN_BASE1 = lambda l: 4 * l
        HN_BASE2 = [8, 11]
        ROPE2 = [16, 21]
        IT2 = [[(h, s, b) for h in range(HEADS) for s in range(n) for b in range(NT)] for n in N_SEQ]
        IT2_BASE = [0, len(IT2[0])]
        HIGH_AT = [NT * h + NT + LAG + 1 for h in range(HEADS - 1)]
        DQ_N, DK_N, ATT_N, DO_N = range(4)
        DN_EARLY = 3
        ROPE_AT = [3, 4, 5, 7, 8, 9, 10, 11]
        ROPES_AFTER = [[0], [1, 2], [3, 4], []]
        FILTER_1 = [0, 4, 8, 12, 14]
        FILTER_2 = [0, 1, 2, 3, 4]

        def by_log(i):
            return i < HN_BASE2[0] and i % 4 >= ATT_N

        def x_done(i, m=KD - 1):
            name, l = {1: ("w_out", 0), 2: ("w_out", 1), 4: ("w_out2", 0), 5: ("down", 0), 6: ("w_out2", 1), 7: ("down", 1)}[i]
            return TAKE[name, l, m + (KD * (FF_PARTS[l] - 1) if name == "down" else 0)] + 1

        early = slice(CONST_AT[EARLY[0]], CONST_AT[EARLY[1]])

        block = ctx.enter_context(nc.Block())

        @block.sync
        def _(sp):
            sp.dma_start(X[:, :, 0:T], xT).then_inc(sem("x_loaded"), 16)
            sp.dma_start(cst[:, early], consts[:, early]).then_inc(sem("first_tables"), 16)
            sp.dma_start(prm[:, :], params).then_inc(sem("loaded"), 16)
            sp.dma_start(ANGI, pos).then_inc(sem("loaded"), 16)
            for s in range(RING):
                sp.dma_start(ring[:, s, :], w_stream[s]).then_inc(sem(f"weights{s}"), 16)
            first, after = slice(0, CONST_AT["tab1"]), slice(early.stop, N_KEPT)
            sp.dma_start(cst[:, first], consts[:, first]).then_inc(sem("tables"), 16)
            sp.dma_start(cst[:, after], consts[:, after]).then_inc(sem("tables"), 16)
            with sp.Fori(1, N_LOADS // RING) as r:
                for s in range(RING):
                    sp.wait_ge(sem("slot_free"), (r - 1) * RING + (s + 1))
                    sp.dma_start(ring[:, s, :], w_stream[bass.ds(r * RING + s, 1), :, :].rearrange("o p n -> p (o n)"))\
                        .then_inc(sem(f"weights{s}"), 16)
            for s in range(RING):
                sp.wait_ge(sem(f"weights{s}"), 16 * (N_LOADS // RING))

        @block.gpsimd
        def _(pool):
            links = [0]

            def link(ins):
                links[0] += 1
                ins.then_inc(sem("pool_link"), 1)
                pool.wait_ge(sem("pool_link"), links[0])

            def taken(name, l, i):
                return TAKE[name, l, i] % 4

            split = [0]

            def ahead(j):
                while split[0] < len(PIECES) and PIECES[split[0]][4] <= j:
                    t, n, place, reader, step, who, count = PIECES[split[0]]
                    split[0] += 1
                    if who:
                        continue
                    cols = slice(t % TILES * P, (t % TILES + n) * P)
                    slot = t // TILES % RING
                    pool.wait_ge(sem("high_ready"), split[0])
                    pool.tensor_tensor(ring_lo[:, slot, cols], ring[:, slot, cols],
                                       ring_hi[:, place * P:(place + n) * P].bitcast(F32), SUB).then_inc(sem(LOW_READY[0]), 1)

            def drained(name, l, i):
                ahead(CHUNK[name, l, i])
                pool.wait_ge(sem("drained"), CHUNK[name, l, i] + 1)

            def zero_conv_pad():
                pool.memset(U[:, :, 0:CONV_K - 1], 0.0).then_inc(sem("conv_pad"), 1)

            def conv_gate(l):
                for m in range(KD):
                    a, g = taken("ag", l, 2 * m), taken("ag", l, 2 * m + 1)
                    drained("ag", l, 2 * m + 1)
                    pool.tensor_tensor(U[:, m, CONV_K - 1:], take[:, a, 0:T], take[:, g, 0:T], MUL)\
                        .then_inc(sem("take_used"), 2)

            def times_z(name, l, m, branch, high, low):
                drained(name, l, m)
                z = take[:, taken(name, l, m), 0:T]
                pool.tensor_tensor(high[:, m, :], branch[:, m, :], z, MUL)
                link(pool.tensor_tensor(branch[:, m, :], branch[:, m, :], z, MUL))
                pool.tensor_tensor(low[:, m, :], branch[:, m, :], high[:, m, :].bitcast(F32), SUB).then_inc(sem("take_used"), 1)

            def merge(name, l, m, first):
                g, y = taken(name, l, 2 * m), taken(name, l, 2 * m + 1)
                drained(name, l, 2 * m + 1)
                if first:
                    pool.tensor_tensor(MG[:, m, :], take[:, g, 0:T], take[:, y, 0:T], MUL).then_inc(sem("take_used"), 2)
                else:
                    link(pool.tensor_tensor(take[:, y, 0:T], take[:, g, 0:T], take[:, y, 0:T], MUL))
                    pool.tensor_tensor(MG[:, m, :], MG[:, m, :], take[:, y, 0:T], ADD).then_inc(sem("take_used"), 2)

            def add_to_x(name, l, n, first=0):
                for m in range(KD):
                    drained(name, l, first + m)
                    pool.tensor_tensor(X[:, m, 0:n], X[:, m, 0:n], take[:, taken(name, l, first + m), 0:n], ADD)\
                        .then_inc(sem("take_used"), 1)

            pool.memset(raw[:, :, 0:SHORT_K - 1], 0.0).then_inc(sem("raw_pad"), 1)
            for l in range(DEPTH):
                if l:
                    pool.wait_ge(sem("take_used"), x_done(l))
                zero_conv_pad()
                conv_gate(l)
                for m in range(KD):
                    times_z("cz", l, m, CV, CVH, CVL)
                for m in range(KD):
                    merge("c_out", l, m, True)
                ahead(CHUNK["az", l, 2])
                pool.wait_ge(sem("hn_done"), HN_BASE1(l) + ATT_N + 1)
                for m in range(KD):
                    times_z("az", l, m, QK, AOH, AOL)
                for m in range(KD):
                    merge("a_out", l, m, False)
                for m in range(KD):
                    merge("d_out", l, m, False)
                add_to_x("w_out", l, T)
            pool.wait_ge(sem("norm_h"), 3 * KD)
            pool.memset(hraw[:, :, 0:1], 0.0)
            pool.memset(hraw[:, :, T + 1:T + 2], 0.0).then_inc(sem("hraw_pad"), 1)
            for l in range(DEPTH):
                n = N_TOK[l]
                for h in range(HEADS if l == DEPTH - 1 else 0):
                    done = sum(att2_fill(l)[:(HIGH_AT + [ATT_STEPS + LAG])[h] + 1], [])
                    if done:
                        ahead(CHUNK[done[-1]])
                    pool.wait_ge(sem("a2_high"), h + 1)
                    pool.tensor_tensor(A2L[:, h, :], Q2_[:, h, 0:T], A2H[:, h, :].bitcast(F32), SUB).then_inc(sem("a2_low"), 1)
                for m in range(KD):
                    g, y = taken("oa", l, 2 * m), taken("oa", l, 2 * m + 1)
                    drained("oa", l, 2 * m + 1)
                    pool.tensor_tensor(MG2[m][:, 0:n], take[:, g, 0:n], take[:, y, 0:n], MUL).then_inc(sem("take_used"), 2)
                for m in range(KD):
                    g, y = taken("oh", l, 2 * m), taken("oh", l, 2 * m + 1)
                    drained("oh", l, 2 * m + 1)
                    link(pool.tensor_tensor(take[:, y, 0:n], take[:, g, 0:n], take[:, y, 0:n], MUL))
                    pool.tensor_tensor(MG2[m][:, 0:n], MG2[m][:, 0:n], take[:, y, 0:n], ADD).then_inc(sem("take_used"), 2)
                add_to_x("w_out2", l, n)
                per = KF // FF_PARTS[l]
                for part in range(FF_PARTS[l]):
                    for i in range(per):
                        j = 2 * (part * per + i) + 1
                        drained("gu", l, j)
                        pool.tensor_tensor(AF[l][:, i, :], AF[l][:, i, :], take[:, taken("gu", l, j), 0:n], MUL)\
                            .then_inc(sem("take_used"), 1)
                    add_to_x("down", l, n, KD * part)

        @block.scalar
        def _(act):
            split = [0]

            def ahead(j):
                while split[0] < len(PIECES) and PIECES[split[0]][4] <= j:
                    t, n, place, reader, step, who, count = PIECES[split[0]]
                    split[0] += 1
                    cols = slice(t % TILES * P, (t % TILES + n) * P)
                    slot = t // TILES % RING
                    act.wait_ge(sem(f"weights{slot}"), 16 * (t // TILES // RING + 1))
                    if reader is not None:
                        act.wait_ge(sem("chunk_ready"), reader + 1)
                    act.activation(ring_hi[:, place * P:(place + n) * P], ring[:, slot, cols], ACT.Copy)\
                        .then_inc(sem("high_ready"), 1)

            def ready(j):
                ahead(j)
                act.wait_ge(sem("chunk_ready"), j + 1)
                return pg[:, j % 4, :]

            def drain(j, dst, func=ACT.Copy, n=T):
                act.activation(dst, ready(j)[:, 0:n], func).then_inc(sem("drained"), 1)

            def to_take(name, l, i, func=ACT.Copy, n=T):
                q = TAKE[name, l, i]
                ahead(CHUNK[name, l, i])
                if q >= 4:
                    act.wait_ge(sem("take_used"), q - 3)
                drain(CHUNK[name, l, i], take[:, q % 4, 0:n], func, n)

            def drain_fill(items):
                for name, l, i in items:
                    if name == "mod":
                        k = MODS * l + i
                        if k >= 2:
                            act.wait_ge(sem("drained"), CHUNK[MOD_TURNS[k - 2]] + 1)
                        act.activation(mod_rows[0:2, i % 2, :], ready(CHUNK[name, l, i])[0:2, :], ACT.Copy).then_inc(sem("drained"), 1)
                    elif name == "modt":
                        drain(CHUNK[name, l, i], mod[:, l, 4 * i:4 * i + 4, :].rearrange("p a b -> p (a b)"), n=8)
                    elif name == "dz":
                        drain(CHUNK[name, l, i], CV[:, i, :], ACT.Silu)
                    elif name in ("cz", "az"):
                        to_take(name, l, i, ACT.Silu)
                    elif name == "hy2":
                        hyena_in(l, i)
                    else:
                        to_take(name, l, i, ACT.Copy if i % 2 else ACT.Sigmoid, N_TOK[l] if name in ("oa", "oh") else T)

            def hyena_in(l, j):
                n, ns = N_TOK[l], N_SEQ[l]
                ahead(CHUNK["hy2", l, j])
                if 12 * l + j >= 2:
                    act.wait_ge(sem("hconv"), 12 * l + j - 1)
                s0 = (j % 2) * 2
                act.activation(hraw[:, s0:s0 + ns, 1:T + 1],
                               ready(CHUNK["hy2", l, j])[:, 0:n].rearrange("p (s t) -> p s t", s=ns), ACT.Copy)\
                    .then_inc(sem("drained"), 1)

            roots = [0]

            def inverse_root(dst, sums, eps, scale, done):
                roots[0] += 1
                act.activation(dst, sums, ACT.Ln, bias=eps, scale=scale).then_inc(sem("log_root"), 1)
                act.wait_ge(sem("log_root"), roots[0])
                act.activation(dst, dst, ACT.Exp, scale=-0.5).then_inc(sem(done), 1)

            def norm_square(i, m):
                n = N_NORM[i]
                if i == 0 and m == 0:
                    act.wait_ge(sem("x_loaded"), 16)
                if i == 3:
                    act.wait_ge(sem("norm_h"), 2 * KD + m + 1)
                    act.wait_ge(sem("ctx_loaded"), 16)
                elif i:
                    act.wait_ge(sem("take_used"), x_done(i, m))
                act.activation(H[:, m, 0:n], X[:, m, 0:n], ACT.Square).then_inc(sem("norm_sq"), 1)

            def norm_root(i):
                n = N_NORM[i]
                act.wait_ge(sem("norm_ss"), i + 1)
                act.activation(rstd[:, 0:n], ps[:, 0, 0:n], ACT.Sqrt, bias=eps6, scale=1.0 / D)\
                    .then_inc(sem("norm_rms"), 1)
                if i in NORM_USER:
                    ahead(CHUNK[NORM_USER[i]])

            def updates(i, put):
                for m in range(KD + 2):
                    if m < KD:
                        put(m)
                    if m >= 2:
                        norm_square(i, m - 2)
                norm_root(i)

            def modulate(i, l, which):
                n = N_NORM[i]
                act.wait_ge(sem("mod_done"), len(MOD_PARTS) * l + which + 1)
                for k in range(KD + 1):
                    if k == KD // 2:
                        drain_fill(norm_mods(i, "after"))
                    if k < KD:
                        act.wait_ge(sem("normed"), KD * (i - 3) + k + 1)
                        for s in range(n // T):
                            ins = act.activation(H[:, k, s * T:(s + 1) * T], H[:, k, s * T:(s + 1) * T], ACT.Identity,
                                                 bias=mod[:, l, 3 * which * KD + k, s:s + 1], scale=gains[:, which, k, s:s + 1])
                        ins.then_inc(sem("h_whole"), 1)
                    if k:
                        high_part(i, k - 1)

            def high_part(i, k):
                act.wait_ge(sem("h_whole"), KD * SPLIT_NORMS.index(i) + k + 1)
                act.activation(HH[:, k, 0:N_NORM[i]], H[:, k, 0:N_NORM[i]], ACT.Copy).then_inc(sem("h_high"), 1)

            def hn_square(src):
                a, b = src.shape[1], src.shape[2]
                act.activation(sq[:, 0:a * b].rearrange("p (a b) -> p a b", a=a), src, ACT.Square)\
                    .then_inc(sem("hn_sq"), 1)

            def hn_root(i, cols, scale):
                act.wait_ge(sem("hn_ss"), i + 1)
                if i >= 1:
                    act.wait_ge(sem("hn_done"), i)
                if by_log(i):
                    inverse_root(hn[:, 0:cols], ps_flat[:, 0:cols], eps6, scale, "hn_rms")
                else:
                    act.activation(hn[:, 0:cols], ps_flat[:, 0:cols], ACT.Sqrt, bias=eps6, scale=scale).then_inc(sem("hn_rms"), 1)

            def filter_sin(l, k):
                act.wait_ge(sem("f_arg"), 3 * l + k + 1)
                act.activation(HQ[0:64, :], RR[0:64, 0, :], ACT.Sin).then_inc(sem("f_sin"), 1)

            def filter_spectrum(l):
                act.wait_ge(sem("kf_ready"), l + 1)
                act.activation(KFT, ps[:, :, :], ACT.Copy).then_inc(sem("kf_done"), 1)

            def attention_exp(l, it):
                i = 2 * HEADS * l + it
                e = P * (it % 2 + 1)
                act.wait_ge(sem("att_max"), i + 1)
                for m in range(2):
                    ins = act.activation(AT_S[:, i % 2, m * T:m * T + e], AT_S[:, i % 2, m * T:m * T + e], ACT.Exp,
                                         bias=at_m[:, i % 2, m:m + 1], accum_out=at_l[:, i % 2, m:m + 1])
                ins.then_inc(sem("att_exp"), 1)

            def attention_turned(l, it):
                i = 2 * HEADS * l + it
                e = P * (it % 2 + 1)
                act.wait_ge(sem("att_turn"), i + 1)
                if i >= 2:
                    act.wait_ge(sem("att_o"), i - 1)
                act.activation(AT_T[:, i % 2, 0:e], ps[:, 2, 0:e], ACT.Copy).then_inc(sem("att_turned"), 1)

            def delta_gates(l):
                drain_fill([("cz", l, 0)])
                act.wait_ge(sem("ba_ready"), l + 1)
                both = ps[:, 0, 0:32].rearrange("p (c n) -> p c n", c=NT)
                act.activation(BETA, both[:, :, 0:HEADS], ACT.Sigmoid).then_inc(sem("beta"), 1)
                act.activation(EXA, PR("dn_a_log", l * HEADS, HEADS), ACT.Exp).then_inc(sem("exp_a"), 1)
                act.wait_ge(sem("abs_a"), l + 1)
                act.activation(B1, B1, ACT.Exp, scale=-1.0).then_inc(sem("exp_abs"), 1)
                act.wait_ge(sem("exp_abs"), l + 1)
                act.activation(B2, B1, ACT.Ln, bias=1.0).then_inc(sem("ln_abs"), 1)
                drain_fill([("cz", l, m) for m in range(1, EARLY_CZ // 2)])
                drain_fill(mods(l, "gates"))
                act.wait_ge(sem("gc_ready"), l + 1)
                act.activation(BEG, ps[:, 1, 0:16].rearrange("p (c h) -> p c h", c=NT), ACT.Exp)\
                    .then_inc(sem("exp_gc"), 1)
                drain_fill([("cz", l, m) for m in range(EARLY_CZ // 2, EARLY_CZ)])

            def delta(l, u):
                i = 4 * l + u
                gaps = iter(delta_fill(l)[u * DELTA_POINTS:(u + 1) * DELTA_POINTS])

                def fill():
                    drain_fill(whole(next(gaps)))

                sums = ps[:, 0, :].rearrange("p (h c n) -> p h c n", h=2, c=NT)
                fill()
                act.wait_ge(sem("d_dt"), i + 1)
                act.activation(EXR, sums[:, :, 1, :], ACT.Exp)
                for p in range(4):
                    h, c = 2 * u + p // 2, p % 2
                    ins = act.activation(DT[:, p * P:(p + 1) * P], DT[:, p * P:(p + 1) * P], ACT.Exp,
                                         bias=NGC[:, c, h:h + 1])
                ins.then_inc(sem("d_exp"), 1)
                fill()
                act.wait_ge(sem("d_t0"), i + 1)
                act.activation(TM, ps[:, 0, :], ACT.Copy).then_inc(sem("d_tm"), 1)
                for s in range(1, 7):
                    fill()
                    act.wait_ge(sem("d_x"), 6 * i + s)
                    act.activation(XS, ps[:, 1, :], ACT.Copy).then_inc(sem("d_xs"), 1)
                    fill()
                fill()
                act.wait_ge(sem("d_w"), i + 1)
                act.activation(NW, ps[:, 2, 0:2 * P].rearrange("p (a b) -> p a b", a=2), ACT.Copy, scale=-1.0)
                act.activation(VN[:, 0:2 * P], ps[:, 2, 2 * P:4 * P], ACT.Copy).then_inc(sem("d_vn0"), 1)
                fill()
                act.wait_ge(sem("d_s"), i + 1)
                act.activation(S1, ps[:, 3, 0:2 * P].rearrange("p (a b) -> p a b", a=2), ACT.Copy).then_inc(sem("d_s1"), 1)
                fill()
                act.wait_ge(sem("d_v1"), i + 1)
                act.activation(VN[:, 2 * P:4 * P], ps[:, 0, 0:2 * P], ACT.Copy).then_inc(sem("d_vn1"), 1)
                fill()
                act.wait_ge(sem("d_o"), i + 1)
                act.activation(DN[:, 2 * u:2 * u + 2, :], ps[:, 1, :].rearrange("p (a b) -> p a b", a=2), ACT.Copy).then_inc(sem("d_out"), 1)

            for m in range(KD):
                norm_square(0, m)
            act.wait_ge(sem("first_tables"), 16)
            norm_root(0)
            ahead(0)
            for k in range(KD):
                high_part(0, k)
            act.wait_ge(sem("loaded"), 32)
            act.activation(WB_HI[:, :], PR("w_ba", 0, PARAM_W["w_ba"]), ACT.Copy).then_inc(sem("wb_high"), 1)
            act.activation(sc[:, :, :], PR("c", 0, 2 * KD), ACT.Silu).then_inc(sem("silu_c"), 1)
            for l in range(DEPTH):
                for m in range(KD):
                    to_take("ag", l, 2 * m)
                    to_take("ag", l, 2 * m + 1, ACT.Sigmoid)
                    if l and m == 0:
                        drain_fill(norm_mods(l, "turns"))
                    if l == 0 and m == 1:
                        act.wait_ge(sem("ang"), 1)
                        act.activation(tab[:, 1, :], POSF, ACT.Sin)
                        act.wait_ge(sem("ang"), 2)
                        act.activation(tab[:, 0, :], RR[:, 0, :], ACT.Sin).then_inc(sem("rope_table"), 1)
                        act.wait_ge(sem("lam_dots"), 1)
                        act.activation(lam[:, 0:4], lam[:, 0:4], ACT.Exp).then_inc(sem("lam_exp"), 1)
                for j in range(16):
                    drain(CHUNK["qk", l, j], QK[:, j, :])
                for j in range(8):
                    drain(CHUNK["v", l, j], V[:, j % 2, (j // 2) * T:(j // 2 + 1) * T])
                def dn_silu(j):
                    act.wait_ge(sem("sconv"), 24 * l + j + 1)
                    act.activation(DN[:, j, :], DN[:, j, :], ACT.Silu).then_inc(sem("dn_silu"), 1)

                for j in range(24):
                    if 24 * l + j >= 4:
                        act.wait_ge(sem("sconv"), 24 * l + j - 3)
                    if l == 0 and j == 0:
                        act.wait_ge(sem("raw_pad"), 1)
                    drain(CHUNK["dn", l, j], raw[:, j % 4, SHORT_K - 1:])
                    if j == DN_EARLY - 1:
                        act.wait_ge(sem("ln_centered"), l + 1)
                        act.activation(sq.rearrange("p (a b) -> p a b", a=KD), CV, ACT.Square).then_inc(sem("ln_sq"), 1)
                    if j >= 2:
                        dn_silu(j - 2)
                    if j == DN_EARLY:
                        act.wait_ge(sem("ln_ss"), l + 1)
                        act.activation(rstd[:, 0:T], ps[:, 1, 0:T], ACT.Sqrt, bias=eps5, scale=1.0 / D).then_inc(sem("ln_rms"), 1)
                    if j == 7:
                        act.wait_ge(sem("ln_normed"), l + 1)
                        for m in range(KD):
                            act.activation(CV[:, m, :], CV[:, m, :], ACT.Silu, bias=PR("conv_ln_b", l * KD + m),
                                           scale=PR("conv_ln_w", l * KD + m)).then_inc(sem("ln_silu"), 1)
                    if j == 9:
                        act.wait_ge(sem("dn_silu"), 24 * l + 8)
                        hn_square(DN[:, 0:8, :])
                    if j == 13:
                        hn_root(HN_BASE1(l) + DQ_N, 2048, 1.0)
                    if j == 17:
                        act.wait_ge(sem("dn_silu"), 24 * l + 16)
                        hn_square(DN[:, 8:16, :])
                    if j == 21:
                        hn_root(HN_BASE1(l) + DK_N, 2048, 1.0)
                dn_silu(22)
                dn_silu(23)
                act.wait_ge(sem("ln_silu"), KD * (l + 1))
                delta_gates(l)
                for it, items in enumerate(att_fill(l)):
                    if it < ATT_STEPS:
                        attention_exp(l, it)
                    drain_fill(items)
                    if LAG <= it < ATT_STEPS + LAG:
                        attention_turned(l, it - LAG)
                act.wait_ge(sem("att_out"), 16 * (l + 1))
                hn_square(QK[:, 0:8, :])
                hn_root(HN_BASE1(l) + ATT_N, 2048, 1.0 / P)
                drain_fill(mods(l, "att"))
                for u in range(UNITS):
                    delta(l, u)
                act.wait_ge(sem("d_out"), 4 * (l + 1))
                if l == DEPTH - 1:
                    act.dma_start(W4[0:64, :], fw4[0]).then_inc(sem("w4_loaded"), 16)
                hn_square(DN[:, 0:8, :])
                hn_root(HN_BASE1(l) + DO_N, 2048, 1.0 / P)
                drain_fill([("d_out", l, 0)])
                drain_fill(mods(l, "do"))
                for m in range(KD):
                    act.wait_ge(sem("dn_whole"), KD * l + m + 1)
                    act.activation(DNH[:, m, :], DN[:, m, :], ACT.Copy).then_inc(sem("dn_high"), 1)
                if l == DEPTH - 1:
                    act.wait_ge(sem("hn_done"), HN_BASE1(l) + DO_N + 1)
                    act.dma_start(hn[:, :], consts[:, N_KEPT:]).then_inc(sem("filter_tables"), 16)
                def merged_high(m):
                    act.wait_ge(sem("take_used"), TAKE["d_out", l, 2 * m + 1] + 1)
                    act.activation(MGH[:, m, :], MG[:, m, :], ACT.Copy).then_inc(sem("mg_high"), 1)

                for i in range(2 * KD):
                    if i:
                        drain_fill([("d_out", l, i)])
                    if i % 2 and i > 1:
                        merged_high(i // 2 - 1)
                    if l == DEPTH - 1 and i + 1 in FILTER_1[1:4]:
                        filter_sin(0, FILTER_1.index(i + 1) - 1)
                    if l == DEPTH - 1 and i == FILTER_1[4] + 1:
                        act.dma_start(X[:, :, T:2 * T], ctxT).then_inc(sem("ctx_loaded"), 16)
                        filter_spectrum(0)
                merged_high(KD - 1)
                updates(l + 1, lambda m: to_take("w_out", l, m))
                if l == 0:
                    for k in range(KD):
                        if k == KD // 2:
                            drain_fill(norm_mods(1, "after"))
                        high_part(1, k)
            drain_fill(norm_mods(2, "after"))
            for m in range(KD):
                norm_square(3, m)
            drain_fill(norm_mods(2, "turns"))
            norm_root(3)

            def attention2_exp(i, s):
                n = 2 * T if s == 0 else T
                act.wait_ge(sem("a2_max"), i + 1)
                act.activation(AT_S[:, i % 2, 0:n], ps[:, i % 2, 0:n], ACT.Exp, bias=at_m[:, i % 2, 0:1],
                               scale=P ** -0.5, accum_out=at_l[:, i % 2, 0:1]).then_inc(sem("a2_exp"), 1)

            def attention2_turned(i, s):
                n = 2 * T if s == 0 else T
                act.wait_ge(sem("a2_turn"), i + 1)
                if i >= 2:
                    act.wait_ge(sem("a2_o"), i - 1)
                act.activation(AT_T[:, i % 2, 0:n], ps[:, 2, 0:n], ACT.Copy).then_inc(sem("a2_turned"), 1)

            def attention2_high(h):
                act.wait_ge(sem("a2_out"), IT2_BASE[DEPTH - 1] + NT * (h + 1))
                act.activation(A2H[:, h, :], Q2_[:, h, 0:T], ACT.Copy).then_inc(sem("a2_high"), 1)

            def gated(name, l, i, m, which):
                q = TAKE[name, l, i]
                ahead(CHUNK[name, l, i])
                act.wait_ge(sem("take_used"), q - 3)
                src = ready(CHUNK[name, l, i])
                for s in range(N_SEQ[l]):
                    ins = act.activation(take[:, q % 4, s * T:(s + 1) * T], src[:, s * T:(s + 1) * T], ACT.Copy,
                                         scale=mod[:, l, which * KD + m, s:s + 1])
                ins.then_inc(sem("drained"), 1)

            for l in range(DEPTH):
                n, ns = N_TOK[l], N_SEQ[l]
                modulate(mix_norm[l], l, 0)
                i = HN_BASE2[l]
                for j in range(2):
                    drain(CHUNK["k2", l, j], K2_[:, j, :], n=2 * T)
                drain_fill(norm_mods(mix_norm[l], "turns"))
                act.wait_ge(sem("drained"), CHUNK["k2", l, 1] + 1)
                hn_square(K2_)
                for j in range(8):
                    drain(CHUNK["q2", l, j], Q2_[:, j, 0:n], n=n)
                    if j == 1:
                        hn_root(i, 1024, 1.0 / P)
                    if j in (3, 7):
                        act.wait_ge(sem("drained"), CHUNK["q2", l, j] + 1)
                        hn_square(Q2_[:, j - 3:j + 1, 0:n])
                    if j == 5:
                        hn_root(i + 1, 4 * n, 1.0 / P)
                for j in range(4):
                    drain(CHUNK["v2", l, j], V2_[:, j, :], n=2 * P)
                    if j == 1:
                        hn_root(i + 2, 4 * n, 1.0 / P)
                if l == 0:
                    act.wait_ge(sem("hraw_pad"), 1)
                drain_fill([("hy2", l, j) for j in range(EARLY_HY)])
                steps = IT2[l]
                for k, items in enumerate(att2_fill(l)):
                    if k < len(steps):
                        attention2_exp(IT2_BASE[l] + k, steps[k][1])
                    drain_fill(items)
                    if LAG <= k < len(steps) + LAG:
                        attention2_turned(IT2_BASE[l] + k - LAG, steps[k - LAG][1])
                    if l == DEPTH - 1 and k in HIGH_AT:
                        attention2_high(HIGH_AT.index(k))
                if l == DEPTH - 1:
                    attention2_high(HEADS - 1)
                gaps = iter(hyena_fill(l))
                drain_fill(next(gaps))
                act.wait_ge(sem("vt_ready"), l + 1)
                act.activation(VTK[:, 0:2 * ns, :], ps[:, 0:2 * ns, :], ACT.Copy).then_inc(sem("vt_done"), 1)
                drain_fill(next(gaps))
                for s in range(ns):
                    act.wait_ge(sem("vf_ready"), 2 * l + s + 1)
                    act.activation(VFT, ps[:, :, :], ACT.Copy).then_inc(sem("vf_done"), 1)
                    drain_fill(next(gaps))
                    if s < ns - 1:
                        drain_fill(next(gaps))
                def merged2_high(m):
                    act.wait_ge(sem("take_used"), TAKE["oh", l, 2 * m + 1] + 1)
                    act.activation(MG2H[:, m, 0:n], MG2[m][:, 0:n], ACT.Copy).then_inc(sem("mg2_high"), 1)

                for i in range(2 * KD):
                    drain_fill([("oh", l, i)])
                    if i % 2 and i > 1:
                        merged2_high(i // 2 - 1)
                merged2_high(KD - 1)
                updates(ffn_norm[l], lambda m: gated("w_out2", l, m, m, 2))
                modulate(ffn_norm[l], l, 1)
                if l == 0:
                    act.wait_ge(sem("hyena"), N_SEQ[0])
                    act.dma_start(W4[0:64, :], fw4[1]).then_inc(sem("w4_loaded"), 16)
                    act.dma_start(hn[:, :], consts[:, N_KEPT:]).then_inc(sem("filter_tables"), 16)
                per = KF // FF_PARTS[l]

                def hidden_high(i):
                    act.wait_ge(sem("take_used"), TAKE["gu", l, 2 * i + 1] + 1)
                    act.activation(AFH[l][:, i % per, :], AF[l][:, i % per, :], ACT.Copy).then_inc(sem("af_high"), 1)

                for i in range(KF):
                    drain(CHUNK["gu", l, 2 * i], AF[l][:, i % per, :], ACT.Silu, n)
                    if l == 0 and i in FILTER_2[1:4]:
                        filter_sin(1, FILTER_2.index(i) - 1)
                    to_take("gu", l, 2 * i + 1, n=n)
                    if i == 0:
                        drain_fill(norm_mods(ffn_norm[l], "turns"))
                    if i % per:
                        hidden_high(i - 1)
                    if l == 0 and i == FILTER_2[4] + 1:
                        filter_spectrum(1)
                    if i % per == per - 1:
                        hidden_high(i)
                        act.wait_ge(sem("mod_done"), len(MOD_PARTS) * (l + 1))
                        if i < KF - 1:
                            for m in range(KD):
                                gated("down", l, m, m, 5)
                updates(mix_norm[1] if l == 0 else 7, lambda m: gated("down", l, KD * (FF_PARTS[l] - 1) + m, m, 5))
            act.wait_ge(sem("norm_h"), 8 * KD)
            act.dma_start(out, H[:, :, 0:T]).then_inc(sem("stored"), 16)
            act.wait_ge(sem("stored"), 16)

        @block.vector
        def _(dve):
            links = [0]

            def link(ins):
                links[0] += 1
                ins.then_inc(sem("dve_link"), 1)
                dve.wait_ge(sem("dve_link"), links[0])

            def within_pi(dst, arg, n, tmp, shift=0.0):
                magic = 1.5 * 2.0 ** 23
                c1 = 6.28125
                c2 = math.floor((TWO_PI - c1) * 2.0 ** 22) / 2.0 ** 22
                c3 = TWO_PI - c1 - c2
                link(dve.tensor_scalar(tmp, arg, 1.0 / TWO_PI, shift / TWO_PI, MUL, ADD))
                link(dve.tensor_scalar(tmp, tmp, magic, None, ADD))
                link(dve.tensor_scalar(tmp, tmp, -magic, None, ADD))
                link(dve.scalar_tensor_tensor(dst, tmp, -c1, arg, MUL, ADD))
                link(dve.scalar_tensor_tensor(dst, tmp, -c2, dst, MUL, ADD))
                link(dve.scalar_tensor_tensor(dst, tmp, -c3, dst, MUL, ADD))
                if shift:
                    link(dve.tensor_scalar(dst, dst, shift, None, ADD))
                lim = 3.1415925
                return dve.tensor_scalar(dst, dst, lim, -lim, ALU.min, MAX)

            def norm(i, gain, at, dst=None):
                n = N_NORM[i]
                norm_sum(i)
                if i == 0:
                    dve.wait_ge(sem("loaded"), 32)
                    dve.wait_ge(sem("first_tables"), 16)
                dve.wait_ge(sem("norm_rms"), i + 1)
                link(dve.reciprocal(rstd[:, 0:n], rstd[:, 0:n]))
                for k in range(KD):
                    dve.scalar_tensor_tensor((H if dst is None else dst)[:, k, 0:n], X[:, k, 0:n], PR(gain, at + k),
                                             rstd[:, 0:n], MUL, MUL).then_inc(sem("h_whole" if i in SPLIT_NORMS else "norm_h"), 1)
                    if i in SPLIT_NORMS and k >= 2:
                        low_part(i, k - 2)
                if i in SPLIT_NORMS:
                    low_part(i, KD - 2)
                    low_part(i, KD - 1)

            def low_part(i, k):
                n = N_NORM[i]
                dve.wait_ge(sem("h_high"), KD * SPLIT_NORMS.index(i) + k + 1)
                dve.tensor_tensor(HL[:, k, 0:n], H[:, k, 0:n], HH[:, k, 0:n].bitcast(F32), SUB).then_inc(sem("norm_h"), 1)

            def norm_sum(i):
                n = N_NORM[i]
                if i == 3:
                    dve.wait_ge(sem("norm_h"), 3 * KD)
                if i == ffn_norm[1]:
                    ahead(CHUNK["w_out2", DEPTH - 1, 3])
                dve.wait_ge(sem("norm_sq"), KD * i + 2)
                ins = dve.tensor_tensor(rstd[:, 0:n], H[:, 0, 0:n], H[:, 1, 0:n], ADD)
                for k in range(2, KD):
                    if i == ffn_norm[1]:
                        ahead(CHUNK["w_out2", DEPTH - 1, min(k + 2, KD - 1)])
                    link(ins)
                    dve.wait_ge(sem("norm_sq"), KD * i + k + 1)
                    ins = dve.tensor_tensor(rstd[:, 0:n], rstd[:, 0:n], H[:, k, 0:n], ADD)
                ins.then_inc(sem("norm_sum"), 1)

            def norm_over(i):
                n = N_NORM[i]
                norm_sum(i)
                dve.wait_ge(sem("norm_rms"), i + 1)
                link(dve.reciprocal(rstd[:, 0:n], rstd[:, 0:n]))
                for k in range(KD + 3):
                    if k < KD:
                        dve.tensor_tensor(H[:, k, 0:n], X[:, k, 0:n], rstd[:, 0:n], MUL).then_inc(sem("normed"), 1)
                    if k >= 3:
                        low_part(i, k - 3)

            def head_norm(i, dst, gain, pieces=1):
                a, b = dst.shape[1] // pieces, dst.shape[2]
                dve.wait_ge(sem("hn_rms"), i + 1)
                for q in range(pieces):
                    if q:
                        yield
                    r = hn[:, q * a * b:(q + 1) * a * b]
                    d = dst[:, q * a:(q + 1) * a, :]
                    if not by_log(i):
                        link(dve.reciprocal(r, r))
                    ins = dve.scalar_tensor_tensor(d, d, gain, r.rearrange("p (a b) -> p a b", a=a), MUL, MUL)
                ins.then_inc(sem("hn_done"), 1)

            def all_of(pieces):
                for piece in pieces:
                    pass

            def conv31(l, m):
                dve.wait_ge(sem("take_used"), TAKE["ag", l, 2 * m + 3] + 1)
                dve.wait_ge(sem("conv_pad"), l + 1)
                before = (l * KD + m) * (CONV_K - 1)
                for t in range(CONV_K):
                    for c in range(2):
                        k = m + c
                        w = (l * KD + k) * CONV_K + t
                        if t == 0:
                            ins = dve.tensor_scalar(CV[:, k, :], U[:, k, 0:T], PR("conv_dw_w", w), PR("conv_dw_b", l * KD + k), MUL, ADD)
                        else:
                            dve.wait_ge(sem("conv_step"), before + 2 * (t - 1) + c + 1)
                            ins = dve.scalar_tensor_tensor(CV[:, k, :], U[:, k, t:t + T], PR("conv_dw_w", w), CV[:, k, :], MUL, ADD)
                        ins.then_inc(sem("conv_step" if t < CONV_K - 1 else "conv_done"), 1)

            def sconv(l, j):
                before = (24 * l + j) * (SHORT_K - 1)
                for t in range(SHORT_K):
                    for c in range(2):
                        k = j + c
                        w = (l * 24 + k) * SHORT_K + t
                        if t == 0:
                            dve.wait_ge(sem("drained"), CHUNK["dn", l, k] + 1)
                            ins = dve.tensor_scalar(DN[:, k, :], raw[:, k % 4, 0:T], PR("dn_conv_w", w), None, MUL)
                        else:
                            dve.wait_ge(sem("sconv_step"), before + 2 * (t - 1) + c + 1)
                            ins = dve.scalar_tensor_tensor(DN[:, k, :], raw[:, k % 4, t:t + T], PR("dn_conv_w", w), DN[:, k, :], MUL, ADD)
                        ins.then_inc(sem("sconv_step" if t < SHORT_K - 1 else "sconv"), 1)

            def attention_scores(l, it):
                i = 2 * HEADS * l + it
                b = it % 2
                e = P * (b + 1)
                dve.wait_ge(sem("att_scores"), i + 1)
                if i >= 2:
                    dve.wait_ge(sem("att_weights"), i - 1)
                s = AT_S[:, i % 2, :].rearrange("p (m k) -> p m k", m=2)[:, :, 0:e]
                mask = C("causal1", P, P) if b == 0 else C("causal1")
                dve.scalar_tensor_tensor(s, ps[:, 0:2, 0:e], QK_S,
                                         rep(mask, 2), MUL, ADD).then_inc(sem("att_masked"), 1)
                dve.wait_ge(sem("att_masked"), i + 1)
                dve.tensor_reduce(at_m[:, i % 2, :], s, AX.X, MAX, negate=True).then_inc(sem("att_max"), 1)

            def attention_weights(l, it):
                i = 2 * HEADS * l + it
                e = P * (it % 2 + 1)
                dve.wait_ge(sem("att_exp"), i + 1)
                if i >= 2:
                    dve.wait_ge(sem("att_turn"), i - 1)
                r = at_l[:, i % 2, :]
                link(dve.reciprocal(r, r))
                link(dve.tensor_scalar(r[:, 1:2], r[:, 1:2], lam[:, 4 + l:5 + l], None, MUL))
                link(dve.tensor_scalar(AT_A[:, i % 2, 0:e], AT_S[:, i % 2, 0:e], r[:, 0:1], None, MUL))
                dve.scalar_tensor_tensor(AT_A[:, i % 2, 0:e], AT_S[:, i % 2, T:T + e], r[:, 1:2], AT_A[:, i % 2, 0:e], MUL, ADD)\
                    .then_inc(sem("att_weights"), 1)

            def attention_out(l, it):
                i = 2 * HEADS * l + it
                dve.wait_ge(sem("att_o"), i + 1)
                dve.tensor_copy(QK[:, it // 2, (it % 2) * P:(it % 2 + 1) * P], ps[:, 3, 0:P]).then_inc(sem("att_out"), 1)

            def delta_gates(l):
                dve.wait_ge(sem("beta"), l + 1)
                both = ps[:, 0, 0:32].rearrange("p (c n) -> p c n", c=NT)
                link(dve.tensor_tensor(B0, both[:, :, HEADS:], rep(PR("dn_dt_bias", l * HEADS, HEADS), NT), ADD))
                dve.scalar_tensor_tensor(B1, B0, -1.0, B0, MUL, MAX).then_inc(sem("abs_a"), 1)
                dve.wait_ge(sem("ln_abs"), l + 1)
                link(dve.tensor_scalar(GC, B1, 1.0, None, ADD))
                link(dve.tensor_scalar(NGC, GC, -1.0, None, ADD))
                link(dve.tensor_tensor(NGC, B1, NGC, SUB))
                link(dve.reciprocal(GC, GC))
                link(dve.tensor_tensor(NGC, NGC, GC, MUL))
                link(dve.tensor_tensor(B2, B2, NGC, ADD))
                link(dve.scalar_tensor_tensor(B0, B0, 0.0, B2, MAX, ADD))
                dve.wait_ge(sem("exp_a"), l + 1)
                dve.scalar_tensor_tensor(G, B0, -1.0, rep(EXA, NT), MUL, MUL).then_inc(sem("g_done"), 1)
                all_of(head_norm(HN_BASE1(l) + DK_N, DN[:, 8:16, :], 1.0))
                dve.wait_ge(sem("exp_gc"), l + 1)
                link(dve.tensor_scalar(NGC, ps[:, 1, 0:16].rearrange("p (c h) -> p c h", c=NT), -1.0, None, MUL))
                dve.tensor_tensor(BEG, BEG, BETA, MUL).then_inc(sem("gates_done"), 1)
                dve.wait_ge(sem("gates_done"), l + 1)

            def level(i, s):
                dve.tensor_tensor(LM[s % 2].rearrange("p (a b) -> p a b", a=4), LT.rearrange("p (a b) -> p a b", a=4),
                                  rep(C("levels", s * P, P), 4), MUL).then_inc(sem("d_lm"), 1)

            def diagonals(l, u):
                for p in range(4):
                    h, c = 2 * u + p // 2, p % 2
                    dve.tensor_scalar(UG[:, p * P:(p + 1) * P], C("until"), G[:, c, h:h + 1], None, MUL)
                    ins = dve.tensor_scalar(IB[:, p * P:(p + 1) * P], ident, BETA[:, c, h:h + 1], None, MUL)
                ins.then_inc(sem("d_ugib"), 1)

            def delta(l, u):
                i = 4 * l + u
                q4 = lambda ap: ap.rearrange("p (a b) -> p a b", a=4)
                dve.wait_ge(sem("d_pre"), 4 * i + 1)
                dve.tensor_tensor(q4(DT), q4(ps[:, 0, :]), rep(C("later"), 4), ADD).then_inc(sem("d_dt"), 1)
                dve.wait_ge(sem("d_pre"), 4 * i + 4)
                dve.wait_ge(sem("d_exp"), i + 1)
                link(dve.tensor_tensor(LT, ps[:, 2, :], DT, MUL))
                dve.tensor_tensor(IN, ps[:, 3, :], DT, MUL)
                dve.tensor_tensor(LT, LT, ps[:, 1, :], MUL).then_inc(sem("d_lt"), 1)
                dve.tensor_tensor(QG, DN[:, 2 * u:2 * u + 2, P:T], EXR, MUL).then_inc(sem("d_qg"), 1)
                dve.wait_ge(sem("d_lt"), i + 1)
                level(i, 0)
                dve.wait_ge(sem("d_lm"), 7 * i + 1)
                dve.scalar_tensor_tensor(q4(TT), q4(LM[0]), -1.0, rep(ident, 4), MUL, ADD).then_inc(sem("d_tt"), 1)
                level(i, 1)
                pieces = head_norm(HN_BASE1(l) + ATT_N, QK[:, 0:8, :], lam[:, 6 + l:7 + l], 2) if u == 0 else iter(())
                dve.wait_ge(sem("d_tt"), i + 1)
                for s in range(1, 7):
                    if s < 6:
                        if s > 1:
                            dve.wait_ge(sem("d_x"), 6 * i + s - 1)
                        level(i, s + 1)
                    next(pieces, None)
                    dve.wait_ge(sem("d_bc"), 6 * i + s)
                    if s < 6:
                        if s == 1:
                            dve.wait_ge(sem("d_tm"), i + 1)
                        dve.tensor_tensor(TM, TM, ps[:, 3, :], SUB)
                    dve.tensor_tensor(TT, TT, ps[:, 2, :], SUB).then_inc(sem("d_upd"), 1)
                    dve.wait_ge(sem("d_upd"), 6 * i + s)
                dve.wait_ge(sem("d_kv"), i + 1)
                for p in range(4):
                    h, c = 2 * u + p // 2, p % 2
                    dve.tensor_scalar(VB[:, p * P:(p + 1) * P], ps[:, 1, p * P:(p + 1) * P], BETA[:, c, h:h + 1], None, MUL)
                    if c:
                        ins = dve.tensor_scalar(KBG[:, p // 2, :], ps[:, 0, p * P:(p + 1) * P], BEG[:, 1, h:h + 1], None, MUL)
                    else:
                        dve.tensor_scalar(KDEC[:, p // 2, :], ps[:, 0, p * P:(p + 1) * P],
                                          DT[:, (p + 1) * P - 1:(p + 1) * P], None, MUL)
                ins.then_inc(sem("d_vb"), 1)
                if u < UNITS - 1:
                    diagonals(l, u + 1)

            dve.wait_ge(sem("x_loaded"), 16)
            norm(0, "norm_w", 0)
            dve.wait_ge(sem("wb_high"), 1)
            dve.tensor_tensor(WB_LO, PR("w_ba", 0, PARAM_W["w_ba"]), WB_HI[:, :].bitcast(F32), SUB).then_inc(sem("wb_low"), 1)
            link(dve.tensor_copy(POSF, ANGI))
            link(dve.tensor_scalar(RR[:, 1, :], POSF, C("inv1"), None, MUL))
            within_pi(POSF, RR[:, 1, :], T, RR[:, 2, :]).then_inc(sem("ang"), 1)
            within_pi(RR[:, 0, :], RR[:, 1, :], T, RR[:, 2, :], math.pi / 2).then_inc(sem("ang"), 1)
            lqp = RR[:, 1:3, :].rearrange("p a b -> p (a b)")[:, 0:4 * QK_DIM]
            lq = PR("lam_qk", 0, DEPTH * 4 * QK_DIM).rearrange("p (l a d) -> p l a d", a=4, d=QK_DIM)
            for l in range(DEPTH):
                for a in range(2):
                    link(dve.tensor_tensor(lqp[:, (2 * l + a) * QK_DIM:(2 * l + a + 1) * QK_DIM], lq[:, l, 2 * a, :], lq[:, l, 2 * a + 1, :], MUL))
            dve.tensor_reduce(lam[:, 0:4], lqp.rearrange("p (a d) -> p a d", a=4), AX.X, ADD).then_inc(sem("lam_dots"), 1)
            dve.wait_ge(sem("lam_exp"), 1)
            for l in range(DEPTH):
                link(dve.tensor_tensor(lam[:, 4 + l:5 + l], lam[:, 2 * l + 1:2 * l + 2], lam[:, 2 * l:2 * l + 1], SUB))
                link(dve.tensor_tensor(lam[:, 4 + l:5 + l], lam[:, 4 + l:5 + l], C("lam_init", l, 1), SUB))
            for l in range(DEPTH):
                link(dve.tensor_scalar(lam[:, 6 + l:7 + l], PR("attn_subln_w", l), 1.0 - (0.8 - 0.6 * math.exp(-0.3 * l)), None, MUL))
            dve.wait_ge(sem("rope_table"), 1)
            def rope(i, qk, cos, sin):
                if i:
                    dve.wait_ge(sem("rope"), i)
                dve.wait_ge(sem("rot"), i + 1)
                dve.tensor_tensor(cut(at_buf, 0, 2, T), qk, rep(cos, 2), MUL).then_inc(sem("rope_cos"), 1)
                link(dve.tensor_tensor(cut(at_buf, 512, 2, T), ps[:, 2 + i % 2, :].rearrange("p (a b) -> p a b", a=2),
                                       rep(sin, 2), MUL))
                dve.wait_ge(sem("rope_cos"), i + 1)
                dve.tensor_tensor(qk, cut(at_buf, 0, 2, T), cut(at_buf, 512, 2, T), ADD).then_inc(sem("rope"), 1)

            split = [0]

            def ahead(j):
                while split[0] < len(PIECES) and PIECES[split[0]][4] <= j:
                    t, n, place, reader, step, who, count = PIECES[split[0]]
                    split[0] += 1
                    if not who:
                        continue
                    cols = slice(t % TILES * P, (t % TILES + n) * P)
                    slot = t // TILES % RING
                    dve.wait_ge(sem("high_ready"), split[0])
                    dve.tensor_tensor(ring_lo[:, slot, cols], ring[:, slot, cols],
                                      ring_hi[:, place * P:(place + n) * P].bitcast(F32), SUB).then_inc(sem(LOW_READY[1]), 1)

            def modulation(l, part):
                first, end = (x * KD for x in MOD_PARTS[part])
                dve.wait_ge(sem("drained"), CHUNK["modt", l, end * P // 512 - 1] + 1)
                bias = PR("b_mod", l * N_MOD * KD + first, end - first)
                ins = dve.tensor_tensor(mod[:, l, first:end, :], mod[:, l, first:end, :], wide(bias, 2), ADD)
                if part < 2:
                    link(ins)
                    gain = PR(("norm_mix", "norm_ffn")[part], l * KD, KD)
                    ins = dve.scalar_tensor_tensor(gains[:, part, :, :], mod[:, l, first + KD:first + 2 * KD, :], 1.0, wide(gain, 2), ADD, MUL)
                ins.then_inc(sem("mod_done"), 1)

            def filters(l):
                for k in range(3):
                    if l == 0:
                        ahead(CHUNK["d_out", DEPTH - 1, FILTER_1[k]])
                    dve.wait_ge(sem("f_ready"), 3 * l + k + 1)
                    link(dve.tensor_scalar(RR[0:64, 1, :], ps[0:64, 1, 0:T], PR("filt_b", 3 * l + k)[0:64],
                                           PR("filt_freq", 3 * l + k)[0:64], ADD, MUL))
                    within_pi(RR[0:64, 0, :], RR[0:64, 1, :], T, RR[0:64, 2, :]).then_inc(sem("f_arg"), 1)

            def filter_decay(l):
                dve.wait_ge(sem("h4_ready"), l + 1)
                dve.wait_ge(sem("filter_tables"), 16 * (l + 1))
                for half in range(2):
                    ins = dve.tensor_tensor(VTK[:, 2 * half:2 * half + 2, :], ps[:, 2 * half:2 * half + 2, :],
                                            DECAY.rearrange("p (a b) -> p a b", a=NT), MUL)
                ins.then_inc(sem("h4_done"), 1)

            for l in range(DEPTH):
                if l:
                    norm(l, "norm_w", l * KD)
                for m in range(0, KD, 2):
                    conv31(l, m)
                dve.wait_ge(sem("ln_mean"), l + 1)
                dve.scalar_tensor_tensor(CV, rep(ps[:, 0, 0:T], KD), -1.0 / D, CV, MUL, ADD).then_inc(sem("ln_centered"), 1)
                for j in range(24):
                    if j in ROPE_AT:
                        jj = ROPE_AT.index(j)
                        rope(8 * l + jj, QK[:, 2 * jj:2 * jj + 2, :], tab[:, 0, :], tab[:, 1, :])
                    if j % 2:
                        sconv(l, j - 1)
                    if j == DN_EARLY:
                        dve.wait_ge(sem("ln_centered"), l + 1)
                        dve.wait_ge(sem("ln_rms"), l + 1)
                        link(dve.reciprocal(rstd[:, 0:T], rstd[:, 0:T]))
                        dve.tensor_tensor(CV, CV, rep(rstd[:, 0:T], KD), MUL).then_inc(sem("ln_normed"), 1)
                    if j in (14, 16, 18, 20):
                        if j == 14:
                            pieces = head_norm(HN_BASE1(l) + DQ_N, DN[:, 0:8, :], DN_S, 4)
                        next(pieces, None)
                dve.wait_ge(sem("tables"), 32)
                delta_gates(l)
                for it in range(ATT_STEPS + LAG + 1):
                    if it < ATT_STEPS:
                        attention_scores(l, it)
                    if 1 <= it <= ATT_STEPS:
                        attention_weights(l, it - 1)
                    if it > LAG:
                        attention_out(l, it - LAG - 1)
                    if it == 16:
                        diagonals(l, 0)
                for u in range(UNITS):
                    delta(l, u)
                all_of(head_norm(HN_BASE1(l) + DO_N, DN[:, 0:8, :], PR("dn_norm_w", l)))
                dve.wait_ge(sem("drained"), CHUNK["dz", l, KD - 1] + 1)
                dve.wait_ge(sem("hn_done"), HN_BASE1(l) + DO_N + 1)
                for m in range(KD):
                    dve.tensor_tensor(DN[:, m, :], DN[:, m, :], CV[:, m, :], MUL).then_inc(sem("dn_whole"), 1)
                for m in range(KD):
                    dve.wait_ge(sem("dn_high"), KD * l + m + 1)
                    dve.tensor_tensor(DNL[:, m, :], DN[:, m, :], DNH[:, m, :].bitcast(F32), SUB).then_inc(sem("dn_ready"), 1)
                if l == DEPTH - 1:
                    for part in range(len(MOD_PARTS)):
                        modulation(0, part)
                    filters(0)
                for m in range(KD):
                    ahead(CHUNK["d_out", l, min(2 * m + 3, 2 * KD - 1)])
                    if l == DEPTH - 1 and m == KD - 2:
                        filter_decay(0)
                    dve.wait_ge(sem("mg_high"), KD * l + m + 1)
                    dve.tensor_tensor(MGL[:, m, :], MG[:, m, :], MGH[:, m, :].bitcast(F32), SUB).then_inc(sem("mg_low"), 1)
            norm(2, "final_norm_w", 0, X)

            def attention2_max(i, s):
                n = 2 * T if s == 0 else T
                dve.wait_ge(sem("a2_scores"), i + 1)
                link(dve.tensor_reduce(at_m[:, i % 2, 0:1], ps[:, i % 2, 0:n], AX.X, MAX, negate=True))
                dve.tensor_scalar(at_m[:, i % 2, 0:1], at_m[:, i % 2, 0:1], P ** -0.5, None, MUL).then_inc(sem("a2_max"), 1)

            def attention2_weights(i, s):
                n = 2 * T if s == 0 else T
                dve.wait_ge(sem("a2_exp"), i + 1)
                if i >= 2:
                    dve.wait_ge(sem("a2_turn"), i - 1)
                link(dve.reciprocal(at_l[:, i % 2, 0:1], at_l[:, i % 2, 0:1]))
                dve.tensor_scalar(AT_A[:, i % 2, 0:n], AT_S[:, i % 2, 0:n], at_l[:, i % 2, 0:1], None, MUL)\
                    .then_inc(sem("a2_weights"), 1)

            def attention2_out(i, step):
                h, s, b = step
                dve.wait_ge(sem("a2_o"), i + 1)
                dve.tensor_copy(Q2_[:, h, s * T + b * P:s * T + (b + 1) * P], ps[:, 3, 0:P]).then_inc(sem("a2_out"), 1)

            def hyena_conv(l, j):
                n, ns = N_TOK[l], N_SEQ[l]
                dve.wait_ge(sem("drained"), CHUNK["hy2", l, j] + 1)
                s0 = (j % 2) * 2
                dst = (X0, X1, VX)[j // 4][:, j % 4, 0:n].rearrange("p (s t) -> p s t", s=ns)
                w = (l * 12 + j) * HY_TAPS
                link(dve.tensor_scalar(dst, hraw[:, s0:s0 + ns, 0:T], PR("conv_w", w), PR("conv_b", l * 12 + j), MUL, ADD))
                yield
                link(dve.scalar_tensor_tensor(dst, hraw[:, s0:s0 + ns, 1:T + 1], PR("conv_w", w + 1), dst, MUL, ADD))
                yield
                ins = dve.scalar_tensor_tensor(dst, hraw[:, s0:s0 + ns, 2:T + 2], PR("conv_w", w + 2), dst, MUL, ADD)
                if j >= 8:
                    link(ins)
                    yield
                    ins = dve.tensor_tensor(VX[:, j - 8, 0:n], VX[:, j - 8, 0:n], X1[:, j - 8, 0:n], MUL)
                ins.then_inc(sem("hconv"), 1)

            def rope2(l, jj):
                rope(ROPE2[l] + jj, Q2_[:, 2 * jj - 2:2 * jj, 0:T] if jj else K2_[:, :, 0:T], C("cos2"), C("sin2"))

            for l in range(DEPTH):
                n, ns = N_TOK[l], N_SEQ[l]
                norm_over(mix_norm[l])
                if l == 1:
                    dve.wait_ge(sem("norm_h"), KD * (ffn_norm[0] + 1))
                    modulation(1, 1)
                i = HN_BASE2[l]
                all_of(head_norm(i, K2_, PR("k_norm", l)))
                all_of(head_norm(i + 1, Q2_[:, 0:4, 0:n], PR("q_norm", l)))
                all_of(head_norm(i + 2, Q2_[:, 4:8, 0:n], PR("q_norm", l)))
                for j in range(EARLY_HY):
                    all_of(hyena_conv(l, j))
                    for jj in ROPES_AFTER[j]:
                        rope2(l, jj)
                steps = IT2[l]
                convs, l_long = [], int(l == 0)
                for k, items in enumerate(att2_fill(l)):
                    i = IT2_BASE[l] + k
                    if k < len(steps):
                        attention2_max(i, steps[k][1])
                    if 1 <= k <= len(steps):
                        attention2_weights(i - 1, steps[k - 1][1])
                    if k > LAG:
                        attention2_out(i - LAG - 1, steps[k - LAG - 1])
                    for name, l_, j in items:
                        convs.append(hyena_conv(l, j))
                    for turn in range(2 - l_long):
                        if convs and next(convs[0], "done") == "done":
                            convs.pop(0)
                for conv in convs:
                    all_of(conv)
                for s in range(ns):
                    k = 2 * l + s
                    re, im = slice(0, 2), slice(2, 4)
                    dve.wait_ge(sem("vf_done"), k + 1)
                    dve.wait_ge(sem("kf_done"), l + 1)
                    dve.tensor_tensor(YFT[:, re, :], VFT[:, re, :], KFT[:, re, :], MUL)
                    link(dve.tensor_tensor(PROD, VFT[:, im, :], KFT[:, im, :], MUL))
                    dve.tensor_tensor(YFT[:, im, :], VFT[:, re, :], KFT[:, im, :], MUL)
                    link(dve.tensor_tensor(YFT[:, re, :], YFT[:, re, :], PROD, SUB))
                    link(dve.tensor_tensor(PROD, VFT[:, im, :], KFT[:, re, :], MUL))
                    link(dve.tensor_tensor(YFT[:, im, :], YFT[:, im, :], PROD, ADD))
                    dve.tensor_tensor(YFT[0:1, 0, :], VFT[0:1, 0, :], KFT[0:1, 0, :], MUL)
                    dve.tensor_tensor(YFT[0:1, 2, :], VFT[0:1, 2, :], KFT[0:1, 2, :], MUL).then_inc(sem("y_done"), 1)
                    dve.wait_ge(sem("yi_ready"), k + 1)
                    for m in range(KH):
                        link(dve.scalar_tensor_tensor(VX[:, m, s * T:(s + 1) * T], VX[:, m, s * T:(s + 1) * T], PR("hyena_bias", l * KH + m),
                                                      ps[:, m // 2, (m % 2) * T:(m % 2 + 1) * T], MUL, ADD))
                    x0, vx, high = (b[:, :, s * T:(s + 1) * T] for b in (X0, VX, X0H))
                    dve.tensor_tensor(X0P, x0, vx, MUL)
                    link(dve.tensor_tensor(high, x0, vx, MUL))
                    dve.tensor_tensor(X0L[:, :, s * T:(s + 1) * T], X0P, high.bitcast(F32), SUB).then_inc(sem("hyena"), 1)
                for m in range(KD):
                    if l == DEPTH - 1:
                        ahead(CHUNK["oh", l, 2 * m + 1])
                    dve.wait_ge(sem("mg2_high"), KD * l + m + 1)
                    dve.tensor_tensor(MG2L[m][:, 0:n], MG2[m][:, 0:n], MG2H[:, m, 0:n].bitcast(F32), SUB).then_inc(sem("mg2_low"), 1)
                norm_over(ffn_norm[l])
                if l == 1:
                    modulation(1, 2)
                if l == 0:
                    dve.wait_ge(sem("norm_h"), KD * (mix_norm[0] + 1))
                    modulation(1, 0)
                    filters(1)
                    filter_decay(1)
                for i in range(KF):
                    c = i % (KF // FF_PARTS[l])
                    ahead(CHUNK["gu", l, 2 * i + 1])
                    dve.wait_ge(sem("af_high"), KF * l + i + 1)
                    dve.tensor_tensor(AFL[l][:, c, :], AF[l][:, c, :], AFH[l][:, c, :].bitcast(F32), SUB).then_inc(sem("af_low"), 1)
            for m in range(KD):
                ahead(CHUNK["down", DEPTH - 1, m])
            norm(7, "norm_final", 0)

        @block.tensor
        def _(pe):
            at = {"tile": 0, "free": 0, "chunk": 0, "split": 0, "raw": False}

            def tile(n=1, split=False):
                t = at["tile"]
                at["tile"] += n
                load, off = divmod(t, TILES)
                if not split and (off == 0 or not at["raw"]):
                    pe.wait_ge(sem(f"weights{load % RING}"), 16 * (load // RING + 1))
                assert off + n <= TILES
                if t in PIECE_OF:
                    who, count = PIECE_OF[t][5:]
                    pe.wait_ge(sem(LOW_READY[who]), count)
                if off + n == TILES:
                    at["free"] += 1
                at["raw"] = not split
                cols = slice(off * P, (off + n) * P)
                if not split:
                    return ring[:, load % RING, cols]
                place = at["split"] % HIGHS
                at["split"] += n
                return ring_hi[:, place * P:(place + n) * P], ring_lo[:, load % RING, cols]

            def parts(out, a, b, start, stop):
                first = pe.matmul(out, a[0], b[0], start=start, stop=False)
                pe.matmul(out, a[1], b[0], start=False, stop=False)
                return first, pe.matmul(out, a[0], b[1], start=False, stop=stop)

            def chunk(name, l, i, k, rhs, n, arrived=None):
                for part in chunk_parts(name, l, i, k, rhs, n, arrived):
                    pass

            def chunk_parts(name, l, i, k, rhs, n, arrived=None):
                j = CHUNK[name, l, i]
                assert j == at["chunk"], (name, l, i)
                at["chunk"] += 1
                if j >= 4:
                    pe.wait_ge(sem("drained"), j - 3)
                for c in range(k):
                    freed = at["free"]
                    if arrived:
                        arrived(c)
                    first = None
                    if is_split(name, l, i):
                        first, ins = parts(pg[:, j % 4, 0:n], tile(split=True), rhs(c), c == 0, c == k - 1)
                    elif name == "mod":
                        ins = pe.matmul(pg[0:2, j % 4, :], sc[:, c, :], tile(4), start=c == 0, stop=c == k - 1)
                    else:
                        ins = pe.matmul(pg[:, j % 4, 0:n], tile(), rhs(c), start=c == 0, stop=c == k - 1)
                    if freed and (first or c < k - 1):
                        (first or ins).then_inc(sem("slot_free"), freed)
                        at["free"] -= freed
                    if (c + 1) % (k // n_parts(name)) == 0 and c < k - 1:
                        yield
                ins.then_inc(sem("chunk_ready"), 1)

            def turn_rows(l, i):
                j = CHUNK["modt", l, i]
                assert j == at["chunk"]
                at["chunk"] += 1
                pe.wait_ge(sem("drained"), max(CHUNK["mod", l, i] + 1, j - 3))
                for q in range(4):
                    ins = pe.transpose(pg[:, j % 4, 2 * q:2 * q + 2], mod_rows[0:2, i % 2, q * P:(q + 1) * P], ident[0:2, 0:2])
                ins.then_inc(sem("chunk_ready"), 1)

            def normed(i):
                def wait(c):
                    pe.wait_ge(sem("norm_h"), KD * i + c + 1)
                return wait

            def low_ready(name, before):
                def wait(c):
                    pe.wait_ge(sem(name), before + c + 1)
                return wait

            started = []

            def fill(items):
                for item in items:
                    if item[0] == "part":
                        if not started:
                            started.append(parts_by_name(*item[1]))
                        next(started[0])
                    elif item[0] == "modt":
                        turn_rows(*item[1:])
                    else:
                        for chunk_of in started or [parts_by_name(*item)]:
                            for part in chunk_of:
                                pass
                        started.clear()

            def parts_by_name(name, l, i):
                if name == "mod":
                    return chunk_parts(name, l, i, KD, None, 512)
                n = N_TOK[l] if name in ("hy2", "oa", "oh") else T
                if i % 2 == 0 or name in ("cz", "az", "dz", "hy2"):
                    return chunk_parts(name, l, i, KD, parts_of(HH, HL, n), n)
                if name in ("c_out", "a_out", "d_out"):
                    z, src = {"c_out": ("cz", parts_of(CVH, CVL, T)), "a_out": ("az", parts_of(AOH, AOL, T)),
                              "d_out": ("dz", parts_of(DNH, DNL, T))}[name]

                    def multiplied(c):
                        if z == "dz":
                            pe.wait_ge(sem("dn_ready"), KD * l + c + 1)
                        else:
                            pe.wait_ge(sem("take_used"), TAKE[z, l, c] + 1)
                    return chunk_parts(name, l, i, KD, src, T, multiplied if i == 1 else None)
                if name == "oh":
                    return chunk_parts(name, l, i, KH, parts_of(X0H, X0L, n), n)
                if l == 0:
                    return chunk_parts(name, l, i, KD, rows_of(Q2_, n), n)
                return chunk_parts(name, l, i, KD, parts_of(A2H, A2L, n), n, low_ready("a2_low", 0) if i == 1 else None)

            def filter_step(l, step):
                if step < 3:
                    if step == 0:
                        lhsT, rhs = PR("filt_w1", l * 64, 64)[0:33], C("zT")[0:33]
                        if l == 0:
                            pe.wait_ge(sem("hn_rms"), HN_BASE1(1) + DO_N + 1)
                        else:
                            pe.wait_ge(sem("norm_rms"), ffn_norm[0] + 1)
                    else:
                        lhsT, rhs = PR(f"filt_w{step + 1}", l * 64, 64)[0:64], HQ[0:64, :]
                        pe.wait_ge(sem("f_sin"), 3 * l + step)
                    pe.matmul(ps[0:64, 1, 0:T], lhsT, rhs, start=True, stop=True).then_inc(sem("f_ready"), 1)
                elif step == 3:
                    pe.wait_ge(sem("f_sin"), 3 * l + 3)
                    pe.wait_ge(sem("w4_loaded"), 16 * (l + 1))
                    for half in range(2):
                        for tt in range(NT):
                            ins = pe.matmul(ps[:, 2 * half + tt, :], HQ[0:64, tt * P:(tt + 1) * P],
                                            W4[0:64, half * HY:(half + 1) * HY], start=True, stop=True)
                    ins.then_inc(sem("h4_ready"), 1)
                else:
                    pe.wait_ge(sem("h4_done"), l + 1)
                    for ft in range(4):
                        for q in range(4):
                            table = C("dft_fwd") if q < 2 else DFT_BWD
                            ins = pe.matmul(ps[:, ft, :], table[:, (q % 2) * N_FFT + ft * P:(q % 2) * N_FFT + (ft + 1) * P], VTK[:, q, :], start=q == 0, stop=q == 3)
                    ins.then_inc(sem("kf_ready"), 1)

            def parts_of(high, low, n):
                return lambda c: (high[:, c, 0:n], low[:, c, 0:n])

            def rows_of(buf, n):
                return lambda c: buf[:, c, 0:n]

            def norm(i):
                n = N_NORM[i]
                fill(norm_mods(i, "before"))
                pe.wait_ge(sem("norm_sum"), i + 1)
                pe.matmul(ps[:, 0, 0:n], ones, rstd[:, 0:n], start=True, stop=True).then_inc(sem("norm_ss"), 1)
                fill(norm_mods(i, "after"))

            def head_norm(i, cols):
                pe.wait_ge(sem("hn_sq"), i + 1)
                for b in range(cols // 512):
                    ins = pe.matmul(ps[:, b, :], ones, sq[:, b * 512:(b + 1) * 512], start=True, stop=True)
                ins.then_inc(sem("hn_ss"), 1)

            def rot(i, table, qk):
                if i >= 2:
                    pe.wait_ge(sem("rope"), i - 1)
                pe.matmul(ps[:, 2 + i % 2, :], table, qk, start=True, stop=True).then_inc(sem("rot"), 1)

            def tokens_first(name, l, i, w, tt, n, freed=0):
                j = CHUNK[name, l, i]
                assert j == at["chunk"]
                at["chunk"] += 1
                if j >= 4:
                    pe.wait_ge(sem("drained"), j - 3)
                for k in range(KD):
                    t = slice(tt * P, (tt + 1) * P)
                    first, ins = parts(pg[:, j % 4, 0:n], (HH[:, k, t], HL[:, k, t]), w[k], k == 0, k == KD - 1)
                    if freed and k == 0:
                        first.then_inc(sem("slot_free"), freed)
                        at["free"] -= freed
                ins.then_inc(sem("chunk_ready"), 1)

            def attention_scores(l, it):
                i = 2 * HEADS * l + it
                h, b = it // 2, it % 2
                e = P * (b + 1)
                if i >= 1:
                    pe.wait_ge(sem("att_masked"), i)
                for m in range(2):
                    r = slice(m * QK_DIM, (m + 1) * QK_DIM)
                    ins = pe.matmul(ps[:, m, 0:e], QK[r, h, b * P:(b + 1) * P], QK[r, HEADS + h, 0:e],
                                    start=True, stop=True)
                ins.then_inc(sem("att_scores"), 1)

            def attention_turn(l, it):
                i = 2 * HEADS * l + it
                pe.wait_ge(sem("att_weights"), i + 1)
                if i >= 1:
                    pe.wait_ge(sem("att_turned"), i)
                for kb in range(it % 2 + 1):
                    ins = pe.transpose(ps[:, 2, kb * P:(kb + 1) * P], AT_A[:, i % 2, kb * P:(kb + 1) * P], ident)
                ins.then_inc(sem("att_turn"), 1)

            def attention_out(l, it):
                i = 2 * HEADS * l + it
                h, b = it // 2, it % 2
                pe.wait_ge(sem("att_turned"), i + 1)
                if i >= 1:
                    pe.wait_ge(sem("att_out"), i)
                for kb in range(b + 1):
                    ins = pe.matmul(ps[:, 3, 0:P], V[:, kb, h * P:(h + 1) * P], AT_T[:, i % 2, kb * P:(kb + 1) * P],
                                    start=kb == 0, stop=kb == b)
                ins.then_inc(sem("att_o"), 1)

            def delta_gates(l):
                fill([("cz", l, 0)])
                pe.wait_ge(sem("hn_rms"), HN_BASE1(l) + DK_N + 1)
                pe.wait_ge(sem("wb_low"), 1)
                for c in range(NT):
                    for k in range(KD):
                        a = slice((l * KD + k) * 16, (l * KD + k + 1) * 16)
                        t = slice(c * P, (c + 1) * P)
                        first, ins = parts(ps[:, 0, c * 16:(c + 1) * 16], (HH[:, k, t], HL[:, k, t]), (WB_HI[:, a], WB_LO[:, a]),
                                           k == 0, k == KD - 1)
                ins.then_inc(sem("ba_ready"), 1)
                fill([("cz", l, m) for m in range(1, EARLY_CZ // 2)] + mods(l, "gates"))
                pe.wait_ge(sem("g_done"), l + 1)
                for c in range(NT):
                    ins = pe.matmul(ps[:, 1, c * HEADS:(c + 1) * HEADS], C("until"), G[:, c, :], start=True, stop=True)
                ins.then_inc(sem("gc_ready"), 1)
                fill([("cz", l, m) for m in range(EARLY_CZ // 2, EARLY_CZ)])
                pe.wait_ge(sem("gates_done"), l + 1)

            def delta(l, u):
                i = 4 * l + u
                pair = [(2 * u + p // 2, p % 2, slice(p * P, (p + 1) * P)) for p in range(4)]
                kT = lambda h, c: DN[:, HEADS + h, c * P:(c + 1) * P]
                vT = lambda h, c: DN[:, 2 * HEADS + h, c * P:(c + 1) * P]
                gaps = iter(delta_fill(l)[u * DELTA_POINTS:(u + 1) * DELTA_POINTS])
                fill(next(gaps))
                pe.wait_ge(sem("d_ugib"), i + 1)
                if u == 0:
                    pe.wait_ge(sem("hn_rms"), HN_BASE1(l) + ATT_N + 1)
                pe.matmul(ps[:, 0, :], ones, UG, start=True, stop=True).then_inc(sem("d_pre"), 1)
                if u:
                    pe.wait_ge(sem("d_out"), i)
                pe.matmul(ps[:, 1, :], ones, IB, start=True, stop=True).then_inc(sem("d_pre"), 1)
                for h, c, s in pair:
                    ins = pe.matmul(ps[:, 2, s], kT(h, c), kT(h, c), start=True, stop=True)
                ins.then_inc(sem("d_pre"), 1)
                for h, c, s in pair:
                    ins = pe.matmul(ps[:, 3, s], kT(h, c), DN[:, h, c * P:(c + 1) * P], start=True, stop=True)
                ins.then_inc(sem("d_pre"), 1)
                fill(next(gaps))
                pe.wait_ge(sem("d_tt"), i + 1)
                for h, c, s in pair:
                    ins = pe.transpose(ps[:, 0, s], TT[:, s], ident)
                ins.then_inc(sem("d_t0"), 1)
                for v in range(1, 7):
                    fill(next(gaps))
                    if v == 1:
                        pe.wait_ge(sem("d_tm"), i + 1)
                    pe.wait_ge(sem("d_lm"), 7 * i + v + 1)
                    if v > 1:
                        pe.wait_ge(sem("d_upd"), 6 * i + v - 1)
                    for h, c, s in pair:
                        ins = pe.matmul(ps[:, 1, s], LM[v % 2][:, s], TM[:, s], start=True, stop=True)
                    ins.then_inc(sem("d_x"), 1)
                    fill(next(gaps))
                    pe.wait_ge(sem("d_xs"), 6 * i + v)
                    if v < 6:
                        for h, c, s in pair:
                            pe.matmul(ps[:, 3, s], TT[:, s], XS[:, s], start=True, stop=True)
                    for h, c, s in pair:
                        ins = pe.matmul(ps[:, 2, s], XS[:, s], TT[:, s], start=True, stop=True)
                    ins.then_inc(sem("d_bc"), 1)
                for h, c, s in pair:
                    pe.transpose(ps[:, 0, s], kT(h, c), ident)
                for h, c, s in pair:
                    ins = pe.transpose(ps[:, 1, s], vT(h, c), ident)
                ins.then_inc(sem("d_kv"), 1)
                fill(next(gaps))
                pe.wait_ge(sem("d_vb"), i + 1)
                for hh in range(2):
                    pe.matmul(ps[:, 2, hh * P:(hh + 1) * P], KBG[:, hh, :], TT[:, pair[2 * hh + 1][2]], start=True, stop=True)
                for hh in range(2):
                    s = pair[2 * hh][2]
                    ins = pe.matmul(ps[:, 2, (2 + hh) * P:(3 + hh) * P], TT[:, s], VB[:, s], start=True, stop=True)
                ins.then_inc(sem("d_w"), 1)
                fill(next(gaps))
                pe.wait_ge(sem("d_vn0"), i + 1)
                for hh in range(2):
                    ins = pe.matmul(ps[:, 3, hh * P:(hh + 1) * P], KDEC[:, hh, :], VN[:, hh * P:(hh + 1) * P], start=True, stop=True)
                ins.then_inc(sem("d_s"), 1)
                fill(next(gaps))
                pe.wait_ge(sem("d_s1"), i + 1)
                for hh in range(2):
                    s = pair[2 * hh + 1][2]
                    pe.matmul(ps[:, 0, hh * P:(hh + 1) * P], TT[:, s], VB[:, s], start=True, stop=False)
                    ins = pe.matmul(ps[:, 0, hh * P:(hh + 1) * P], NW[:, hh, :], S1[:, hh, :], start=False, stop=True)
                ins.then_inc(sem("d_v1"), 1)
                fill(next(gaps))
                pe.wait_ge(sem("d_vn1"), i + 1)
                pe.wait_ge(sem("d_qg"), i + 1)
                for hh in range(2):
                    o = hh * T
                    pe.matmul(ps[:, 1, o:o + P], VN[:, hh * P:(hh + 1) * P], IN[:, pair[2 * hh][2]], start=True, stop=True)
                    pe.matmul(ps[:, 1, o + P:o + T], S1[:, hh, :], QG[:, hh, :], start=True, stop=False)
                    ins = pe.matmul(ps[:, 1, o + P:o + T], VN[:, (2 + hh) * P:(3 + hh) * P], IN[:, pair[2 * hh + 1][2]],
                                    start=False, stop=True)
                ins.then_inc(sem("d_o"), 1)

            pe.wait_ge(sem("first_tables"), 16)
            norm(0)
            for l in range(DEPTH):
                hx = parts_of(HH, HL, T)
                for i in range(16):
                    chunk("ag", l, i, KD, hx, T, normed(l) if i == 0 else None)
                    if l and i == 1:
                        fill(norm_mods(l, "turns"))
                for i in range(16):
                    chunk("qk", l, i, KD, hx, T)
                for part in range(4):
                    freed = at["free"]
                    w = [tile(2, split=True) for k in range(KD)]
                    for tt in range(NT):
                        tokens_first("v", l, 2 * part + tt, w, tt, T, freed if tt == 0 else 0)
                pe.wait_ge(sem("drained"), CHUNK["qk", l, 15] + 1)
                if l == 0:
                    pe.wait_ge(sem("rope_table"), 1)
                    pe.wait_ge(sem("tables"), 32)
                for i in range(24):
                    if i == DN_EARLY:
                        pe.wait_ge(sem("conv_done"), KD * (l + 1))
                        for m in range(KD):
                            ins = pe.matmul(ps[:, 0, 0:T], ones, CV[:, m, :], start=m == 0, stop=m == KD - 1)
                        ins.then_inc(sem("ln_mean"), 1)
                    if i in ROPE_AT:
                        jj = ROPE_AT.index(i)
                        rot(8 * l + jj, C("rot1"), QK[:, 2 * jj:2 * jj + 2, :])
                    if i == 13:
                        pe.wait_ge(sem("rope"), 8 * (l + 1))
                        head_norm(HN_BASE1(l) + DQ_N, 2048)
                    if i == 20:
                        pe.wait_ge(sem("hn_rms"), HN_BASE1(l) + DQ_N + 1)
                        head_norm(HN_BASE1(l) + DK_N, 2048)
                    chunk("dn", l, i, KD, hx, T)
                    if i == DN_EARLY:
                        pe.wait_ge(sem("ln_sq"), l + 1)
                        for m in range(KD):
                            ins = pe.matmul(ps[:, 1, 0:T], ones, sq[:, m * T:(m + 1) * T], start=m == 0, stop=m == KD - 1)
                        ins.then_inc(sem("ln_ss"), 1)
                if l == 0:
                    pe.wait_ge(sem("silu_c"), 1)
                delta_gates(l)
                for it, items in enumerate(att_fill(l)):
                    if it < ATT_STEPS:
                        attention_scores(l, it)
                    fill(items)
                    if LAG <= it < ATT_STEPS + LAG:
                        attention_turn(l, it - LAG)
                    if it > LAG:
                        attention_out(l, it - LAG - 1)
                fill([("part", mods(l, "att")[0])] * 2)
                head_norm(HN_BASE1(l) + ATT_N, 2048)
                fill(mods(l, "att"))
                for u in range(UNITS):
                    delta(l, u)
                fill([("d_out", l, 0)])
                head_norm(HN_BASE1(l) + DO_N, 2048)
                fill(mods(l, "do"))
                for i in range(2 * KD):
                    if i:
                        fill([("d_out", l, i)])
                    if l == DEPTH - 1 and i in FILTER_1:
                        filter_step(0, FILTER_1.index(i))
                for m in range(KD):
                    chunk("w_out", l, m, KD, parts_of(MGH, MGL, T), T, low_ready("mg_low", KD * l) if m == 0 else None)
                norm(l + 1)
            fill(norm_mods(2, "turns"))
            norm(3)

            def attention2_scores(i, step):
                h, s, b = step
                keys = slice(0, 2 * T) if s == 0 else slice(T, 2 * T)
                if i >= 2:
                    pe.wait_ge(sem("a2_exp"), i - 1)
                pe.matmul(ps[:, i % 2, 0:keys.stop - keys.start], Q2_[:, h, s * T + b * P:s * T + (b + 1) * P],
                          K2_[:, h // 4, keys], start=True, stop=True).then_inc(sem("a2_scores"), 1)

            def attention2_turn(i, step):
                pe.wait_ge(sem("a2_weights"), i + 1)
                if i >= 1:
                    pe.wait_ge(sem("a2_turned"), i)
                for kb in range(4 if step[1] == 0 else 2):
                    ins = pe.transpose(ps[:, 2, kb * P:(kb + 1) * P], AT_A[:, i % 2, kb * P:(kb + 1) * P], ident)
                ins.then_inc(sem("a2_turn"), 1)

            def attention2_out(i, step):
                h, s, b = step
                blocks = [0, 1, 2, 3] if s == 0 else [2, 3]
                g = h // 4
                pe.wait_ge(sem("a2_turned"), i + 1)
                if i >= 1:
                    pe.wait_ge(sem("a2_out"), i)
                for n, kb in enumerate(blocks):
                    ins = pe.matmul(ps[:, 3, 0:P], V2_[:, kb, g * P:(g + 1) * P], AT_T[:, i % 2, n * P:(n + 1) * P],
                                    start=n == 0, stop=n == len(blocks) - 1)
                ins.then_inc(sem("a2_o"), 1)

            for l in range(DEPTH):
                n, ns = N_TOK[l], N_SEQ[l]
                hx = parts_of(HH, HL, n)
                i = HN_BASE2[l]
                for j in range(2):
                    chunk("k2", l, j, KD, parts_of(HH, HL, 2 * T), 2 * T, normed(mix_norm[l]) if j == 0 else None)
                fill(norm_mods(mix_norm[l], "turns"))
                for j in range(8):
                    chunk("q2", l, j, KD, hx, n)
                    if j == 1:
                        head_norm(i, 1024)
                    if j == 5:
                        pe.wait_ge(sem("hn_rms"), i + 1)
                        head_norm(i + 1, 4 * n)
                freed = at["free"]
                w = [tile(2, split=True) for k in range(KD)]
                for tt in range(4):
                    tokens_first("v2", l, tt, w, tt, 2 * P, freed if tt == 0 else 0)
                    if tt == 1:
                        pe.wait_ge(sem("hn_rms"), i + 2)
                        head_norm(i + 2, 4 * n)
                for j in range(EARLY_HY):
                    fill([("hy2", l, j)])
                    for jj in ROPES_AFTER[j]:
                        pe.wait_ge(sem("hn_done"), i + (1 if jj == 0 else 2 if jj < 3 else 3))
                        if jj == 0:
                            pe.wait_ge(sem("hn_rms"), i + 3)
                        rot(ROPE2[l] + jj, C("rot2"), Q2_[:, 2 * jj - 2:2 * jj, 0:T] if jj else K2_[:, :, 0:T])
                pe.wait_ge(sem("rope"), ROPE2[l] + 5)
                steps = IT2[l]
                for k, items in enumerate(att2_fill(l)):
                    i = IT2_BASE[l] + k
                    if k < len(steps):
                        attention2_scores(i, steps[k])
                    fill(items)
                    if LAG <= k < len(steps) + LAG:
                        attention2_turn(i - LAG, steps[k - LAG])
                    if k > LAG:
                        attention2_out(i - LAG - 1, steps[k - LAG - 1])
                pe.wait_ge(sem("a2_out"), IT2_BASE[l] + len(steps))
                gaps = iter(hyena_fill(l))
                fill(next(gaps))
                pe.wait_ge(sem("hconv"), 12 * (l + 1))
                for s in range(ns):
                    for tt in range(NT):
                        for m in range(KH):
                            ins = pe.transpose(ps[:, 2 * s + tt, m * P:(m + 1) * P],
                                               VX[:, m, s * T + tt * P:s * T + (tt + 1) * P], ident)
                ins.then_inc(sem("vt_ready"), 1)
                fill(next(gaps))
                pe.wait_ge(sem("vt_done"), l + 1)
                for s in range(ns):
                    k = 2 * l + s
                    if s:
                        fill(next(gaps))
                        pe.wait_ge(sem("hyena"), k)
                    for ft in range(4):
                        for tt in range(NT):
                            ins = pe.matmul(ps[:, ft, :], C("dft_fwd", tt * N_FFT + ft * P, P), VTK[:, 2 * s + tt, :],
                                            start=tt == 0, stop=tt == NT - 1)
                    ins.then_inc(sem("vf_ready"), 1)
                    fill(next(gaps))
                    pe.wait_ge(sem("y_done"), k + 1)
                    for m in range(KH):
                        for ft in range(4):
                            ins = pe.matmul(ps[:, m // 2, (m % 2) * T:(m % 2 + 1) * T], YFT[:, ft, m * P:(m + 1) * P],
                                            C("idft", ft * T, T), start=ft == 0, stop=ft == 3)
                    ins.then_inc(sem("yi_ready"), 1)
                fill([("oh", l, 0)])
                pe.wait_ge(sem("hyena"), 2 * l + ns)
                fill([("oh", l, i) for i in range(1, 2 * KD)])
                for m in range(KD):
                    chunk("w_out2", l, m, KD, lambda c: (MG2H[:, c, 0:n], MG2L[c][:, 0:n]), n, low_ready("mg2_low", KD * l) if m == 0 else None)
                norm(ffn_norm[l])
                per = KF // FF_PARTS[l]
                for i in range(KF):
                    for half in range(2):
                        chunk("gu", l, 2 * i + half, KD, hx, n, normed(ffn_norm[l]) if i + half == 0 else None)
                    if i == 0:
                        fill(norm_mods(ffn_norm[l], "turns"))
                    if l == 0 and i in FILTER_2:
                        filter_step(1, FILTER_2.index(i))
                    if i % per == per - 1:
                        for m in range(KD):
                            chunk("down", l, KD * (i // per) + m, per, parts_of(AFH[l], AFL[l], n), n,
                                  low_ready("af_low", KF * l + i + 1 - per) if m == 0 else None)
                norm(mix_norm[1] if l == 0 else 7)




def lay_out(inp):
    a = {k: np.asarray(v) for k, v in inp.items()}

    def tiles_of(w):
        return lambda col: [w[k:k + P, col:col + P] for k in range(0, w.shape[0], P)]

    w1, w2 = [tiles_of(w) for w in a["w_in"]], [tiles_of(w) for w in a["w_in_2"]]
    names = {"mod": "w_mod_2", "w_out": "w_out", "w_out2": "w_out_2", "down": "w_down_2", "c_out": "w_conv_out",
             "a_out": "w_attn_out", "d_out": "w_dn_out", "oa": "w_o_attn_2", "oh": "w_o_hyena_2"}
    single1 = {"qk": AQ, "dn": DQ, "cz": CZ, "az": AZ, "dz": DZ}
    single2 = {"q2": Q2, "k2": K2, "hy2": HY2}
    gates1 = {"c_out": GATE + D, "a_out": GATE, "d_out": GATE + 2 * D}
    gates2 = {"oa": G2, "oh": G2 + D}
    rest = {(name, l): tiles_of(a[key][l]) for name, key in names.items() for l in range(DEPTH)}
    gate_up = [tiles_of(w) for w in a["w_gate_up_2"]]

    def chunk_tiles(name, l, i):
        m = i // 2
        if name == "ag":
            return w1[l](GLU + D * (i % 2) + m * P)
        if name in single1:
            return w1[l](single1[name] + i * P)
        if name in single2:
            return w2[l](single2[name] + i * P)
        if name == "v":
            return [] if i % 2 else [t for k in zip(*(w1[l](AV + m * 2 * P + j * P) for j in range(2))) for t in k]
        if name == "mod":
            return [t for k in zip(*(rest[name, l](i * 512 + j * P) for j in range(4))) for t in k]
        if name == "modt":
            return []
        if name == "v2":
            return [] if i else [t for k in zip(*(w2[l](V2 + j * P) for j in range(2))) for t in k]
        if name in gates1:
            return rest[name, l](m * P) if i % 2 else w1[l](gates1[name] + m * P)
        if name in gates2:
            return rest[name, l](m * P) if i % 2 else w2[l](gates2[name] + m * P)
        if name == "gu":
            return gate_up[l](D_FF * (i % 2) + m * P)
        if name == "down":
            k = KF // FF_PARTS[l]
            return rest[name, l](i % KD * P)[i // KD * k:(i // KD + 1) * k]
        return rest[name, l](i * P)

    w_stream = np.zeros((N_LOADS, P, TILES, P), np.float32)
    at = 0
    for name, l, i in ORDER:
        own = chunk_tiles(name, l, i)
        assert len(own) == n_tiles(name, l, i)
        for t in own:
            w_stream[at // TILES, :, at % TILES, :] = t
            at += 1

    prm = np.zeros((P, N_PARAM), np.float32)

    def put(name, at, cols):
        cols = np.asarray(cols)
        s = PARAM_AT[name] + at
        prm[:cols.shape[0], s:s + cols.shape[1]] = cols

    by_p = lambda v: v.reshape(-1, P).T
    rows = lambda v: np.broadcast_to(v.reshape(1, -1), (P, v.size))
    for l in range(DEPTH):
        put("norm_w", l * KD, by_p(a["norm_w"][l]))
        put("attn_subln_w", l, by_p(a["attn_subln_w"][l]))
        put("conv_dw_w", l * KD * CONV_K, a["conv_dw_w"][l].reshape(CONV_K, KD, P).transpose(2, 1, 0).reshape(P, -1))
        put("conv_dw_b", l * KD, by_p(a["conv_dw_b"][l]))
        put("conv_ln_w", l * KD, by_p(a["conv_ln_w"][l]))
        put("conv_ln_b", l * KD, by_p(a["conv_ln_b"][l]))
        put("dn_conv_w", l * 24 * SHORT_K, a["dn_conv_w"][l].reshape(SHORT_K, 24, P).transpose(2, 1, 0).reshape(P, -1))
        put("dn_a_log", l * HEADS, rows(a["dn_a_log"][l]))
        put("dn_dt_bias", l * HEADS, rows(a["dn_dt_bias"][l]))
        put("dn_norm_w", l, by_p(a["dn_norm_w"][l]))
        put("lam_qk", l * 4 * QK_DIM, rows(a["lam_qk"][l]))
        put("w_ba", l * KD * 16, a["w_in"][l][:, DB:DB + 16].reshape(KD, P, 16).transpose(1, 0, 2).reshape(P, -1))
        put("b_mod", l * N_MOD * KD, by_p(a["b_mod_2"][l]))
        put("norm_mix", l * KD, by_p(a["norm_mix_2"][l]))
        put("q_norm", l, by_p(a["q_norm_2"][l]))
        put("k_norm", l, by_p(a["k_norm_2"][l]))
        put("conv_w", l * 12 * HY_TAPS, a["conv_w_2"][l].reshape(HY_TAPS, 12, P).transpose(2, 1, 0).reshape(P, -1))
        put("conv_b", l * 12, by_p(a["conv_b_2"][l]))
        for k in (1, 2, 3):
            put(f"filt_w{k}", l * 64, a[f"filt_w{k}_2"][l])
            put("filt_b", 3 * l + k - 1, a[f"filt_b{k}_2"][l][:, None])
            put("filt_freq", 3 * l + k - 1, a["filt_freq_2"][l][k - 1][:, None])
        put("hyena_bias", l * KH, by_p(a["hyena_bias_2"][l]))
        put("norm_ffn", l * KD, by_p(a["norm_ffn_2"][l]))
    put("final_norm_w", 0, by_p(a["final_norm_w"]))
    put("norm_final", 0, by_p(a["norm_final_2"]))
    conds = np.stack([a["c_2"].reshape(-1), a["c_ctx_2"].reshape(-1)], 1)
    put("c", 0, conds.reshape(KD, P, 2).transpose(1, 0, 2).reshape(P, -1))

    made = constants()
    cst = np.zeros((P, N_CONST), np.float32)
    for name, n in CONST_W.items():
        assert made[name].shape == (P, n), (name, made[name].shape)
        cst[:, CONST_AT[name]:CONST_AT[name] + n] = made[name].astype(np.float32)

    turned = lambda x: np.ascontiguousarray(x.reshape(T, KD, P).transpose(2, 1, 0))
    return {
        "w_stream": w_stream.reshape(N_LOADS, P, TILES * P),
        "params": prm,
        "fw4": np.ascontiguousarray(a["filt_w4_2"]),
        "pos": np.ascontiguousarray(np.broadcast_to(a["positions"].reshape(1, T), (P, T))),
        "xT": turned(a["x"]),
        "ctxT": turned(a["ctx_2"]),
        "consts": cst,
    }




def kernel(**inputs):
    import concourse.bacc as _bacc
    from concourse.bass_utils import run_bass_kernel_spmd as _run

    arrays = lay_out(inputs)
    nc = _bacc.Bacc("TRN2", target_bir_lowering=False, num_devices=1, dynamic_dma_scratch_size=1024)
    args = [nc.dram_tensor(f"in_{n}_dram", v.shape, mybir.dt.from_np(v.dtype), kind="ExternalInput").ap()
            for n, v in arrays.items()]
    args.append(nc.dram_tensor("out_0_dram", (P, KD, T), mybir.dt.float32, kind="ExternalOutput").ap())
    build(nc, *args)
    r = _run(nc, [{f"in_{n}_dram": v for n, v in arrays.items()}], core_ids=[0])
    got = r.results[0]["out_0_dram"]
    return np.ascontiguousarray(np.asarray(got).transpose(2, 1, 0)).reshape(1, T, D)
```
